# Optimizing a Trainium2 kernel written in Bass

```python
import math
import jax, jax.numpy as jnp
from jax import lax
import numpy as np

D_MODEL = 1024
BATCH = 1
SEQ = 256
DEPTH = 1
DEC_BATCH = 1
DEC_SEQ = 1024
PAST_LEN = 256

GRID_W = 64
N_HEADS = 8
HEAD_DIM = 64
V_DIM = 2 * HEAD_DIM
ATTN_WIDTH = N_HEADS * V_DIM
D_HYENA = D_MODEL // 2
HYENA_ORDER = 2
FILTER_EMB = 33
FILTER_HIDDEN = 64
D_FF = 4 * D_MODEL
ROPE_THETA = 10000.0
EPS = 1e-6
Q_BLOCK = 128
DECAY_TARGET = 1e-2
FAST_DECAY_PCT = 0.3
SLOW_DECAY_PCT = 1.5

Q_COLS = N_HEADS * 2 * HEAD_DIM
K_COLS = N_HEADS * 2 * HEAD_DIM
V_COLS = N_HEADS * V_DIM
HY_COLS = 3 * D_HYENA
GATE_COLS = 2 * D_MODEL
IN_COLS = Q_COLS + K_COLS + V_COLS + HY_COLS + GATE_COLS
SPLITS = (Q_COLS, Q_COLS + K_COLS, Q_COLS + K_COLS + V_COLS, Q_COLS + K_COLS + V_COLS + HY_COLS)

kernel_name = "diff_hyena_prefix_dit_step"

def _rmsnorm(x, g):
    xf = x.astype(jnp.float32)
    y = xf * lax.rsqrt(jnp.mean(xf * xf, axis=-1, keepdims=True) + EPS)
    return (y * g.astype(jnp.float32)).astype(x.dtype)

def _rope_half(x, pos):
    n = x.shape[-1] // 2
    inv = ROPE_THETA ** (-jnp.arange(n, dtype=jnp.float32) / n)
    ang = pos.astype(jnp.float32)[:, None] * inv[None, :]
    cos = jnp.cos(ang)[None, :, None, None, :]
    sin = jnp.sin(ang)[None, :, None, None, :]
    x1 = x[..., :n].astype(jnp.float32)
    x2 = x[..., n:].astype(jnp.float32)
    return jnp.concatenate([x1 * cos - x2 * sin, x2 * cos + x1 * sin], axis=-1).astype(x.dtype)

def _rope2d(x, n_tokens):
    rows = n_tokens // GRID_W
    row = jnp.repeat(jnp.arange(rows), GRID_W)
    col = jnp.tile(jnp.arange(GRID_W), rows)
    half = HEAD_DIM // 2
    return jnp.concatenate([_rope_half(x[..., :half], row), _rope_half(x[..., half:], col)], axis=-1)

def _diff_attention(q, k, v, lam, lam_init, subln_g):
    B, Lq = q.shape[0], q.shape[1]
    nblk = Lq // Q_BLOCK
    qb = jnp.moveaxis(q.reshape(B, nblk, Q_BLOCK, N_HEADS, 2, HEAD_DIM), 1, 0)

    def one_block(qi):
        s = jnp.einsum('bqhmd,bkhmd->bhmqk', qi, k, preferred_element_type=jnp.float32) * (HEAD_DIM ** -0.5)
        p = jax.nn.softmax(s, axis=-1)
        a = p[:, :, 0] - lam * p[:, :, 1]
        return jnp.einsum('bhqk,bkhe->bqhe', a.astype(v.dtype), v)

    o = lax.map(one_block, qb)
    o = jnp.moveaxis(o, 0, 1).reshape(B, Lq, N_HEADS, V_DIM)
    o = _rmsnorm(o, subln_g) * (1.0 - lam_init)
    return o.reshape(B, Lq, ATTN_WIDTH)

def _short_conv(x, w, b):
    xp = jnp.pad(x, ((0, 0), (1, 1), (0, 0)))
    return xp[:, :-2] * w[0] + xp[:, 1:-1] * w[1] + xp[:, 2:] * w[2] + b

def _hyena_filters(L, w1, b1, w2, b2, w3, freq):
    bands = (FILTER_EMB - 1) // 2
    t = jnp.linspace(0.0, 1.0, L, dtype=jnp.float32)[:, None]
    wpos = 2.0 * math.pi * jnp.arange(L, dtype=jnp.float32)[:, None] / L
    f = jnp.linspace(1e-4, bands - 1, bands, dtype=jnp.float32)[None, :]
    emb = jnp.concatenate([t, jnp.cos(f * wpos), -jnp.sin(f * wpos)], axis=-1)
    fr = freq.astype(jnp.float32)
    h = jnp.sin(fr * (emb @ w1.astype(jnp.float32) + b1.astype(jnp.float32)))
    h = jnp.sin(fr * (h @ w2.astype(jnp.float32) + b2.astype(jnp.float32)))
    h = (h @ w3.astype(jnp.float32)).reshape(L, 2, HYENA_ORDER, D_HYENA)
    deltas = jnp.linspace(math.log(DECAY_TARGET) / FAST_DECAY_PCT,
                          math.log(DECAY_TARGET) / SLOW_DECAY_PCT, D_HYENA, dtype=jnp.float32)
    h = h * jnp.exp(-t * jnp.abs(deltas))[:, None, None, :]
    fwd, bwd = h[:, 0], h[:, 1]
    two_sided = jnp.concatenate([fwd[:1] + bwd[:1], fwd[1:],
                                 jnp.zeros((1, HYENA_ORDER, D_HYENA), jnp.float32),
                                 bwd[1:][::-1]], axis=0)
    return jnp.fft.rfft(two_sided, axis=0)

def _fftconv(u, hf, bias):
    L = u.shape[1]
    uf = u.astype(jnp.float32)
    U = jnp.fft.rfft(uf, n=2 * L, axis=1)
    y = jnp.fft.irfft(U * hf[None], n=2 * L, axis=1)[:, :L]
    return (y + uf * bias.astype(jnp.float32)).astype(u.dtype)

def _hyena(u, conv_w, conv_b, w1, b1, w2, b2, w3, freq, hy_bias):
    L = u.shape[1]
    u = _short_conv(u, conv_w, conv_b)
    v, x1, x2 = jnp.split(u, 3, axis=-1)
    hf = _hyena_filters(L, w1, b1, w2, b2, w3, freq)
    z = x1 * _fftconv(v, hf[:, 0], hy_bias[0])
    return x2 * _fftconv(z, hf[:, 1], hy_bias[1])

def _layer(x, mod, ctx_kv, lam_init, p):
    (norm1_g, norm2_g, w_in, lam_q1, lam_k1, lam_q2, lam_k2, attn_subln_g, conv_w, conv_b,
     filt_w1, filt_b1, filt_w2, filt_b2, filt_w3, filt_freq, hy_bias,
     w_br_attn, w_br_hy, w_out, w_up, w_down) = p
    B, L, _ = x.shape
    shift1, scale1, gate1, shift2, scale2, gate2 = [m[:, None, :] for m in jnp.split(mod, 6, axis=-1)]
    h = _rmsnorm(x, norm1_g) * (1.0 + scale1) + shift1
    proj = h @ w_in
    q, k, v, u_hy, gates = jnp.split(proj, SPLITS, axis=-1)
    q = q.reshape(B, L, N_HEADS, 2, HEAD_DIM)
    k = k.reshape(B, L, N_HEADS, 2, HEAD_DIM)
    v = v.reshape(B, L, N_HEADS, V_DIM)
    if ctx_kv is None:
        q_att, k_all, v_all = q, k, v
    else:
        q_att = _rope2d(q, L)
        k_all = jnp.concatenate([ctx_kv[0], _rope2d(k, L)], axis=1)
        v_all = jnp.concatenate([ctx_kv[1], v], axis=1)
    lam = (jnp.exp(jnp.sum(lam_q1.astype(jnp.float32) * lam_k1.astype(jnp.float32)))
           - jnp.exp(jnp.sum(lam_q2.astype(jnp.float32) * lam_k2.astype(jnp.float32))) + lam_init)
    o_attn = _diff_attention(q_att, k_all, v_all, lam, lam_init, attn_subln_g)
    o_hy = _hyena(u_hy, conv_w, conv_b, filt_w1, filt_b1, filt_w2, filt_b2, filt_w3, filt_freq, hy_bias)
    g_attn, g_hy = jnp.split(jax.nn.sigmoid(gates), 2, axis=-1)
    merged = g_attn * (o_attn @ w_br_attn) + g_hy * (o_hy @ w_br_hy)
    x = x + gate1 * (merged @ w_out)
    h2 = _rmsnorm(x, norm2_g) * (1.0 + scale2) + shift2
    x = x + gate2 * (jnp.square(jax.nn.relu(h2 @ w_up)) @ w_down)
    return x, k, v

def setup_inputs(seed: int = 0) -> dict:
    key = jax.random.key(seed)
    ks = jax.random.split(key, 31)
    f32 = jnp.float32

    def nrm(k, shape, scale):
        return jax.random.normal(k, shape, f32) * scale

    return {
        "x_prompt": nrm(ks[0], (BATCH, SEQ, D_MODEL), 1.0),
        "x_sample": nrm(ks[1], (DEC_BATCH, DEC_SEQ, D_MODEL), 1.0),
        "cache_k": nrm(ks[2], (DEC_BATCH, DEPTH, PAST_LEN, N_HEADS, 2, HEAD_DIM), 1.0),
        "cache_v": nrm(ks[3], (DEC_BATCH, DEPTH, PAST_LEN, N_HEADS, V_DIM), 1.0),
        "c": nrm(ks[4], (DEC_BATCH, D_MODEL), 1.0),
        "c_ctx": nrm(ks[5], (D_MODEL,), 1.0),
        "w_ada": nrm(ks[6], (DEPTH, D_MODEL, 6 * D_MODEL), 0.5 * D_MODEL ** -0.5),
        "b_ada": nrm(ks[7], (DEPTH, 6 * D_MODEL), 0.01),
        "norm1_g": 1.0 + nrm(ks[8], (DEPTH, D_MODEL), 0.02),
        "norm2_g": 1.0 + nrm(ks[9], (DEPTH, D_MODEL), 0.02),
        "w_in": nrm(ks[10], (DEPTH, D_MODEL, IN_COLS), D_MODEL ** -0.5),
        "lam_q1": nrm(ks[11], (DEPTH, HEAD_DIM), 0.1),
        "lam_k1": nrm(ks[12], (DEPTH, HEAD_DIM), 0.1),
        "lam_q2": nrm(ks[13], (DEPTH, HEAD_DIM), 0.1),
        "lam_k2": nrm(ks[14], (DEPTH, HEAD_DIM), 0.1),
        "attn_subln_g": 1.0 + nrm(ks[15], (DEPTH, V_DIM), 0.02),
        "conv_w": nrm(ks[16], (DEPTH, 3, HY_COLS), 0.5),
        "conv_b": nrm(ks[17], (DEPTH, HY_COLS), 0.01),
        "filt_w1": nrm(ks[18], (DEPTH, FILTER_EMB, FILTER_HIDDEN), FILTER_EMB ** -0.5),
        "filt_b1": nrm(ks[19], (DEPTH, FILTER_HIDDEN), 0.1),
        "filt_w2": nrm(ks[20], (DEPTH, FILTER_HIDDEN, FILTER_HIDDEN), FILTER_HIDDEN ** -0.5),
        "filt_b2": nrm(ks[21], (DEPTH, FILTER_HIDDEN), 0.1),
        "filt_w3": nrm(ks[22], (DEPTH, FILTER_HIDDEN, 2 * HYENA_ORDER * D_HYENA), 0.1 * FILTER_HIDDEN ** -0.5),
        "filt_freq": 1.0 + nrm(ks[23], (DEPTH, FILTER_HIDDEN), 0.1),
        "hy_bias": nrm(ks[24], (DEPTH, HYENA_ORDER, D_HYENA), 0.5),
        "w_br_attn": nrm(ks[25], (DEPTH, ATTN_WIDTH, D_MODEL), ATTN_WIDTH ** -0.5),
        "w_br_hy": nrm(ks[26], (DEPTH, D_HYENA, D_MODEL), D_HYENA ** -0.5),
        "w_out": nrm(ks[27], (DEPTH, D_MODEL, D_MODEL), D_MODEL ** -0.5),
        "w_up": nrm(ks[28], (DEPTH, D_MODEL, D_FF), D_MODEL ** -0.5),
        "w_down": nrm(ks[29], (DEPTH, D_FF, D_MODEL), D_FF ** -0.5),
        "final_g": 1.0 + nrm(ks[30], (D_MODEL,), 0.02),
    }

def reference(x_prompt, x_sample, cache_k, cache_v, c, c_ctx, w_ada, b_ada, norm1_g, norm2_g, w_in,
              lam_q1, lam_k1, lam_q2, lam_k2, attn_subln_g, conv_w, conv_b, filt_w1, filt_b1,
              filt_w2, filt_b2, filt_w3, filt_freq, hy_bias, w_br_attn, w_br_hy, w_out, w_up,
              w_down, final_g):
    y_p = x_prompt
    y_s = x_sample
    new_k = []
    new_v = []
    for l in range(DEPTH):
        p = (norm1_g[l], norm2_g[l], w_in[l], lam_q1[l], lam_k1[l], lam_q2[l], lam_k2[l],
             attn_subln_g[l], conv_w[l], conv_b[l], filt_w1[l], filt_b1[l], filt_w2[l],
             filt_b2[l], filt_w3[l], filt_freq[l], hy_bias[l], w_br_attn[l], w_br_hy[l],
             w_out[l], w_up[l], w_down[l])
        lam_init = 0.8 - 0.6 * math.exp(-0.3 * l)
        mod_ctx = (jax.nn.silu(c_ctx) @ w_ada[l] + b_ada[l])[None, :]
        mod_lat = jax.nn.silu(c) @ w_ada[l] + b_ada[l]
        y_p, k_ctx, v_ctx = _layer(y_p, mod_ctx, None, lam_init, p)
        new_k.append(k_ctx)
        new_v.append(v_ctx)
        y_s, _, _ = _layer(y_s, mod_lat, (cache_k[:, l], cache_v[:, l]), lam_init, p)
    y_prompt = _rmsnorm(y_p, final_g)
    y_sample = _rmsnorm(y_s, final_g)
    new_cache_k = jnp.stack(new_k, axis=1)
    new_cache_v = jnp.stack(new_v, axis=1)
    return (y_prompt, y_sample, new_cache_k, new_cache_v)


_drawn_inputs = setup_inputs


def setup_inputs(seed=0):
    import zlib

    import numpy as np

    out = dict(_drawn_inputs(seed))
    spreads = {}
    factors = {'cache_k': 4.36,
     'cache_v': 3.738,
     'b_ada': 2.923,
     'norm1_g': 3.118,
     'norm2_g': 6.005,
     'lam_q1': 3.455,
     'lam_k1': 8.0,
     'lam_q2': 8.0,
     'lam_k2': 8.0,
     'attn_subln_g': 35.727,
     'conv_b': 7.169,
     'filt_freq': 2.707,
     'final_g': 7.574}
    for name, (base, spread) in spreads.items():
        noise = np.random.default_rng([zlib.crc32(name.encode()), seed]).standard_normal(out[name].shape)
        drawn = base * np.exp(spread * noise) if base else spread * noise
        out[name] = __import__('jax').numpy.asarray(drawn.astype(out[name].dtype))
    for name, factor in factors.items():
        out[name] = (out[name] * factor).astype(out[name].dtype)
    return out
```

```python
from contextlib import ExitStack, contextmanager
import math

import numpy as np
import concourse.bass as bass
from concourse import mybir

F32 = mybir.dt.float32
F32R = mybir.dt.float32r
ALU = mybir.AluOpType
ACT = mybir.ActivationFunctionType
AX = mybir.AxisListType

P = 128
D = 1024
KD = D // P
CTX, LAT, PAST = 256, 1024, 256
T = CTX + LAT
TT = T // P
SEGS = [(0, CTX), (CTX, LAT)]
CHUNKS = [(0, 256), (256, 512), (768, 512)]
NC = len(CHUNKS)
BANKS = 2 * NC
HEADS, HD, VD = 8, 64, 128
CH = 512
CHT = CH // P
FF = 4 * D
EMB, HID = 33, 64
EPS = 1e-6
GRID_W = 64
Q_U, K_U, U_U, G_U = 8, 8, 12, 16
PROJ_U = Q_U + K_U + U_U + G_U
ADA_U = 6 * KD
FIRST_ADA = 2 * KD


class Shared:
    pass


class Room:

    def __init__(self, nc, name, ctx):
        self.nc, self.name, self.ctx, self.sems = nc, name, ctx, []

    def sb(self, name, shape, dt=F32):
        return self.ctx.enter_context(self.nc.sbuf_tensor(f"{self.name}_{name}", shape, dt))

    def bank(self, name):
        return self.ctx.enter_context(self.nc.psum_tensor(f"{self.name}_{name}", [P, 512], F32))

    def sem(self, name):
        self.sems.append(self.nc.alloc_semaphore(name=f"{self.name}_{name}"))
        return self.sems[-1]

    def block(self):
        return self.ctx.enter_context(self.nc.Block())


@contextmanager
def stage(nc, name):
    with ExitStack() as ctx:
        room = Room(nc, name, ctx)
        yield room
    if room.sems:
        nc.clear_and_free_semaphores(room.sems)
        nc.all_engine_barrier()


def stage_consts(nc, g):
    LAM_INIT = 0.8 - 0.6 * math.exp(0.0)
    with stage(nc, "cst") as st:
        loaded, cleared, made, sig, done, lam_mm, lam_e = (
            st.sem(n) for n in ("loaded", "cleared", "made", "sig", "done", "lam_mm", "lam_e"))
        raw = st.sb("cond", [P, KD, 2])
        sg = st.sb("sg", [P, KD, 2])
        lam = st.sb("lam", [1, 4 * HD])
        lam_b, lam_p = st.sb("lamb", [P, 2 * HD]), st.sb("lamp", [P, 2, HD])
        lam_s, lam_x = st.sb("lams", [P, 2]), st.sb("lamx", [P, 2])
        bank = st.bank("b")
        block = st.block()
        LOADS = 7

        @block.sync
        def _(sp):
            for dst, src in ((raw[:], g.d["cond"]), (g.bada[:], g.d["b_ada"]), (g.n1[:], g.d["n1"]), (g.n2[:], g.d["n2"]),
                             (g.fg[:], g.d["fg"]), (lam[:], g.d["lam"]), (g.subln[:], g.d["subln"])):
                sp.dma_start(dst, src).then_inc(loaded, 16)
            sp.wait_ge(loaded, 16 * LOADS)

        @block.gpsimd
        def _(pool):
            pool.memset(g.ident[:], 0.0).then_inc(cleared, 1)
            pool.memset(g.ones[:], 1.0).then_inc(made, 1)
            pool.wait_ge(cleared, 1)
            pool.affine_select(out=g.ident[:], in_=g.ident[:], compare_op=ALU.not_equal, fill=1.0, base=0,
                               pattern=[[-1, P]], channel_multiplier=1).then_inc(made, 1)

        @block.tensor
        def _(pe):
            pe.wait_ge(loaded, 16 * LOADS)
            pe.wait_ge(made, 2)
            pe.matmul(bank[:, 0:4 * HD], g.ones[0:1, :], lam[:], start=True, stop=True).then_inc(lam_mm, 1)

        @block.scalar
        def _(act):
            act.wait_ge(loaded, 16 * LOADS)
            act.activation(sg[:], raw[:], ACT.Sigmoid).then_inc(sig, 1)
            act.wait_ge(done, 5)
            act.activation(lam_x[:], lam_s[:], ACT.Exp).then_inc(lam_e, 1)

        @block.vector
        def _(dve):
            n = [0]

            def step(ins):
                ins.then_inc(done, 1)
                n[0] += 1
                dve.wait_ge(done, n[0])

            dve.wait_ge(sig, 1)
            step(dve.tensor_tensor(g.silu[:], sg[:], raw[:], ALU.mult))
            step(dve.tensor_scalar(g.subln[:], g.subln[:], 1.0 - LAM_INIT, None, ALU.mult))
            dve.wait_ge(lam_mm, 1)
            step(dve.tensor_copy(lam_b[:], bank[:, 0:2 * HD]))
            step(dve.tensor_tensor(lam_p[:].rearrange("p a d -> p (a d)"), lam_b[:], bank[:, 2 * HD:4 * HD], ALU.mult))
            step(dve.tensor_reduce(lam_s[:], lam_p[:], AX.X, ALU.add))
            dve.wait_ge(lam_e, 1)
            step(dve.scalar_tensor_tensor(out=g.neg_lam[:], in0=lam_x[:, 1:2], scalar=-LAM_INIT, in1=lam_x[:, 0:1],
                                          op0=ALU.add, op1=ALU.subtract))


def stage_norm1(nc, g, h_hi, h_lo):
    with stage(nc, "n1") as st:
        NW = 4
        wa = st.sb("wa", [P, 2, NW, KD, P])
        x = st.sb("x", [P, KD, T])
        ab = st.sb("ab", [P, 2, KD, 2])
        pm = st.bank("mod")[:, 0:FIRST_ADA * 2].rearrange("p (u s) -> p u s", s=2)
        nrm = norm_buffers(st)
        w_in, w_used, x_in, mod_mm, mod_done, ab_done = (
            st.sem(n) for n in ("w_in", "w_used", "x_in", "mod_mm", "mod_done", "ab_done"))
        w_ins = [w_in, st.sem("w_in1")]
        block = st.block()

        @block.sync
        def _(sp):
            sp.dma_start(x[:], g.d["xT"].rearrange("k p t -> p k t")).then_inc(x_in, 16)
            for j in range(FIRST_ADA // NW):
                if j >= 2:
                    sp.wait_ge(w_used, j - 1)
                sp.dma_start(wa[:, j % 2], g.d["w_ada"][j * NW:(j + 1) * NW].rearrange("u p k m -> p u k m")
                             ).then_inc(w_ins[j % 2], 16)

        @block.tensor
        def _(pe):
            for j in range(FIRST_ADA // NW):
                pe.wait_ge(w_ins[j % 2], 16 * (j // 2 + 1))
                for u in range(NW):
                    for k in range(KD):
                        mm = pe.matmul(pm[:, j * NW + u, :], wa[:, j % 2, u, k, :], g.silu[:, k, :],
                                       start=(k == 0), stop=(k == KD - 1))
                mm.then_inc(w_used, 1)
            norm_pe(pe, g, nrm)

        @block.vector
        def _(dve):
            dve.wait_ge(w_used, FIRST_ADA // NW)
            for s in range(2):
                m = dve.tensor_tensor(g.mod[:, 0:FIRST_ADA, s], pm[:, :, s], g.bada[:, 0:FIRST_ADA], ALU.add)
            m.then_inc(mod_done, 1)
            dve.wait_ge(mod_done, 1)
            for s in range(2):
                m = dve.scalar_tensor_tensor(out=ab[:, 0, :, s], in0=g.mod[:, KD:2 * KD, s], scalar=1.0,
                                             in1=g.n1[:], op0=ALU.add, op1=ALU.mult)
                m = dve.tensor_copy(ab[:, 1, :, s], g.mod[:, 0:KD, s])
            m.then_inc(ab_done, 1)
            norm_sum_dve(dve, g, nrm)
            dve.wait_ge(ab_done, 1)
            norm_apply_dve(dve, x, nrm, lambda k, s: (ab[:, 0, k, s:s + 1], ab[:, 1, k, s:s + 1]))

        @block.scalar
        def _(act):
            act.wait_ge(x_in, 16)
            norm_act(act, x, nrm)
            split_hi_act(act, nrm, h_hi)

        @block.gpsimd
        def _(pool):
            split_lo_pool(pool, nrm, h_hi, h_lo)


def norm_buffers(st):
    b = Shared()
    b.sq = st.sb("sq", [P, 2, T])
    b.acc = st.sb("acc", [P, T])
    b.var = st.sb("var", [P, TT])
    b.std = st.sb("std", [P, TT])
    b.rstd = st.sb("rstd", [P, TT])
    b.diag = st.sb("diag", [P, TT, P])
    b.xn = st.sb("xn", [P, 2, T])
    b.hf = st.sb("hf", [P, 2, T])
    b.p_sum = st.bank("psum")[:, 0:TT]
    b.p_r = [st.bank(f"pr{c}") for c in range(NC)]
    (b.squared, b.summed, b.token_sums, b.var_done, b.std_done, b.rstd_done, b.diag_done, b.spread, b.xn_done,
     b.hf_done, b.hi_done, b.lo_done) = (
        st.sem(n) for n in ("squared", "summed", "token_sums", "var_done", "std_done", "rstd_done", "diag_done",
                            "spread", "xn_done", "hf_done", "hi_done", "lo_done"))
    return b


def norm_act(act, x, b):
    for k in range(KD):
        if k >= 2:
            act.wait_ge(b.summed, k - 1)
        act.activation(b.sq[:, k % 2], x[:, k, :], ACT.Square).then_inc(b.squared, 1)
    act.wait_ge(b.var_done, 1)
    act.activation(b.std[:], b.var[:], ACT.Sqrt).then_inc(b.std_done, 1)


def norm_sum_dve(dve, g, b):
    for k in range(KD):
        dve.wait_ge(b.squared, k + 1)
        if k == 0:
            dve.tensor_copy(b.acc[:], b.sq[:, 0]).then_inc(b.summed, 1)
        else:
            dve.wait_ge(b.summed, k)
            dve.tensor_tensor(b.acc[:], b.acc[:], b.sq[:, k % 2], ALU.add).then_inc(b.summed, 1)
    dve.wait_ge(b.token_sums, 1)
    dve.tensor_scalar(b.var[:], b.p_sum[:], 1.0 / D, EPS, ALU.mult, ALU.add).then_inc(b.var_done, 1)
    dve.wait_ge(b.std_done, 1)
    dve.reciprocal(b.rstd[:], b.std[:]).then_inc(b.rstd_done, 1)
    dve.wait_ge(b.rstd_done, 1)
    for t in range(TT):
        m = dve.tensor_scalar(b.diag[:, t], g.ident[:], b.rstd[:, t:t + 1], None, ALU.mult)
    m.then_inc(b.diag_done, 1)


def norm_pe(pe, g, b):
    pe.wait_ge(b.summed, KD)
    for t in range(TT):
        mm = pe.matmul(b.p_sum[:, t:t + 1], b.acc[:, t * P:(t + 1) * P], g.ones[:, 0:1], start=True, stop=True)
    mm.then_inc(b.token_sums, 1)
    pe.wait_ge(b.diag_done, 1)
    for c, (at, n) in enumerate(CHUNKS):
        for t in range(n // P):
            mm = pe.matmul(b.p_r[c][:, t * P:(t + 1) * P], g.ones[:], b.diag[:, at // P + t],
                           start=True, stop=True)
    mm.then_inc(b.spread, 1)


def norm_apply_dve(dve, x, b, affine):
    dve.wait_ge(b.spread, 1)
    for k in range(KD):
        if k >= 2:
            dve.wait_ge(b.lo_done, k - 1)
        for c, (at, n) in enumerate(CHUNKS):
            m = dve.tensor_tensor(b.xn[:, k % 2, at:at + n], x[:, k, at:at + n], b.p_r[c][:, 0:n], ALU.mult)
        m.then_inc(b.xn_done, 1)
        dve.wait_ge(b.xn_done, k + 1)
        for s, (at, n) in enumerate(SEGS):
            a, sh = affine(k, s)
            m = dve.tensor_scalar(b.hf[:, k % 2, at:at + n], b.xn[:, k % 2, at:at + n], a, sh, ALU.mult,
                                  ALU.add)
        m.then_inc(b.hf_done, 1)


def split_hi_act(act, b, hi):
    for k in range(KD):
        act.wait_ge(b.hf_done, k + 1)
        act.activation(hi[:, k, :], b.hf[:, k % 2], ACT.Copy).then_inc(b.hi_done, 1)


def split_lo_pool(pool, b, hi, lo):
    for k in range(KD):
        pool.wait_ge(b.hi_done, k + 1)
        pool.tensor_tensor(lo[:, k, :], b.hf[:, k % 2], hi[:, k, :], ALU.subtract).then_inc(b.lo_done, 1)
    pool.wait_ge(b.lo_done, KD)


def products(pe, out, w_hi, w_lo, x_hi, x_lo, first, last):
    pe.matmul(out, w_hi, x_hi, start=first, stop=False)
    pe.matmul(out, w_hi, x_lo, start=False, stop=False)
    return pe.matmul(out, w_lo, x_hi, start=False, stop=last)


def stage_project(nc, g, h_hi, h_lo):
    N = PROJ_U
    WITH_ADA = ADA_U - FIRST_ADA
    assert WITH_ADA % 2 == 0 and N % 2 == 0 and WITH_ADA < N
    with stage(nc, "prj") as st:
        raw = [st.sb(f"raw{s}", [P, KD, P]) for s in range(2)]
        w_hi = [st.sb(f"whi{s}", [P, KD, P], F32R) for s in range(2)]
        w_lo = [st.sb(f"wlo{s}", [P, KD, P], F32R) for s in range(2)]
        wa = [st.sb(f"wa{s}", [P, KD, P]) for s in range(2)]
        ob = [st.sb(f"ob{s}", [P, T]) for s in range(2)]
        mod2 = st.sb("mod2", [P, WITH_ADA, 2])
        bank = [st.bank(f"b{i}") for i in range(BANKS)]
        pa = [st.bank(f"pa{s}")[:, 0:2] for s in range(2)]
        raw_in = [st.sem(f"raw_in{s}") for s in range(2)]
        wa_in = [st.sem(f"wa_in{s}") for s in range(2)]
        stored = [st.sem(f"stored{s}") for s in range(2)]
        hi_done, lo_done, chunk_mm, evac, ada_mm, ada_out, fin = (
            st.sem(n) for n in ("hi_done", "lo_done", "chunk_mm", "evac", "ada_mm", "ada_out", "fin"))
        block = st.block()

        @block.sync
        def _(sp):
            def load(n, s):
                sp.dma_start(raw[s][:], g.d["w_proj"][n]).then_inc(raw_in[s], 16)

            def load_ada(n, s):
                sp.dma_start(wa[s][:], g.d["w_ada"][n]).then_inc(wa_in[s], 16)

            def store(n, s):
                sp.wait_ge(evac, n * NC + NC + BANKS)
                sp.dma_start(g.projT[n], ob[s][:]).then_inc(stored[s], 16)

            for s in range(2):
                sp.sem_inc(stored[s], 16)
                load(s, s)
                load_ada(FIRST_ADA + s, s)
            with sp.Fori(0, WITH_ADA // 2 - 1) as i:
                for s in range(2):
                    sp.wait_ge(lo_done, 2 * i + s + 1)
                    load(2 * i + s + 2, s)
                    sp.wait_ge(ada_mm, 2 * i + s + 1)
                    load_ada(2 * i + s + 2 + FIRST_ADA, s)
                    store(2 * i + s, s)
            with sp.Fori(WITH_ADA // 2 - 1, N // 2 - 1) as i:
                for s in range(2):
                    sp.wait_ge(lo_done, 2 * i + s + 1)
                    load(2 * i + s + 2, s)
                    store(2 * i + s, s)
            for s in range(2):
                store(N - 2 + s, s)
            for s in range(2):
                sp.wait_ge(stored[s], 16 * (N // 2 + 1))

        @block.scalar
        def _(act):
            def split(i, s):
                act.wait_ge(raw_in[s], 16 * i + 16)
                act.activation(w_hi[s][:], raw[s][:], ACT.Copy).then_inc(hi_done, 1)

            for s in range(2):
                split(0, s)
            with act.Fori(1, N // 2) as i:
                for s in range(2):
                    act.wait_ge(chunk_mm, (2 * i + s - 1) * NC)
                    split(i, s)

        @block.gpsimd
        def _(pool):
            with pool.Fori(0, N // 2) as i:
                for s in range(2):
                    pool.wait_ge(hi_done, 2 * i + s + 1)
                    pool.tensor_tensor(w_lo[s][:], raw[s][:], w_hi[s][:], ALU.subtract).then_inc(lo_done, 1)

        @block.tensor
        def _(pe):
            def unit(i, s, ada):
                pe.wait_ge(lo_done, 2 * i + s + 1)
                for c, (at, n) in enumerate(CHUNKS):
                    pe.wait_ge(evac, (2 * i + s) * NC + c + 1)
                    out = bank[s * NC + c][:, 0:n]
                    for k in range(KD):
                        mm = products(pe, out, w_hi[s][:, k], w_lo[s][:, k], h_hi[:, k, at:at + n],
                                      h_lo[:, k, at:at + n], k == 0, k == KD - 1)
                    mm.then_inc(chunk_mm, 1)
                if ada:
                    pe.wait_ge(wa_in[s], 16 * i + 16)
                    pe.wait_ge(ada_out, 2 * i + s + 1)
                    for k in range(KD):
                        mm = pe.matmul(pa[s][:], wa[s][:, k], g.silu[:, k, :], start=(k == 0),
                                       stop=(k == KD - 1))
                    mm.then_inc(ada_mm, 1)

            with pe.Fori(0, WITH_ADA // 2) as i:
                for s in range(2):
                    unit(i, s, True)
            with pe.Fori(WITH_ADA // 2, N // 2) as i:
                for s in range(2):
                    unit(i, s, False)

        @block.vector
        def _(dve):
            def unit(i, s):
                dve.wait_ge(stored[s], 16 * i + 16)
                for c, (at, n) in enumerate(CHUNKS):
                    dve.wait_ge(chunk_mm, (2 * i + s) * NC + c + 1)
                    dve.tensor_copy(ob[s][:, at:at + n], bank[s * NC + c][:, 0:n]).then_inc(evac, 1)

            dve.sem_inc(evac, BANKS)
            dve.sem_inc(ada_out, 2)
            with dve.Fori(0, WITH_ADA // 2) as i:
                for s in range(2):
                    unit(i, s)
                    dve.wait_ge(ada_mm, 2 * i + s + 1)
                    dve.tensor_copy(mod2[:, bass.ds(2 * i + s, 1), :].rearrange("p u s -> p (u s)"), pa[s]
                                    ).then_inc(ada_out, 1)
            with dve.Fori(WITH_ADA // 2, N // 2) as i:
                for s in range(2):
                    unit(i, s)
            dve.wait_ge(ada_out, 2 + WITH_ADA)
            for s in range(2):
                m = dve.tensor_tensor(g.mod[:, FIRST_ADA:ADA_U, s], mod2[:, :, s], g.bada[:, FIRST_ADA:ADA_U],
                                      ALU.add)
            m.then_inc(fin, 1)
            dve.wait_ge(fin, 1)


def stage_values(nc, g, h_hi, h_lo):
    NB = D // 512
    with stage(nc, "val") as st:
        raw = [st.sb(f"raw{j}", [P, KD // 2, 512]) for j in range(2)]
        w_hi = st.sb("whi", [P, KD, 512], F32R)
        w_lo = st.sb("wlo", [P, KD, 512], F32R)
        ob = [st.sb(f"ob{s}", [P, 512]) for s in range(4)]
        bank = [st.bank(f"b{i}") for i in range(4)]
        raw_in = [st.sem(f"raw_in{j}") for j in range(2)]
        stored = [st.sem(f"stored{s}") for s in range(4)]
        hi_done, lo_done, mm_done, evac = (st.sem(n) for n in ("hi_done", "lo_done", "mm_done", "evac"))
        block = st.block()

        @block.sync
        def _(sp):
            def load(n, j):
                sp.dma_start(raw[j][:], g.d["w_v"][n, :, j * (KD // 2):(j + 1) * (KD // 2), :]).then_inc(raw_in[j], 16)

            for j in range(2):
                load(0, j)
            for n in range(NB):
                if n + 1 < NB:
                    for j in range(2):
                        sp.wait_ge(lo_done, 2 * n + j + 1)
                        load(n + 1, j)
                for t in range(TT):
                    o = n * TT + t
                    sp.wait_ge(evac, o + 1)
                    sp.dma_start(g.v[t, :, n * 512:(n + 1) * 512], ob[o % 4][:]).then_inc(stored[o % 4], 16)
            for s in range(4):
                sp.wait_ge(stored[s], 16 * (NB * TT // 4))

        @block.scalar
        def _(act):
            for n in range(NB):
                if n:
                    act.wait_ge(mm_done, n * TT)
                for j in range(2):
                    act.wait_ge(raw_in[j], 16 * (n + 1))
                    act.activation(w_hi[:, j * 4:j * 4 + 4, :], raw[j][:], ACT.Copy).then_inc(hi_done, 1)

        @block.gpsimd
        def _(pool):
            for n in range(NB * 2):
                pool.wait_ge(hi_done, n + 1)
                j = n % 2
                pool.tensor_tensor(w_lo[:, j * 4:j * 4 + 4, :], raw[j][:], w_hi[:, j * 4:j * 4 + 4, :],
                                   ALU.subtract).then_inc(lo_done, 1)

        @block.tensor
        def _(pe):
            for n in range(NB):
                for t in range(TT):
                    o = n * TT + t
                    if o >= 4:
                        pe.wait_ge(evac, o - 3)
                    for k in range(KD):
                        if t == 0 and k % 4 == 0:
                            pe.wait_ge(lo_done, 2 * n + k // 4 + 1)
                        tok = slice(t * P, (t + 1) * P)
                        mm = products(pe, bank[o % 4][:], h_hi[:, k, tok], h_lo[:, k, tok], w_hi[:, k], w_lo[:, k],
                                      k == 0, k == KD - 1)
                    mm.then_inc(mm_done, 1)

        @block.vector
        def _(dve):
            for o in range(NB * TT):
                dve.wait_ge(mm_done, o + 1)
                if o >= 4:
                    dve.wait_ge(stored[o % 4], 16 * (o // 4))
                dve.tensor_copy(ob[o % 4][:], bank[o % 4][:]).then_inc(evac, 1)


CTX_Q, LAT_Q = CTX // P, LAT // P
UNITS = CTX_Q + LAT_Q
KEYS = CTX + PAST + LAT
PAIR = 2 * UNITS
TBLOCKS = 4


def unit_keys(u):
    return (0, CTX) if u % UNITS < CTX_Q else (CTX, PAST + LAT)


def key_chunks(n):
    return [(at, min(512, n - at)) for at in range(0, n, 512)]


def block_groups(u):
    nb = unit_keys(u)[1] // P
    return [(at, min(TBLOCKS, nb - at)) for at in range(0, nb, TBLOCKS)]


GROUPS_BEFORE, A_BEFORE, B_BEFORE = [0], [0], [0]
for _u in range(PAIR):
    _n = len(block_groups(_u))
    GROUPS_BEFORE.append(GROUPS_BEFORE[-1] + _n)
    B_BEFORE.append(B_BEFORE[-1] + _n // 2)
    A_BEFORE.append(A_BEFORE[-1] + _n - _n // 2)
PAIR_GROUPS, PAIR_A, PAIR_B = GROUPS_BEFORE[PAIR], A_BEFORE[PAIR], B_BEFORE[PAIR]
SPLIT_AT = 6


def stage_attention(nc, g, o_all, l0_all):
    with stage(nc, "att") as st:
        q_cos, q_sin = st.sb("qcos", [P, T]), st.sb("qsin", [P, LAT])
        k_cos, k_sin = st.sb("kcos", [P, LAT]), st.sb("ksin", [P, LAT])
        q_raw = [st.sb(f"qraw{s}", [P, T]) for s in range(2)]
        q_swp = [st.sb(f"qswp{s}", [P, LAT]) for s in range(2)]
        k_raw = [st.sb(f"kraw{s}", [P, KEYS]) for s in range(2)]
        k_swp = [st.sb(f"kswp{s}", [P, LAT]) for s in range(2)]
        v = [st.sb(f"v{s}", [P, KEYS // P, VD]) for s in range(2)]
        q_hi, q_lo = ([st.sb(f"q{x}{s}", [P, T], F32R) for s in range(2)] for x in ("hi", "lo"))
        k_hi, k_lo = ([st.sb(f"k{x}{s}", [P, KEYS], F32R) for s in range(2)] for x in ("hi", "lo"))
        e = [st.sb(f"e{m}", [P, PAST + LAT]) for m in range(2)]
        a = st.sb("a", [P, PAST + LAT])
        aT = st.sb("aT", [P, (PAST + LAT) // P, P])
        nmax = st.sb("nmax", [P, 2])
        l1, rl1, coef = (st.sb(n, [P, 1]) for n in ("l1", "rl1", "coef"))
        scores = [st.ctx.enter_context(nc.psum_tensor(f"att_s{m}", [P, 3 * 512], F32)) for m in range(2)]
        bank_a, bank_b = st.bank("turn_a"), st.bank("turn_b")
        tables_in, q_in, k_in, v_in = st.sem("tables_in"), *([st.sem(f"{n}_in{s}") for s in range(2)] for n in "qkv")
        prep, rotated, ready, split = (st.sem(n) for n in ("prep", "rotated", "ready", "split"))
        qk = [st.sem(f"qk{m}") for m in range(2)]
        maxed = [st.sem(f"maxed{m}") for m in range(2)]
        exped = [st.sem(f"exped{m}") for m in range(2)]
        small, combined, turned, moved_a, moved_b, pv, o_out = (
            st.sem(n) for n in ("small", "combined", "turned", "moved_a", "moved_b", "pv", "o_out"))
        block = st.block()
        PREP = 2
        Q_DMAS = 5
        K_DMAS = 7

        @block.sync
        def _(sp):
            def load_qk(h, s):
                sp.dma_start(q_raw[s][:], g.projT[h]).then_inc(q_in[s], 16)
                sp.dma_start(k_raw[s][:, 0:CTX], g.projT[h + HEADS, :, 0:CTX]).then_inc(k_in[s], 16)
                sp.dma_start(k_raw[s][:, CTX:CTX + PAST], g.d["cache_kT"][h]).then_inc(k_in[s], 16)
                sp.dma_start(k_raw[s][:, CTX + PAST:], g.projT[h + HEADS, :, CTX:]).then_inc(k_in[s], 16)
                for b in range(4):
                    dst, src = slice(32 * b, 32 * b + 32), slice(32 * (b ^ 1), 32 * (b ^ 1) + 32)
                    sp.dma_start(q_swp[s][dst], g.projT[h, src, CTX:]).then_inc(q_in[s], 16)
                    sp.dma_start(k_swp[s][dst], g.projT[h + HEADS, src, CTX:]).then_inc(k_in[s], 16)

            def load_v(h, s):
                sp.dma_start(v[s][:, 0:2], g.v_heads[h, :, 0:2]).then_inc(v_in[s], 16)
                sp.dma_start(v[s][:, 2:4], g.d["cache_v"][h]).then_inc(v_in[s], 16)
                sp.dma_start(v[s][:, 4:], g.v_heads[h, :, 2:]).then_inc(v_in[s], 16)

            for t, src in ((q_cos, g.d["q_cos"]), (q_sin, g.d["q_sin"]), (k_cos, g.d["k_cos"]), (k_sin, g.d["k_sin"])):
                sp.dma_start(t[:], src).then_inc(tables_in, 16)
            for s in range(2):
                load_qk(s, s)
                load_v(s, s)
            with sp.Fori(1, HEADS // 2) as i:
                for s in range(2):
                    sp.wait_ge(ready, 2 * i + s - 1)
                    load_qk(2 * i + s, s)
                    sp.wait_ge(pv, (2 * i + s - 1) * UNITS)
                    load_v(2 * i + s, s)

        @block.gpsimd
        def _(pool):
            def head(i, s):
                done = (2 * i + s) * PREP
                parts = ((q_raw[s][:], q_raw[s][:, CTX:], q_cos, q_swp[s], q_sin, q_in[s], Q_DMAS),
                         (k_raw[s][:, CTX + PAST:], k_raw[s][:, CTX + PAST:], k_cos, k_swp[s], k_sin, k_in[s], K_DMAS))
                for j, (full, lat, cos, swp, sin, came, dmas) in enumerate(parts):
                    pool.wait_ge(came, 16 * dmas * (i + 1))
                    pool.tensor_tensor(full, full, cos[:], ALU.mult)
                    pool.tensor_tensor(swp[:], swp[:], sin[:], ALU.mult).then_inc(prep, 1)
                    pool.wait_ge(prep, done + j + 1)
                    pool.tensor_tensor(lat, lat, swp[:], ALU.add).then_inc(rotated, 1)
                pool.wait_ge(split, 2 * (2 * i + s) + 2)
                pool.tensor_tensor(q_lo[s][:], q_raw[s][:], q_hi[s][:], ALU.subtract)
                pool.tensor_tensor(k_lo[s][:], k_raw[s][:], k_hi[s][:], ALU.subtract).then_inc(ready, 1)

            pool.wait_ge(tables_in, 64)
            head(0, 0)
            with pool.Fori(0, HEADS // 2 - 1) as i:
                head(i, 1)
                head(i + 1, 0)
            head(HEADS // 2 - 1, 1)

        @block.tensor
        def _(pe):
            def qk_map(i, u, m, first):
                s, col = u // UNITS, (u % UNITS) * P
                key0, nk = unit_keys(u)
                if m == 0 and u % UNITS == 0:
                    pe.wait_ge(ready, 2 * i + s + 1)
                if not first:
                    pe.wait_ge(exped[m], i * PAIR + u)
                rows = slice(HD * m, HD * m + HD)
                for at, n in key_chunks(nk):
                    keys = slice(key0 + at, key0 + at + n)
                    mm = products(pe, scores[m][:, at:at + n], q_hi[s][rows, col:col + P], q_lo[s][rows, col:col + P],
                                  k_hi[s][rows, keys], k_lo[s][rows, keys], True, True)
                mm.then_inc(qk[m], 1)

            def turn(i, u, r, first):
                at, nb = block_groups(u)[r]
                if r == 0:
                    pe.wait_ge(combined, i * PAIR + u + 1)
                    if not first:
                        pe.wait_ge(moved_a, i * PAIR_A + A_BEFORE[u])
                elif r == 1:
                    if not first:
                        pe.wait_ge(o_out, i * PAIR + u)
                else:
                    pe.wait_ge(moved_a, i * PAIR_A + A_BEFORE[u] + 1)
                bank = bank_b if r == 1 else bank_a
                for b in range(nb):
                    mm = pe.transpose(bank[:, b * P:(b + 1) * P], a[:, (at + b) * P:(at + b + 1) * P], g.ident[:])
                mm.then_inc(turned, 1)

            def values(i, u):
                s = u // UNITS
                nb = unit_keys(u)[1] // P
                if u % UNITS == 0:
                    pe.wait_ge(v_in[s], 48 * (i + 1))
                pe.wait_ge(moved_a, i * PAIR_A + A_BEFORE[u + 1])
                if len(block_groups(u)) > 1:
                    pe.wait_ge(moved_b, i * PAIR_B + B_BEFORE[u + 1])
                elif not (isinstance(i, int) and i == 0 and u == 0):
                    pe.wait_ge(o_out, i * PAIR + u)
                for b in range(nb):
                    mm = pe.matmul(bank_b[:, 0:VD], aT[:, b], v[s][:, unit_keys(u)[0] // P + b], start=(b == 0),
                                   stop=(b == nb - 1))
                mm.then_inc(pv, 1)

            def back(i, u, r0, r1):
                for r in range(r0, min(r1, len(block_groups(u)))):
                    turn(i, u, r, isinstance(i, int) and i == 0 and u == 0)

            def body(i, peeled):
                for u in range(PAIR):
                    j, w = (i, u - 1) if u else (i - 1, PAIR - 1)
                    qk_map(i, u, 0, peeled and u == 0)
                    if not (peeled and u == 0):
                        back(j, w, 0, 1)
                    qk_map(i, u, 1, peeled and u == 0)
                    if not (peeled and u == 0):
                        back(j, w, 1, 3)
                        values(j, w)

            body(0, True)
            with pe.Fori(1, HEADS // 2) as i:
                body(i, False)
            back(HEADS // 2 - 1, PAIR - 1, 0, 3)
            values(HEADS // 2 - 1, PAIR - 1)

        @block.scalar
        def _(act):
            def exp_map(i, u, m, first):
                nk = unit_keys(u)[1]
                act.wait_ge(maxed[m], i * PAIR + u + 1)
                if not first:
                    act.wait_ge(combined, i * PAIR + u)
                l = l0_all[:, bass.ds(i * PAIR + u, 1)] if m == 0 else l1[:]
                act.activation(e[m][:, 0:nk], scores[m][:, 0:nk], ACT.Exp, bias=nmax[:, m:m + 1],
                               accum_out=l).then_inc(exped[m], 1)

            def move(i, u, r, first):
                at, nb = block_groups(u)[r]
                act.wait_ge(turned, i * PAIR_GROUPS + GROUPS_BEFORE[u] + r + 1)
                if r == 0 and not first:
                    act.wait_ge(pv, i * PAIR + u)
                act.activation(aT[:, at:at + nb], bank_a[:, 0:nb * P], ACT.Copy).then_inc(moved_a, 1)

            def split_head(i, s, first):
                if not first:
                    act.wait_ge(qk[1], (2 * i + s - 1) * UNITS)
                act.wait_ge(rotated, 2 * (2 * i + s) + 1)
                act.activation(q_hi[s][:], q_raw[s][:], ACT.Copy).then_inc(split, 1)
                act.wait_ge(rotated, 2 * (2 * i + s) + 2)
                act.activation(k_hi[s][:], k_raw[s][:], ACT.Copy).then_inc(split, 1)

            def output(i, u):
                act.wait_ge(pv, i * PAIR + u + 1)
                act.activation(o_all[:, bass.ds(i * PAIR + u, 1), :].rearrange("p u e -> p (u e)"), bank_b[:, 0:VD],
                               ACT.Copy).then_inc(o_out, 1)

            def body(i, peeled, last):
                for u in range(PAIR):
                    j, w = (i, u - 1) if u else (i - 1, PAIR - 1)
                    start = peeled and u == 0
                    second = peeled and u == 1
                    if not start:
                        move(j, w, 0, second)
                    exp_map(i, u, 0, start)
                    if not start and len(block_groups(w)) > 2:
                        move(j, w, 2, second)
                    exp_map(i, u, 1, start)
                    if not start:
                        output(j, w)
                    if u == SPLIT_AT:
                        split_head(i, 1, peeled)
                    if u == UNITS + SPLIT_AT and not last:
                        split_head(i + 1, 0, False)

            split_head(0, 0, True)
            body(0, True, False)
            with act.Fori(1, HEADS // 2 - 1) as i:
                body(i, False, False)
            body(HEADS // 2 - 1, False, True)
            for r in (0, 2):
                move(HEADS // 2 - 1, PAIR - 1, r, False)
            output(HEADS // 2 - 1, PAIR - 1)

        @block.vector
        def _(dve):
            def row_max(i, u, m, first):
                nk = unit_keys(u)[1]
                dve.wait_ge(qk[m], i * PAIR + u + 1)
                if not first:
                    dve.wait_ge(exped[m], i * PAIR + u)
                dve.tensor_reduce(nmax[:, m:m + 1], scores[m][:, 0:nk], AX.X, ALU.max, negate=True
                                  ).then_inc(maxed[m], 1)

            def move(i, u):
                at, nb = block_groups(u)[1]
                dve.wait_ge(turned, i * PAIR_GROUPS + GROUPS_BEFORE[u] + 2)
                if not (isinstance(i, int) and i == 0 and u == 0):
                    dve.wait_ge(pv, i * PAIR + u)
                dve.tensor_copy(aT[:, at:at + nb].rearrange("p b q -> p (b q)"), bank_b[:, 0:nb * P]
                                ).then_inc(moved_b, 1)

            def combine(i, u, first):
                nk = unit_keys(u)[1]
                c = i * PAIR + u
                for m in range(2):
                    dve.wait_ge(exped[m], c + 1)
                dve.reciprocal(rl1[:], l1[:]).then_inc(small, 1)
                dve.wait_ge(small, 2 * c + 1)
                dve.scalar_tensor_tensor(out=coef[:], in0=l0_all[:, bass.ds(c, 1)], scalar=rl1[:], in1=g.neg_lam[:],
                                         op0=ALU.mult, op1=ALU.mult).then_inc(small, 1)
                dve.wait_ge(small, 2 * c + 2)
                if not first:
                    dve.wait_ge(turned, i * PAIR_GROUPS + GROUPS_BEFORE[u])
                dve.scalar_tensor_tensor(out=a[:, 0:nk], in0=e[1][:, 0:nk], scalar=coef[:], in1=e[0][:, 0:nk],
                                         op0=ALU.mult, op1=ALU.add).then_inc(combined, 1)

            def body(i, peeled):
                for u in range(PAIR):
                    j, w = (i, u - 1) if u else (i - 1, PAIR - 1)
                    start = peeled and u == 0
                    row_max(i, u, 0, start)
                    row_max(i, u, 1, start)
                    if not start and len(block_groups(w)) > 1:
                        move(j, w)
                    combine(i, u, start)

            body(0, True)
            with dve.Fori(1, HEADS // 2) as i:
                body(i, False)
            move(HEADS // 2 - 1, PAIR - 1)
            dve.wait_ge(o_out, HEADS * UNITS)


def stage_attn_norm(nc, g, o_all, l0_all):
    N = HEADS * UNITS
    G = 2
    NG = N // G
    HG = UNITS // G
    with stage(nc, "an") as st:
        sq = st.sb("sq", [P, 2, UNITS, VD])
        ss, e2, var, std, scale = (st.sb(n, [P, N]) for n in ("ss", "e2", "var", "std", "scale"))
        oT = st.sb("oT", [P, 2, T])
        banks = [st.bank(f"t{i}") for i in range(4)]
        squared, summed, small, stdd, scaled, turned, out = (
            st.sem(n) for n in ("squared", "summed", "small", "stdd", "scaled", "turned", "out"))
        stored = [st.sem(f"stored{s}") for s in range(2)]
        block = st.block()

        @block.sync
        def _(sp):
            for h in range(HEADS):
                sp.wait_ge(out, (h + 1) * HG)
                sp.dma_start(g.oT[h], oT[:, h % 2]).then_inc(stored[h % 2], 16)
            for s in range(2):
                sp.wait_ge(stored[s], 16 * HEADS // 2)

        @block.scalar
        def _(act):
            for h in range(HEADS):
                if h >= 2:
                    act.wait_ge(summed, h - 1)
                act.activation(sq[:, h % 2], o_all[:, h * UNITS:(h + 1) * UNITS, :], ACT.Square).then_inc(squared, 1)
            act.wait_ge(small, 2)
            act.activation(std[:], var[:], ACT.Sqrt).then_inc(stdd, 1)
            for n in range(NG):
                h, u = divmod(n, HG)
                act.wait_ge(turned, n + 1)
                if h >= 2 and u == 0:
                    act.wait_ge(stored[h % 2], 16 * (h // 2))
                act.activation(oT[:, h % 2, u * G * P:(u + 1) * G * P], banks[n % 4][:, 0:G * P], ACT.Copy,
                               scale=g.subln[:]).then_inc(out, 1)

        @block.vector
        def _(dve):
            dve.tensor_tensor(e2[:], l0_all[:], l0_all[:], ALU.mult).then_inc(small, 1)
            for h in range(HEADS):
                dve.wait_ge(squared, h + 1)
                dve.tensor_reduce(ss[:, h * UNITS:(h + 1) * UNITS], sq[:, h % 2], AX.X, ALU.add).then_inc(summed, 1)
            dve.wait_ge(small, 1)
            dve.wait_ge(summed, HEADS)
            dve.scalar_tensor_tensor(out=var[:], in0=e2[:], scalar=EPS * VD, in1=ss[:], op0=ALU.mult, op1=ALU.add
                                     ).then_inc(small, 1)
            dve.wait_ge(stdd, 1)
            dve.reciprocal(scale[:], std[:]).then_inc(small, 1)
            dve.wait_ge(small, 3)
            for n in range(N):
                m = dve.tensor_scalar(o_all[:, n], o_all[:, n], scale[:, n:n + 1], VD ** 0.5, ALU.mult, ALU.mult)
                if n % G == G - 1:
                    m.then_inc(scaled, 1)

        @block.tensor
        def _(pe):
            for n in range(NG):
                pe.wait_ge(scaled, n + 1)
                if n >= 4:
                    pe.wait_ge(out, n - 3)
                for j in range(G):
                    mm = pe.transpose(banks[n % 4][:, j * P:(j + 1) * P], o_all[:, n * G + j], g.ident[:])
                mm.then_inc(turned, 1)


LAT_FT, CTX_FT = LAT // P, CTX // P
FTILES = LAT_FT + CTX_FT
HALF_T = [LAT // 2 // P, CTX // 2 // P]
HT = sum(HALF_T)
KU = 4
SPEC = 3
FILT_LAT_U, FILT_CTX_U = 2 * LAT_FT + 1, 2 * CTX_FT + 1
N_FILT_U = FILT_LAT_U + FILT_CTX_U
FWD_U = 2 * LAT_FT + 1
INV_U = 4 * HALF_T[0] + 1
TWO_PI_HI = 6.28125
TWO_PI_LO = 2 * math.pi - TWO_PI_HI
ROUND = 1.5 * 2.0 ** 23
PI_F = 3.1415925


def even_tile(j):
    return j < LAT_FT // 2 if j < LAT_FT else j - LAT_FT < CTX_FT // 2


def filter_units():
    lat = [(j, c) for j in range(LAT_FT) for c in range(2)]
    ctx = [(LAT_FT + j, c) for j in range(CTX_FT) for c in range(2)]
    return lat + [(0, 2)] + ctx + [(LAT_FT, 2)]


def stage_filters(nc, g):
    N = CTX + LAT
    NB = 4
    UN = filter_units()
    with stage(nc, "flt") as st:
        emb = st.sb("emb", [EMB, N])
        w1, w2 = st.sb("w1", [EMB, HID]), st.sb("w2", [HID, HID])
        w3 = st.sb("w3", [HID, 2, 2, CH])
        w3_hi, w3_lo = st.sb("w3hi", [HID, 2, 2, CH], F32R), st.sb("w3lo", [HID, 2, 2, CH], F32R)
        vec = st.sb("vec", [HID, 3])
        y, n, h = (st.sb(x, [HID, N]) for x in ("y", "n", "h"))
        h_hi, h_lo = st.sb("hhi", [HID, N], F32R), st.sb("hlo", [HID, N], F32R)
        decay = st.sb("decay", [P, 2 * HT, CH])
        wf = st.sb("wf", [P, FTILES])
        cb = st.sb("cb", [P, 2, CH])
        t = st.sb("t", [P, 4, CH])
        eo = st.sb("eo", [P, 5, CH])
        NL = 4 * HALF_T[0] + 1
        NX = 4 * HALF_T[1]
        x_hi, x_lo = st.sb("xhi", [P, NL + NX, CH], F32R), st.sb("xlo", [P, NL + NX, CH], F32R)
        raw = [st.sb(f"raw{s}", [P, KU, P]) for s in range(2)]
        t_hi = [st.sb(f"thi{s}", [P, KU, P], F32R) for s in range(2)]
        t_lo = [st.sb(f"tlo{s}", [P, KU, P], F32R) for s in range(2)]
        ob = [st.sb(f"ob{s}", [P, CH]) for s in range(2)]
        bank = [st.bank(f"b{i}") for i in range(8)]
        names = ("loaded mlp_mm mlp hs w3s taps copied mixed split_hi split_lo tab_hi tab_lo spec_mm scaled fix made").split()
        loaded, mlp_mm, mlp, hs, w3s, taps, copied, mixed, split_hi, split_lo, tab_hi, tab_lo, spec_mm, scaled, fix, made = (
            st.sem(x) for x in names)
        raw_in = [st.sem(f"raw_in{s}") for s in range(2)]
        stored = [st.sem(f"stored{s}") for s in range(2)]
        block = st.block()
        LOADS = 7
        MLP_CH = [(0, 512), (512, 512), (1024, 256)]
        PAIRS = HALF_T[0] + HALF_T[1]
        SLOTS = [0]
        for p in range(PAIRS):
            SLOTS.append(SLOTS[-1] + (5 if p == 0 else 4))

        def slots(p):
            if p < HALF_T[0]:
                base = [p, HALF_T[0] + p, 2 * HALF_T[0] + p, 3 * HALF_T[0] + p]
                return base + ([4 * HALF_T[0]] if p == 0 else [])
            return [NL + k for k in range(4)]

        def operands(j, c):
            H = HALF_T[0]
            if j >= LAT_FT:
                return [NL + 0, NL + 1] if c != 1 else [NL + 2, NL + 3]
            if c == 1:
                kind = 3 if even_tile(j) else 2
            else:
                kind = 0 if even_tile(j) else 1
            out = [kind * H + k for k in range(H)]
            if c != 1 and LAT_FT // 4 <= j < LAT_FT // 2:
                out[0] = 4 * H
            return out

        @block.sync
        def _(sp):
            for dst, src in ((emb[:], g.d["emb"]), (w1[:], g.d["filt_w1"]), (w2[:], g.d["filt_w2"]), (vec[:], g.d["filt_vec"]),
                             (w3[:], g.d["filt_w3"]), (decay[:], g.d["decay"]), (wf[:], g.d["wf"])):
                sp.dma_start(dst, src).then_inc(loaded, 16)
            total = 2 * len(UN)
            for m in range(2):
                sp.dma_start(raw[m][:], g.d["filt_tab"][m]).then_inc(raw_in[m], 16)
            for m in range(total):
                if m + 2 < total:
                    sp.wait_ge(tab_lo, m + 1)
                    sp.dma_start(raw[m % 2][:], g.d["filt_tab"][(m + 2) % len(UN)]).then_inc(raw_in[m % 2], 16)
                sp.wait_ge(scaled, m + 1)
                o, (j, c) = m // len(UN), UN[m % len(UN)]
                sp.dma_start(g.spec[o, j, :, c, :], ob[m % 2][:]).then_inc(stored[m % 2], 16)
            for s in range(2):
                sp.wait_ge(stored[s], 16 * (total // 2))

        @block.tensor
        def _(pe):
            pe.wait_ge(loaded, 16 * LOADS)
            for layer in range(2):
                if layer:
                    pe.wait_ge(mlp, 5)
                w, x = (w1, emb) if layer == 0 else (w2, h)
                for i, (at, m) in enumerate(MLP_CH):
                    mm = pe.matmul(bank[i][0:HID, 0:m], w[:], x[:, at:at + m], start=True, stop=True)
                mm.then_inc(mlp_mm, 1)
            pe.wait_ge(hs, 2)
            pe.wait_ge(w3s, 2)

            def taps_of(o, p):
                k = o * PAIRS + p
                if k:
                    pe.wait_ge(mixed, k)
                for i in range(4):
                    tile = 2 * p + i // 2
                    mm = products(pe, bank[i][:], h_hi[:, tile * P:(tile + 1) * P], h_lo[:, tile * P:(tile + 1) * P],
                                  w3_hi[:, i % 2, o], w3_lo[:, i % 2, o], True, True)
                mm.then_inc(taps, 1)

            for o in range(2):
                for p in range(PAIRS):
                    taps_of(o, p)
                for u, (j, c) in enumerate(UN):
                    m = o * len(UN) + u
                    pe.wait_ge(tab_lo, m + 1)
                    if u == 0:
                        pe.wait_ge(split_lo, (o + 1) * SLOTS[PAIRS])
                    if m >= NB:
                        pe.wait_ge(scaled, m - NB + 1)
                    ops = operands(j, c)
                    for k, x in enumerate(ops):
                        mm = products(pe, bank[4 + m % NB][:], t_hi[m % 2][:, k], t_lo[m % 2][:, k], x_hi[:, x],
                                      x_lo[:, x], k == 0, k == len(ops) - 1)
                    mm.then_inc(spec_mm, 1)

        @block.scalar
        def _(act):
            act.wait_ge(loaded, 16 * LOADS)
            act.activation(w3_hi[:], w3[:], ACT.Copy).then_inc(w3s, 1)
            for layer in range(2):
                act.wait_ge(mlp, 5 * layer + 4)
                act.activation(h[:], y[:], ACT.Sin).then_inc(mlp, 1)
            act.wait_ge(mlp, 10)
            act.activation(h_hi[:], h[:], ACT.Copy).then_inc(hs, 1)

            def table(m):
                act.wait_ge(raw_in[m % 2], 16 * (m // 2 + 1))
                if m >= 2:
                    act.wait_ge(spec_mm, m - 1)
                act.activation(t_hi[m % 2][:], raw[m % 2][:], ACT.Copy).then_inc(tab_hi, 1)

            for o in range(2):
                if o:
                    act.wait_ge(spec_mm, len(UN))
                for p in range(PAIRS):
                    k = o * PAIRS + p
                    act.wait_ge(taps, k + 1)
                    if k:
                        act.wait_ge(mixed, k)
                    for i in range(2):
                        a = act.activation(cb[:, i], bank[2 * i + 1][:], ACT.Copy)
                    a.then_inc(copied, 1)
                    for i, x in enumerate(slots(p)):
                        if i == 0:
                            act.wait_ge(made, k + 1)
                        act.activation(x_hi[:, x], eo[:, i], ACT.Copy).then_inc(split_hi, 1)
                for u in range(len(UN)):
                    table(o * len(UN) + u)

        @block.gpsimd
        def _(pool):
            pool.wait_ge(w3s, 1)
            pool.tensor_tensor(w3_lo[:], w3[:], w3_hi[:], ALU.subtract).then_inc(w3s, 1)
            pool.wait_ge(hs, 1)
            pool.tensor_tensor(h_lo[:], h[:], h_hi[:], ALU.subtract).then_inc(hs, 1)
            for o in range(2):
                for p in range(PAIRS):
                    for i, x in enumerate(slots(p)):
                        pool.wait_ge(split_hi, o * SLOTS[PAIRS] + SLOTS[p] + i + 1)
                        pool.tensor_tensor(x_lo[:, x], eo[:, i], x_hi[:, x], ALU.subtract).then_inc(split_lo, 1)
                for u in range(len(UN)):
                    m = o * len(UN) + u
                    pool.wait_ge(tab_hi, m + 1)
                    pool.tensor_tensor(t_lo[m % 2][:], raw[m % 2][:], t_hi[m % 2][:], ALU.subtract).then_inc(tab_lo, 1)

        @block.vector
        def _(dve):
            dve.wait_ge(loaded, 16 * LOADS)
            for layer in range(2):
                dve.wait_ge(mlp_mm, layer + 1)
                base = 5 * layer
                for i, (at, m) in enumerate(MLP_CH):
                    a = dve.tensor_scalar(y[:, at:at + m], bank[i][0:HID, 0:m], vec[:, layer:layer + 1], vec[:, 2:3],
                                          ALU.add, ALU.mult)
                a.then_inc(mlp, 1)
                dve.wait_ge(mlp, base + 1)
                dve.tensor_scalar(n[:], y[:], 1 / (2 * math.pi), ROUND, ALU.mult, ALU.add).then_inc(fix, 1)
                dve.wait_ge(fix, 2 * layer + 1)
                dve.tensor_scalar(n[:], n[:], -ROUND, None, ALU.add).then_inc(fix, 1)
                dve.wait_ge(fix, 2 * layer + 2)
                dve.scalar_tensor_tensor(out=y[:], in0=n[:], scalar=-TWO_PI_HI, in1=y[:], op0=ALU.mult, op1=ALU.add
                                         ).then_inc(mlp, 1)
                dve.wait_ge(mlp, base + 2)
                dve.scalar_tensor_tensor(out=y[:], in0=n[:], scalar=-TWO_PI_LO, in1=y[:], op0=ALU.mult, op1=ALU.add
                                         ).then_inc(mlp, 1)
                dve.wait_ge(mlp, base + 3)
                dve.tensor_scalar(y[:], y[:], PI_F, -PI_F, ALU.min, ALU.max).then_inc(mlp, 1)
            done = [4]

            def step(ins):
                ins.then_inc(fix, 1)
                done[0] += 1
                dve.wait_ge(fix, done[0])

            def pair(o, p):
                k = o * PAIRS + p
                S0 = o * SLOTS[PAIRS] + SLOTS[p]
                if k:
                    dve.wait_ge(split_lo, S0)
                dve.wait_ge(copied, k + 1)
                for i in range(2):
                    dve.tensor_tensor(t[:, i], bank[2 * i][:], cb[:, i], ALU.add)
                    a = dve.tensor_tensor(t[:, 2 + i], bank[2 * i][:], cb[:, i], ALU.subtract)
                a.then_inc(mixed, 1)
                dve.wait_ge(mixed, k + 1)
                lat = p < HALF_T[0]
                for i in range(2):
                    dst = t if lat else eo
                    dve.tensor_tensor(dst[:, i], t[:, i], decay[:, 2 * p + i], ALU.mult)
                    a = dve.tensor_tensor(dst[:, 2 + i], t[:, 2 + i], decay[:, 2 * p + i], ALU.mult)
                step(a)
                if lat:
                    for i in range(2):
                        dve.tensor_tensor(eo[:, 2 * i], t[:, 2 * i], t[:, 2 * i + 1], ALU.add)
                        a = dve.tensor_tensor(eo[:, 2 * i + 1], t[:, 2 * i], t[:, 2 * i + 1], ALU.subtract)
                    step(a)
                if p == 0:
                    step(dve.tensor_copy(eo[:, 4], eo[:, 0]))
                    step(dve.tensor_copy(eo[0:1, 4], eo[0:1, 1]))
                    step(dve.tensor_copy(eo[0:1, 1], t[0:1, 0]))
                    step(dve.tensor_copy(eo[0:1, 2], t[0:1, 3]))
                dve.sem_inc(made, 1)

            for o in range(2):
                for p in range(PAIRS):
                    pair(o, p)
                for u, (j, c) in enumerate(UN):
                    m = o * len(UN) + u
                    dve.wait_ge(spec_mm, m + 1)
                    if m >= 2:
                        dve.wait_ge(stored[m % 2], 16 * (m // 2))
                    dve.tensor_scalar(ob[m % 2][:], bank[4 + m % NB][:], wf[:, j:j + 1], None, ALU.mult
                                      ).then_inc(scaled, 1)


def stored_columns(mirror, tile):
    first, L, tile = (CTX, LAT, tile) if tile < HALF_T[0] else (0, CTX, tile - HALF_T[0])
    first += mirror * (L // 2)
    return slice(first + tile * P, first + (tile + 1) * P)


def folded_columns(mirror, tile):
    if not mirror:
        return stored_columns(mirror, tile)
    first, L, tile = (CTX, LAT, tile) if tile < HALF_T[0] else (0, CTX, tile - HALF_T[0])
    last = first + L - 1 - tile * P
    return slice(last, last - P if last >= P else None, -1)


def stage_short_conv(nc, g, z):
    NT = 3 * CHT
    PAD = T + 3
    with stage(nc, "sc") as st:
        u = [st.sb(f"u{s}", [P, PAD]) for s in range(2)]
        acc = [st.sb(f"acc{s}", [P, T]) for s in range(2)]
        out = st.sb("out", [P, 2 * CHT, T])
        x2 = [st.sb(f"x2{s}", [P, T]) for s in range(2)]
        cw = st.sb("cw", [P, NT, 4])
        x1 = st.sb("x1", [P, 2, HT, CH])
        bank = [st.bank(f"b{i}") for i in range(4)]
        cached = st.sem("cached")
        cleared, w_in, mid, conv, turned, moved, x1_out = (
            st.sem(x) for x in ("cleared", "w_in", "mid", "conv", "turned", "moved", "x1_out"))
        u_in = [st.sem(f"u_in{s}") for s in range(2)]
        stored = [st.sem(f"stored{s}") for s in range(2)]
        block = st.block()
        AT = [(1, 0, CTX), (CTX + 2, CTX, LAT)]
        JOBS = []
        for src in range(2):
            for mirror in range(2):
                for tile in range(HT):
                    JOBS.append((src, mirror, tile))

        @block.sync
        def _(sp):
            sp.dma_start(cw[:], g.d["conv"]).then_inc(w_in, 16)
            sp.dma_start(g.new_k, g.projT[Q_U:Q_U + K_U, :, 0:CTX]).then_inc(cached, 16)
            sp.dma_start(g.new_v, g.v[0:CTX // P]).then_inc(cached, 16)
            sp.wait_ge(cleared, 1)
            for n in range(NT + 1):
                if n < NT:
                    if n >= 2:
                        sp.wait_ge(conv, n - 1)
                    for col, tok, m in AT:
                        sp.dma_start(u[n % 2][:, col:col + m], g.projT[Q_U + K_U + n, :, tok:tok + m]
                                     ).then_inc(u_in[n % 2], 16)
                if n - 1 >= 2 * CHT:
                    x = n - 1
                    sp.wait_ge(conv, x + 1)
                    sp.dma_start(g.x2T[x - 2 * CHT], x2[x % 2][:]).then_inc(stored[x % 2], 16)
            for n in range(HT):
                sp.wait_ge(moved, 3 * HT + n + 1)
                sp.dma_start(g.x1t[n], x1[:, :, n]).then_inc(x1_out, 16)
            for s in range(2):
                sp.wait_ge(stored[s], 16 * (CHT // 2))
            sp.wait_ge(x1_out, 16 * HT)
            sp.wait_ge(cached, 32)

        @block.vector
        def _(dve):
            for s in range(2):
                m = dve.memset(u[s][:], 0.0)
            m.then_inc(cleared, 1)
            dve.wait_ge(w_in, 16)
            for n in range(NT):
                s = n % 2
                dve.wait_ge(u_in[s], 32 * (n // 2 + 1))
                dst = out[:, n] if n < 2 * CHT else x2[s][:]
                if n >= 2 * CHT + 2:
                    dve.wait_ge(stored[s], 16 * ((n - 2 * CHT) // 2))
                for k, (col, tok, m) in enumerate(AT):
                    a = dve.tensor_scalar(acc[s][:, tok:tok + m], u[s][:, col:col + m], cw[:, n, 1:2], cw[:, n, 3:4],
                                          ALU.mult, ALU.add)
                a.then_inc(mid, 1)
                dve.wait_ge(mid, 2 * n + 1)
                for k, (col, tok, m) in enumerate(AT):
                    a = dve.scalar_tensor_tensor(out=acc[s][:, tok:tok + m], in0=u[s][:, col - 1:col - 1 + m],
                                                 scalar=cw[:, n, 0:1], in1=acc[s][:, tok:tok + m], op0=ALU.mult,
                                                 op1=ALU.add)
                a.then_inc(mid, 1)
                dve.wait_ge(mid, 2 * n + 2)
                for k, (col, tok, m) in enumerate(AT):
                    for at, to in ((0, slice(tok, tok + m // 2)),
                                   (m // 2, slice(tok + m - 1, tok + m // 2 - 1, -1))):
                        a = dve.scalar_tensor_tensor(out=dst[:, to], in0=u[s][:, col + 1 + at:col + 1 + at + m // 2],
                                                     scalar=cw[:, n, 2:3],
                                                     in1=acc[s][:, tok + at:tok + at + m // 2], op0=ALU.mult,
                                                     op1=ALU.add)
                a.then_inc(conv, 1)
                dve.wait_ge(conv, n + 1)

        @block.tensor
        def _(pe):
            for n, (src, mirror, tile) in enumerate(JOBS):
                if n % (2 * HT) == 0:
                    pe.wait_ge(conv, CHT * (src + 1))
                if n >= 4:
                    pe.wait_ge(moved, n - 3)
                for c in range(CHT):
                    mm = pe.transpose(bank[n % 4][:, c * P:(c + 1) * P], out[:, src * CHT + c, stored_columns(mirror, tile)],
                                      g.ident[:])
                mm.then_inc(turned, 1)

        @block.scalar
        def _(act):
            for n, (src, mirror, tile) in enumerate(JOBS):
                act.wait_ge(turned, n + 1)
                dst = x1[:, mirror, tile] if src else z[mirror][:, tile]
                act.activation(dst, bank[n % 4][:], ACT.Copy).then_inc(moved, 1)
            act.wait_ge(moved, len(JOBS))


FWD_RUNS = 2 * FTILES
RUNS = FWD_RUNS + 4 * HT
NU = FWD_U + INV_U


def runs_after_unit(m):
    o, u = divmod(m, NU)
    if u < FWD_U - 1:
        n = u + 1
    elif u == FWD_U - 1:
        n = FWD_RUNS
    elif u < NU - 1:
        n = FWD_RUNS + u - FWD_U + 1
    else:
        n = RUNS
    return o * RUNS + n


def next_units(o, j=None, tile=None):
    if j is not None:
        u = [2 * j, 2 * j + 1] if j < LAT_FT else [FWD_U - 1] if j == FTILES - 1 else []
    else:
        u = [FWD_U + 4 * tile + k for k in range(4)] if tile < HALF_T[0] else [NU - 1]
    return [m for m in (o * NU + x + 2 for x in u) if m < 2 * NU]


def stage_hyena(nc, g, z):
    with stage(nc, "hy") as st:
        e_hi, e_lo, o_hi, o_lo = (st.sb(x, [P, HT, CH], F32R) for x in ("ehi", "elo", "ohi", "olo"))
        gc_hi, gc_lo, gs_hi, gs_lo = (st.sb(x, [P, FTILES, CH], F32R) for x in ("gchi", "gclo", "gshi", "gslo"))
        raw = [st.sb(f"raw{s}", [P, KU, P]) for s in range(2)]
        t_hi = [st.sb(f"thi{s}", [P, KU, P], F32R) for s in range(2)]
        t_lo = [st.sb(f"tlo{s}", [P, KU, P], F32R) for s in range(2)]
        spec = [st.sb(f"spec{s}", [P, SPEC, CH]) for s in range(2)]
        scr = [st.sb(f"scr{s}", [P, 4, CH]) for s in range(2)]
        gate = [st.sb(f"gate{s}", [P, 2, CH]) for s in range(2)]
        p_sb = [st.sb(f"p{s}", [P, CH]) for s in range(2)]
        bias = st.sb("bias_b", [P, 2, CH])
        bank = [st.bank(f"b{i}") for i in range(8)]
        names = ("bias_in", "runs", "tab_hi", "tab_lo", "folded", "fold_hi", "fold_lo", "fwd_read", "g_ready", "g_hi",
                 "g_lo", "biased", "p_copied", "q_read", "zdone", "step")
        (bias_in, runs, tab_hi, tab_lo, folded, fold_hi, fold_lo, fwd_read, g_ready, g_hi, g_lo, biased, p_copied,
         q_read, zdone, step_sem) = (st.sem(x) for x in names)
        raw_in = [st.sem(f"raw_in{s}") for s in range(2)]
        spec_in = [st.sem(f"spec_in{s}") for s in range(2)]
        gate_in = [st.sem(f"gate_in{s}") for s in range(2)]
        block = st.block()

        def spectra(j):
            return SPEC if j in (0, LAT_FT) else 2

        @block.sync
        def _(sp):
            def load(m):
                sp.dma_start(raw[m % 2][:], g.d["hy_tab"][m % NU]).then_inc(raw_in[m % 2], 16)

            def load_spec(n):
                o, j = divmod(n, FTILES)
                if n >= 2:
                    sp.wait_ge(fwd_read, n - 1)
                sp.dma_start(spec[n % 2][:, 0:spectra(j)], g.spec[o, j, :, 0:spectra(j), :]
                             ).then_inc(spec_in[n % 2], 16)

            def load_gate(i):
                if i >= 2:
                    sp.wait_ge(zdone, i - 1)
                sp.dma_start(gate[i % 2][:], g.x1t[i]).then_inc(gate_in[i % 2], 16)

            sp.dma_start(bias[:], g.d["hy_bias"]).then_inc(bias_in, 16)
            for m in range(2):
                load(m)
                load_spec(m)
                load_gate(m)
            for o in range(2):
                for j in range(FTILES):
                    for m in next_units(o, j=j):
                        sp.wait_ge(tab_lo, m - 1)
                        load(m)
                    if o * FTILES + j + 2 < 2 * FTILES:
                        load_spec(o * FTILES + j + 2)
                for i in range(HT):
                    for m in next_units(o, tile=i):
                        sp.wait_ge(tab_lo, m - 1)
                        load(m)
                    if o == 0 and i + 2 < HT:
                        load_gate(i + 2)

        @block.tensor
        def _(pe):
            for o in range(2):
                pe.wait_ge(fold_lo, (o + 1) * HT)
                for j in range(FTILES):
                    n = o * FTILES + j
                    if n >= 2:
                        pe.wait_ge(fwd_read, n - 1)
                    for c in range(2):
                        hi, lo = (e_hi, e_lo) if even_tile(j) == (c == 0) else (o_hi, o_lo)
                        if j < LAT_FT:
                            unit, at, tiles = 2 * j + c, 0, range(HALF_T[0])
                        else:
                            unit, at, tiles = FWD_U - 1, 2 * (j - LAT_FT) + c, range(HALF_T[0], HT)
                        m = o * NU + unit
                        pe.wait_ge(tab_lo, m + 1)
                        for k, tile in enumerate(tiles):
                            mm = products(pe, bank[2 * (n % 2) + c][:], t_hi[m % 2][:, at + k], t_lo[m % 2][:, at + k],
                                          hi[:, tile], lo[:, tile], k == 0, k == len(tiles) - 1)
                        mm.then_inc(runs, 1)
                for i in range(HT):
                    n = o * HT + i
                    if n >= 2:
                        pe.wait_ge(q_read, n - 1)
                    for q in range(2):
                        for half in range(2):
                            hi, lo = (gs_hi, gs_lo) if half else (gc_hi, gc_lo)
                            odd = half ^ q
                            if i < HALF_T[0]:
                                unit, at = FWD_U + 4 * i + 2 * q + half, 0
                                tiles = range(LAT_FT // 2 * odd, LAT_FT // 2 * (odd + 1))
                            else:
                                unit, at, tiles = NU - 1, 2 * q + half, range(LAT_FT + odd, LAT_FT + odd + 1)
                            m = o * NU + unit
                            pe.wait_ge(tab_lo, m + 1)
                            if q == 0 and half == 0 and i == 0:
                                pe.wait_ge(g_lo, 2 * (o + 1) * FTILES)
                            for k, tile in enumerate(tiles):
                                mm = products(pe, bank[4 + 2 * (n % 2) + q][:], t_hi[m % 2][:, at + k],
                                              t_lo[m % 2][:, at + k], hi[:, tile], lo[:, tile],
                                              half == 0 and k == 0, half == 1 and k == len(tiles) - 1)
                            mm.then_inc(runs, 1)

        @block.scalar
        def _(act):
            def table(m):
                act.wait_ge(raw_in[m % 2], 16 * (m // 2 + 1))
                if m >= 2:
                    act.wait_ge(runs, runs_after_unit(m - 2))
                act.activation(t_hi[m % 2][:], raw[m % 2][:], ACT.Copy).then_inc(tab_hi, 1)

            def split_fold(n):
                act.wait_ge(folded, n + 1)
                act.activation(e_hi[:, n % HT], scr[n % 2][:, 0], ACT.Copy).then_inc(fold_hi, 1)
                act.activation(o_hi[:, n % HT], scr[n % 2][:, 1], ACT.Copy).then_inc(fold_hi, 1)

            for i in range(HT):
                split_fold(i)
            for m in range(2):
                table(m)
            for o in range(2):
                for j in range(FTILES):
                    for m in next_units(o, j=j):
                        table(m)
                    n = o * FTILES + j
                    act.wait_ge(g_ready, n + 1)
                    act.activation(gc_hi[:, j], scr[n % 2][:, 0], ACT.Copy).then_inc(g_hi, 1)
                    act.activation(gs_hi[:, j], scr[n % 2][:, 2], ACT.Copy).then_inc(g_hi, 1)
                for i in range(HT):
                    for m in next_units(o, tile=i):
                        table(m)
                    n = o * HT + i
                    act.wait_ge(runs, o * RUNS + FWD_RUNS + 4 * (i + 1))
                    if n >= 2:
                        act.wait_ge(q_read, n - 1)
                    act.activation(p_sb[n % 2][:], bank[4 + 2 * (n % 2)][:], ACT.Copy).then_inc(p_copied, 1)
                    if o == 0 and i:
                        split_fold(HT + i - 1)
                if o == 0:
                    split_fold(2 * HT - 1)

        @block.gpsimd
        def _(pool):
            def table(m):
                pool.wait_ge(tab_hi, m + 1)
                pool.tensor_tensor(t_lo[m % 2][:], raw[m % 2][:], t_hi[m % 2][:], ALU.subtract).then_inc(tab_lo, 1)

            def split_fold(n):
                pool.wait_ge(fold_hi, 2 * n + 2)
                pool.tensor_tensor(e_lo[:, n % HT], scr[n % 2][:, 0], e_hi[:, n % HT], ALU.subtract)
                pool.tensor_tensor(o_lo[:, n % HT], scr[n % 2][:, 1], o_hi[:, n % HT], ALU.subtract
                                   ).then_inc(fold_lo, 1)

            pool.wait_ge(bias_in, 16)
            for i in range(HT):
                split_fold(i)
            for m in range(2):
                table(m)
            for o in range(2):
                for j in range(FTILES):
                    for m in next_units(o, j=j):
                        table(m)
                    n = o * FTILES + j
                    pool.wait_ge(g_hi, 2 * n + 2)
                    pool.tensor_tensor(gc_lo[:, j], scr[n % 2][:, 0], gc_hi[:, j], ALU.subtract).then_inc(g_lo, 1)
                    pool.tensor_tensor(gs_lo[:, j], scr[n % 2][:, 2], gs_hi[:, j], ALU.subtract).then_inc(g_lo, 1)
                pool.wait_ge(g_lo, 2 * (o + 1) * FTILES)
                for i in range(HT):
                    n = o * HT + i
                    if i >= 2:
                        pool.wait_ge(zdone, n - 1)
                    for h in range(2):
                        m = pool.tensor_tensor(scr[n % 2][:, 2 + h], z[h][:, i], bias[:, o], ALU.mult)
                    m.then_inc(biased, 1)
                    for m in next_units(o, tile=i):
                        table(m)
                    if o == 0 and i:
                        split_fold(HT + i - 1)
                if o == 0:
                    split_fold(2 * HT - 1)

        @block.vector
        def _(dve):
            n_steps = [0]

            def step(ins):
                ins.then_inc(step_sem, 1)
                n_steps[0] += 1
                dve.wait_ge(step_sem, n_steps[0])

            def fold(n):
                if n >= 2:
                    dve.wait_ge(fold_lo, n - 1)
                i = n % HT
                dve.tensor_tensor(scr[n % 2][:, 0], z[0][:, i], z[1][:, i], ALU.add)
                dve.tensor_tensor(scr[n % 2][:, 1], z[0][:, i], z[1][:, i], ALU.subtract).then_inc(folded, 1)

            for i in range(HT):
                fold(i)
            dve.wait_ge(fold_lo, HT)
            for o in range(2):
                for j in range(FTILES):
                    n = o * FTILES + j
                    w, sp_, c, s = scr[n % 2], spec[n % 2], bank[2 * (n % 2)], bank[2 * (n % 2) + 1]
                    dve.wait_ge(runs, o * RUNS + 2 * j + 2)
                    dve.wait_ge(spec_in[n % 2], 16 * (n // 2 + 1))
                    if n >= 2:
                        dve.wait_ge(g_lo, 2 * n - 2)
                    dve.tensor_tensor(w[:, 0], c[:], sp_[:, 0], ALU.mult)
                    dve.tensor_tensor(w[:, 1], s[:], sp_[:, 1], ALU.mult)
                    dve.tensor_tensor(w[:, 2], s[:], sp_[:, spectra(j) - 1 if spectra(j) == SPEC else 0], ALU.mult)
                    dve.tensor_tensor(w[:, 3], c[:], sp_[:, 1], ALU.mult).then_inc(fwd_read, 1)
                    dve.wait_ge(fwd_read, n + 1)
                    dve.tensor_tensor(w[:, 0], w[:, 0], w[:, 1], ALU.subtract)
                    dve.tensor_tensor(w[:, 2], w[:, 2], w[:, 3], ALU.add).then_inc(g_ready, 1)
                for i in range(HT):
                    n = o * HT + i
                    q = bank[4 + 2 * (n % 2) + 1]
                    dve.wait_ge(p_copied, n + 1)
                    dve.wait_ge(biased, n + 1)
                    if o == 0:
                        dve.wait_ge(gate_in[i % 2], 16 * (i // 2 + 1))
                    dve.tensor_tensor(z[0][:, i], p_sb[n % 2][:], q[:], ALU.add)
                    dve.tensor_tensor(z[1][:, i], p_sb[n % 2][:], q[:], ALU.subtract).then_inc(q_read, 1)
                    dve.wait_ge(q_read, n + 1)
                    for h in range(2):
                        a = dve.tensor_tensor(z[h][:, i], z[h][:, i], scr[n % 2][:, 2 + h], ALU.add)
                    if o == 0:
                        step(a)
                        for h in range(2):
                            a = dve.tensor_tensor(z[h][:, i], z[h][:, i], gate[i % 2][:, h], ALU.mult)
                    a.then_inc(zdone, 1)
                    dve.wait_ge(zdone, n + 1)
                    if o == 0:
                        fold(HT + i)


def stage_hyena_out(nc, g, z):
    JOBS = [(m, tile) for m in range(2) for tile in range(HT)]
    with stage(nc, "ho") as st:
        x2 = st.sb("x2", [P, CHT, T])
        o = st.sb("o", [P, CHT, T])
        bank = [st.bank(f"b{i}") for i in range(4)]
        x_in, turned, gated, stored = (st.sem(x) for x in ("x_in", "turned", "gated", "stored"))
        block = st.block()

        @block.sync
        def _(sp):
            sp.dma_start(x2[:], g.x2T.rearrange("c p t -> p c t")).then_inc(x_in, 16)
            sp.wait_ge(gated, len(JOBS))
            sp.dma_start(g.ohT.rearrange("c p t -> p c t"), o[:]).then_inc(stored, 16)
            sp.wait_ge(stored, 16)

        @block.tensor
        def _(pe):
            for n, (m, tile) in enumerate(JOBS):
                if n >= 4:
                    pe.wait_ge(gated, n - 3)
                for c in range(CHT):
                    mm = pe.transpose(bank[n % 4][:, c * P:(c + 1) * P], z[m][:, tile, c * P:(c + 1) * P], g.ident[:])
                mm.then_inc(turned, 1)

        @block.vector
        def _(dve):
            dve.wait_ge(x_in, 16)
            for n, (m, tile) in enumerate(JOBS):
                dve.wait_ge(turned, n + 1)
                cols = folded_columns(m, tile)
                dve.tensor_tensor(o[:, :, cols], bank[n % 4][:].rearrange("p (c t) -> p c t", c=CHT),
                                  x2[:, :, stored_columns(m, tile)], ALU.mult).then_inc(gated, 1)


GATE1, SHIFT2, SCALE2, GATE2 = (n * KD for n in (2, 3, 4, 5))
SEG_OF = [0, 1, 1]


def stage_merge(nc, g):
    K = HEADS + CHT
    with stage(nc, "mg") as st:
        o_raw = [st.sb(f"oraw{s}", [P, T]) for s in range(2)]
        o_hi, o_lo = (st.sb(x, [P, K, T], F32R) for x in ("ohi", "olo"))
        raw = [st.sb(f"raw{s}", [P, K, P]) for s in range(2)]
        w_hi = [st.sb(f"whi{s}", [P, K, P], F32R) for s in range(2)]
        w_lo = [st.sb(f"wlo{s}", [P, K, P], F32R) for s in range(2)]
        gate = [st.sb(f"gate{s}", [P, 2, T]) for s in range(2)]
        bank = [[st.bank(f"{x}{c}") for c in range(NC)] for x in "ah"]
        raw_in, o_in, gate_in, stored = ([st.sem(f"{n}{s}") for s in range(2)] for n in
                                         ("raw_in", "o_in", "gate_in", "stored"))
        hi_done, lo_done, o_h, o_l, sig, mm, gated, summed = (
            st.sem(x) for x in ("hi_done", "lo_done", "oh_h", "oh_l", "sig", "mm", "gated", "summed"))
        block = st.block()

        @block.sync
        def _(sp):
            def load_w(n, s):
                sp.dma_start(raw[s][:], g.d["w_br"][n]).then_inc(raw_in[s], 16)

            def load_gates(n, s):
                for h in range(2):
                    sp.dma_start(gate[s][:, h], g.projT[Q_U + K_U + U_U + h * KD + n]).then_inc(gate_in[s], 16)

            for s in range(2):
                load_w(s, s)
                sp.dma_start(o_raw[s][:], g.ohT[s]).then_inc(o_in[s], 16)
            for k in range(2, K):
                sp.wait_ge(o_l, k - 1)
                sp.dma_start(o_raw[k % 2][:], g.ohT[k] if k < CHT else g.oT[k - CHT]).then_inc(o_in[k % 2], 16)
            for s in range(2):
                load_gates(s, s)
            for n in range(KD):
                s = n % 2
                if n + 2 < KD:
                    sp.wait_ge(lo_done, n + 1)
                    load_w(n + 2, s)
                sp.wait_ge(summed, NC * (n + 1))
                sp.dma_start(g.mT[n], gate[s][:, 0]).then_inc(stored[s], 16)
                if n + 2 < KD:
                    sp.wait_ge(stored[s], 16 * (n // 2 + 1))
                    load_gates(n + 2, s)
            for s in range(2):
                sp.wait_ge(stored[s], 16 * KD // 2)

        @block.scalar
        def _(act):
            def weights(n):
                s = n % 2
                act.wait_ge(raw_in[s], 16 * (n // 2 + 1))
                if n >= 2:
                    act.wait_ge(mm, NC * (n - 1))
                act.activation(w_hi[s][:], raw[s][:], ACT.Copy).then_inc(hi_done, 1)

            def gates(n):
                s = n % 2
                act.wait_ge(gate_in[s], 32 * (n // 2 + 1))
                act.activation(gate[s][:], gate[s][:], ACT.Sigmoid).then_inc(sig, 1)

            weights(0)
            weights(1)
            for k in range(K):
                act.wait_ge(o_in[k % 2], 16 * (k // 2 + 1))
                act.activation(o_hi[:, k], o_raw[k % 2][:], ACT.Copy).then_inc(o_h, 1)
            gates(0)
            gates(1)
            for n in range(2, KD):
                weights(n)
                gates(n)

        @block.gpsimd
        def _(pool):
            def weights(n):
                pool.wait_ge(hi_done, n + 1)
                pool.tensor_tensor(w_lo[n % 2][:], raw[n % 2][:], w_hi[n % 2][:], ALU.subtract).then_inc(lo_done, 1)

            weights(0)
            weights(1)
            for n in range(KD):
                for c, (at, m) in enumerate(CHUNKS):
                    pool.wait_ge(gated, n * NC + c + 1)
                    gt = gate[n % 2]
                    pool.tensor_tensor(gt[:, 0, at:at + m], gt[:, 0, at:at + m], gt[:, 1, at:at + m], ALU.add
                                       ).then_inc(summed, 1)
                if n + 2 < KD:
                    weights(n + 2)

        @block.tensor
        def _(pe):
            for n in range(KD):
                s = n % 2
                pe.wait_ge(lo_done, n + 1)
                for c, (at, m) in enumerate(CHUNKS):
                    if n:
                        pe.wait_ge(gated, (n - 1) * NC + c + 1)
                    for k in range(K):
                        if n == 0 and c == 0:
                            pe.wait_ge(o_l, k + 1)
                        a = products(pe, bank[k < CHT][c][:, 0:m], w_hi[s][:, k], w_lo[s][:, k],
                                     o_hi[:, k, at:at + m], o_lo[:, k, at:at + m], k in (0, CHT), k in (CHT - 1, K - 1))
                    a.then_inc(mm, 1)

        @block.vector
        def _(dve):
            for k in range(K):
                dve.wait_ge(o_h, k + 1)
                dve.tensor_tensor(o_lo[:, k], o_raw[k % 2][:], o_hi[:, k], ALU.subtract).then_inc(o_l, 1)
            for n in range(KD):
                dve.wait_ge(sig, n + 1)
                for c, (at, m) in enumerate(CHUNKS):
                    dve.wait_ge(mm, n * NC + c + 1)
                    for h in range(2):
                        part = gate[n % 2][:, h, at:at + m]
                        a = dve.tensor_tensor(part, part, bank[h][c][:, 0:m], ALU.mult)
                    a.then_inc(gated, 1)


def stage_out(nc, g, x1):
    with stage(nc, "ou") as st:
        m_raw = [st.sb(f"mraw{s}", [P, T]) for s in range(2)]
        m_hi, m_lo = (st.sb(x, [P, KD, T], F32R) for x in ("mhi", "mlo"))
        raw = [st.sb(f"raw{s}", [P, KD, P]) for s in range(2)]
        w_hi = [st.sb(f"whi{s}", [P, KD, P], F32R) for s in range(2)]
        w_lo = [st.sb(f"wlo{s}", [P, KD, P], F32R) for s in range(2)]
        bank = [st.bank(f"b{i}") for i in range(BANKS)]
        raw_in, m_in = ([st.sem(f"{n}{s}") for s in range(2)] for n in ("raw_in", "m_in"))
        x_in, hi_done, lo_done, m_h, m_l, mm, added = (
            st.sem(x) for x in ("x_in", "hi_done", "lo_done", "m_h", "m_l", "mm", "added"))
        block = st.block()

        @block.sync
        def _(sp):
            for s in range(2):
                sp.dma_start(raw[s][:], g.d["w_out"][s]).then_inc(raw_in[s], 16)
                sp.dma_start(m_raw[s][:], g.mT[s]).then_inc(m_in[s], 16)
            sp.dma_start(x1[:], g.d["xT"].rearrange("k p t -> p k t")).then_inc(x_in, 16)
            for k in range(2, KD):
                sp.wait_ge(m_l, k - 1)
                sp.dma_start(m_raw[k % 2][:], g.mT[k]).then_inc(m_in[k % 2], 16)
            for n in range(2, KD):
                sp.wait_ge(lo_done, n - 1)
                sp.dma_start(raw[n % 2][:], g.d["w_out"][n]).then_inc(raw_in[n % 2], 16)

        @block.scalar
        def _(act):
            def weights(n):
                s = n % 2
                act.wait_ge(raw_in[s], 16 * (n // 2 + 1))
                if n >= 2:
                    act.wait_ge(mm, NC * (n - 1))
                act.activation(w_hi[s][:], raw[s][:], ACT.Copy).then_inc(hi_done, 1)

            weights(0)
            for k in range(KD):
                act.wait_ge(m_in[k % 2], 16 * (k // 2 + 1))
                act.activation(m_hi[:, k], m_raw[k % 2][:], ACT.Copy).then_inc(m_h, 1)
            for n in range(1, KD):
                weights(n)

        @block.gpsimd
        def _(pool):
            for n in range(KD):
                pool.wait_ge(hi_done, n + 1)
                pool.tensor_tensor(w_lo[n % 2][:], raw[n % 2][:], w_hi[n % 2][:], ALU.subtract).then_inc(lo_done, 1)

        @block.tensor
        def _(pe):
            for n in range(KD):
                s = n % 2
                pe.wait_ge(lo_done, n + 1)
                for c, (at, m) in enumerate(CHUNKS):
                    o = n * NC + c
                    if o >= BANKS:
                        pe.wait_ge(added, o - BANKS + 1)
                    for k in range(KD):
                        if n == 0 and c == 0:
                            pe.wait_ge(m_l, k + 1)
                        a = products(pe, bank[o % BANKS][:, 0:m], w_hi[s][:, k], w_lo[s][:, k], m_hi[:, k, at:at + m],
                                     m_lo[:, k, at:at + m], k == 0, k == KD - 1)
                    a.then_inc(mm, 1)

        @block.vector
        def _(dve):
            for k in range(KD):
                dve.wait_ge(m_h, k + 1)
                dve.tensor_tensor(m_lo[:, k], m_raw[k % 2][:], m_hi[:, k], ALU.subtract).then_inc(m_l, 1)
            dve.wait_ge(x_in, 16)
            for n in range(KD):
                for c, (at, m) in enumerate(CHUNKS):
                    o = n * NC + c
                    dve.wait_ge(mm, o + 1)
                    dve.scalar_tensor_tensor(out=x1[:, n, at:at + m], in0=bank[o % BANKS][:, 0:m],
                                             scalar=g.mod[:, GATE1 + n, SEG_OF[c]:SEG_OF[c] + 1],
                                             in1=x1[:, n, at:at + m], op0=ALU.mult, op1=ALU.add).then_inc(added, 1)
            dve.wait_ge(added, KD * NC)


def stage_norm2(nc, g, x1, h_hi, h_lo):
    with stage(nc, "n2") as st:
        a = st.sb("a", [P, KD, 2])
        a_done = st.sem("a_done")
        nrm = norm_buffers(st)
        block = st.block()

        @block.tensor
        def _(pe):
            norm_pe(pe, g, nrm)

        @block.vector
        def _(dve):
            for s in range(2):
                m = dve.scalar_tensor_tensor(out=a[:, :, s], in0=g.mod[:, SCALE2:SCALE2 + KD, s], scalar=1.0,
                                             in1=g.n2[:], op0=ALU.add, op1=ALU.mult)
            m.then_inc(a_done, 1)
            norm_sum_dve(dve, g, nrm)
            dve.wait_ge(a_done, 1)
            norm_apply_dve(dve, x1, nrm, lambda k, s: (a[:, k, s:s + 1], g.mod[:, SHIFT2 + k, s:s + 1]))

        @block.scalar
        def _(act):
            norm_act(act, x1, nrm)
            split_hi_act(act, nrm, h_hi)

        @block.gpsimd
        def _(pool):
            split_lo_pool(pool, nrm, h_hi, h_lo)


def stage_mlp(nc, g, x1, h_hi, h_lo):
    GT = 4
    GROUPS = FF // P // GT
    UP_U, DOWN_U = GT, KD * GT // KD
    U = UP_U + DOWN_U
    PER_DOWN = KD // DOWN_U
    UP_O, DOWN_O = UP_U * NC, KD * NC
    OUTS = UP_O + DOWN_O
    assert U % 2 == 0 and OUTS % BANKS == 0

    def outs_after(k):
        return NC * (k + 1) if k < UP_U else UP_O + NC * PER_DOWN * (k - UP_U + 1)

    with stage(nc, "ml") as st:
        raw = [st.sb(f"raw{s}", [P, KD, P]) for s in range(2)]
        w_hi = [st.sb(f"whi{s}", [P, KD, P], F32R) for s in range(2)]
        w_lo = [st.sb(f"wlo{s}", [P, KD, P], F32R) for s in range(2)]
        u_hi, u_lo = (st.sb(x, [P, GT, T], F32R) for x in ("uhi", "ulo"))
        r = [st.sb(f"r{s}", [P, 512]) for s in range(2)]
        sq = [st.sb(f"sq{s}", [P, 512]) for s in range(2)]
        bank = [st.bank(f"b{i}") for i in range(BANKS)]
        raw_in = [st.sem(f"raw_in{s}") for s in range(2)]
        hi_done, lo_done, mm, relu, squared, u_h, u_l, added = (
            st.sem(x) for x in ("hi_done", "lo_done", "mm", "relu", "squared", "u_h", "u_l", "added"))
        block = st.block()

        @block.sync
        def _(sp):
            def load(n, s):
                sp.dma_start(raw[s][:], g.d["w_mlp"][n]).then_inc(raw_in[s], 16)

            for s in range(2):
                load(s, s)
            with sp.Fori(1, GROUPS * U // 2) as i:
                for s in range(2):
                    sp.wait_ge(lo_done, 2 * i + s - 1)
                    load(2 * i + s, s)

        @block.scalar
        def _(act):
            def weights(i, k, first):
                j, kk = (i, k) if k < U else (i + 1, 0)
                act.wait_ge(raw_in[kk % 2], 16 * (j * (U // 2) + kk // 2 + 1))
                if k >= 2:
                    act.wait_ge(mm, i * OUTS + outs_after(k - 2))
                elif not first:
                    act.wait_ge(mm, (i - 1) * OUTS + outs_after(U + k - 2))
                act.activation(w_hi[kk % 2][:], raw[kk % 2][:], ACT.Copy).then_inc(hi_done, 1)

            def group(i, first, last):
                for k in range(U):
                    if not (last and k == U - 1):
                        weights(i, k + 1, first)
                    if k >= UP_U:
                        continue
                    for c, (at, m) in enumerate(CHUNKS):
                        o = k * NC + c
                        act.wait_ge(mm, i * OUTS + o + 1)
                        if o >= 2 or not first:
                            act.wait_ge(squared, i * UP_O + o - 1)
                        act.activation(r[o % 2][:, 0:m], bank[o % BANKS][:, 0:m], ACT.Relu).then_inc(relu, 1)
                        act.wait_ge(squared, i * UP_O + o + 1)
                        act.activation(u_hi[:, k, at:at + m], sq[o % 2][:, 0:m], ACT.Copy).then_inc(u_h, 1)

            weights(0, 0, True)
            group(0, True, False)
            with act.Fori(1, GROUPS - 1) as i:
                group(i, False, False)
            group(GROUPS - 1, False, True)

        @block.gpsimd
        def _(pool):
            def weights(i, k):
                pool.wait_ge(hi_done, i * U + k + 1)
                pool.tensor_tensor(w_lo[k % 2][:], raw[k % 2][:], w_hi[k % 2][:], ALU.subtract).then_inc(lo_done, 1)

            def group(i, last):
                for k in range(U):
                    if not (last and k == U - 1):
                        weights(i, k + 1)
                    if k >= UP_U:
                        continue
                    for c, (at, m) in enumerate(CHUNKS):
                        o = k * NC + c
                        pool.wait_ge(u_h, i * UP_O + o + 1)
                        pool.tensor_tensor(u_lo[:, k, at:at + m], sq[o % 2][:, 0:m], u_hi[:, k, at:at + m],
                                           ALU.subtract).then_inc(u_l, 1)

            weights(0, 0)
            with pool.Fori(0, GROUPS - 1) as i:
                group(i, False)
            group(GROUPS - 1, True)

        @block.tensor
        def _(pe):
            def free(i, o):
                q = o - BANKS
                if 0 <= q < UP_O:
                    pe.wait_ge(relu, i * UP_O + q + 1)
                else:
                    done = q - UP_O + 1 if q >= 0 else q + 1
                    pe.wait_ge(added, i * DOWN_O + done + BANKS)

            with pe.Fori(0, GROUPS) as i:
                for k in range(U):
                    s = k % 2
                    pe.wait_ge(lo_done, i * U + k + 1)
                    for n in range(1 if k < UP_U else PER_DOWN):
                        for c, (at, m) in enumerate(CHUNKS):
                            o = k * NC + c if k < UP_U else UP_O + ((k - UP_U) * PER_DOWN + n) * NC + c
                            free(i, o)
                            if k < UP_U:
                                ops = [(kk, h_hi[:, kk, at:at + m], h_lo[:, kk, at:at + m]) for kk in range(KD)]
                            else:
                                if k == UP_U and n == 0:
                                    pe.wait_ge(u_l, i * UP_O + (UP_U - 1) * NC + c + 1)
                                ops = [(n * GT + kk, u_hi[:, kk, at:at + m], u_lo[:, kk, at:at + m])
                                       for kk in range(GT)]
                            for kk, (row, hi, lo) in enumerate(ops):
                                a = products(pe, bank[o % BANKS][:, 0:m], w_hi[s][:, row], w_lo[s][:, row], hi, lo,
                                             kk == 0, kk == len(ops) - 1)
                            a.then_inc(mm, 1)

        @block.vector
        def _(dve):
            dve.sem_inc(added, BANKS)
            def group(i, first):
                for o in range(UP_O):
                    k, c = divmod(o, NC)
                    m = CHUNKS[c][1]
                    dve.wait_ge(relu, i * UP_O + o + 1)
                    if not first or o >= 2:
                        dve.wait_ge(u_l, i * UP_O + o - 1)
                    dve.tensor_tensor(sq[o % 2][:, 0:m], r[o % 2][:, 0:m], r[o % 2][:, 0:m], ALU.mult
                                      ).then_inc(squared, 1)
                for n in range(KD):
                    for c, (at, m) in enumerate(CHUNKS):
                        j = n * NC + c
                        o = UP_O + j
                        dve.wait_ge(mm, i * OUTS + o + 1)
                        if not first:
                            dve.wait_ge(added, (i - 1) * DOWN_O + j + 1 + BANKS)
                        dve.scalar_tensor_tensor(out=x1[:, n, at:at + m], in0=bank[o % BANKS][:, 0:m],
                                                 scalar=g.mod[:, GATE2 + n, SEG_OF[c]:SEG_OF[c] + 1],
                                                 in1=x1[:, n, at:at + m], op0=ALU.mult, op1=ALU.add
                                                 ).then_inc(added, 1)

            group(0, True)
            with dve.Fori(1, GROUPS) as i:
                group(i, False)
            dve.wait_ge(added, GROUPS * DOWN_O + BANKS)


def stage_final(nc, g, x1):
    with stage(nc, "fi") as st:
        nrm = norm_buffers(st)
        scaled, stored = st.sem("scaled"), st.sem("stored")
        block = st.block()

        @block.sync
        def _(sp):
            for k in range(KD):
                sp.wait_ge(scaled, k + 1)
                sp.dma_start(g.y[k], x1[:, k]).then_inc(stored, 16)
            sp.wait_ge(stored, 16 * KD)

        @block.tensor
        def _(pe):
            norm_pe(pe, g, nrm)

        @block.scalar
        def _(act):
            norm_act(act, x1, nrm)

        @block.vector
        def _(dve):
            norm_sum_dve(dve, g, nrm)
            dve.wait_ge(nrm.spread, 1)
            for k in range(KD):
                for c, (at, n) in enumerate(CHUNKS):
                    m = dve.scalar_tensor_tensor(out=x1[:, k, at:at + n], in0=x1[:, k, at:at + n],
                                                 scalar=g.fg[:, k:k + 1], in1=nrm.p_r[c][:, 0:n], op0=ALU.mult,
                                                 op1=ALU.mult)
                m.then_inc(scaled, 1)


def build(nc, d, upto=99):
    g = Shared()
    g.d = d
    kind = "ExternalOutput" if upto < 99 else "Internal"

    def dram(name, shape):
        return nc.dram_tensor(name, shape, F32, kind=kind).ap()

    g.projT = dram("s_projT", (PROJ_U, P, T))
    g.v = dram("s_v", (TT, P, D))
    g.v_heads = g.v.rearrange("t p (h e) -> h p t e", h=HEADS)
    g.oT = dram("s_oT", (HEADS, P, T))
    g.spec = dram("s_spec", (2, FTILES, P, SPEC, CH))
    g.x2T = dram("s_x2T", (CHT, P, T))
    g.x1t = dram("s_x1t", (HT, P, 2, CH))
    g.ohT = dram("s_ohT", (CHT, P, T))
    g.mT = dram("s_mT", (KD, P, T))
    g.y, g.new_k, g.new_v = d["y"], d["new_k"], d["new_v"]
    with stage(nc, "all") as st:
        g.ident = st.sb("ident", [P, P])
        g.ones = st.sb("ones", [P, P])
        g.silu = st.sb("silu", [P, KD, 2])
        g.bada = st.sb("bada", [P, ADA_U])
        g.n1, g.n2, g.fg = (st.sb(n, [P, KD]) for n in ("n1", "n2", "fg"))
        g.mod = st.sb("mod", [P, ADA_U, 2])
        g.subln, g.neg_lam = st.sb("subln", [P, 1]), st.sb("neglam", [P, 1])
        stage_consts(nc, g)
        if upto >= 3:
            stage_filters(nc, g)
        with stage(nc, "h") as hs:
            h_hi = hs.sb("hi", [P, KD, T], F32R)
            h_lo = hs.sb("lo", [P, KD, T], F32R)
            stage_norm1(nc, g, h_hi, h_lo)
            stage_project(nc, g, h_hi, h_lo)
            stage_values(nc, g, h_hi, h_lo)
        if upto < 2:
            return
        if upto >= 3:
            with stage(nc, "z") as zs:
                z = [zs.sb(n, [P, HT, CH]) for n in ("F", "M")]
                stage_short_conv(nc, g, z)
                stage_hyena(nc, g, z)
                stage_hyena_out(nc, g, z)
        if upto == 3:
            return
        with stage(nc, "o") as os_:
            o_all = os_.sb("all", [P, HEADS * UNITS, VD])
            l0_all = os_.sb("l0", [P, HEADS * UNITS])
            stage_attention(nc, g, o_all, l0_all)
            stage_attn_norm(nc, g, o_all, l0_all)
        if upto == 2:
            return
        stage_merge(nc, g)
        with stage(nc, "x") as xs:
            x1 = xs.sb("x1", [P, KD, T])
            stage_out(nc, g, x1)
            with stage(nc, "h2") as hs:
                h_hi = hs.sb("hi", [P, KD, T], F32R)
                h_lo = hs.sb("lo", [P, KD, T], F32R)
                stage_norm2(nc, g, x1, h_hi, h_lo)
                stage_mlp(nc, g, x1, h_hi, h_lo)
            stage_final(nc, g, x1)


def tiles_T(a):
    return np.ascontiguousarray(a.reshape(-1, P).T)


def units(w):
    k, m = w.shape[0] // P, w.shape[1] // P
    return np.ascontiguousarray(w.reshape(k, P, m, P).transpose(2, 1, 0, 3))


def mlp_units(up, down):
    u = units(up).reshape(-1, 4, P, KD, P)
    d = down.reshape(-1, 4, P, KD // 2, 2, P).transpose(0, 3, 2, 4, 1, 5).reshape(-1, 4, P, KD, P)
    return np.ascontiguousarray(np.stack([u, d], axis=1)).reshape(-1, P, KD, P)


def head_order(w):
    return w.reshape(w.shape[:-1] + (-1, 2, 2, 16)).swapaxes(-3, -2).reshape(w.shape)


def rope_tables():
    n = HD // 4
    inv = np.float32(10000.0) ** (-np.arange(n, dtype=np.float32) / np.float32(n))
    pos = np.arange(LAT)
    ang = [(p.astype(np.float32)[None, :] * inv[:, None]).astype(np.float64) for p in (pos // GRID_W, pos % GRID_W)]
    both = np.concatenate(ang, axis=0)
    cos, sin = np.cos(both), np.sin(both)
    cos, sin = np.concatenate([cos] * 4), np.concatenate([-sin, sin, -sin, sin])
    q_cos = np.concatenate([np.ones((P, CTX)), cos], axis=1) * HD ** -0.5
    t = {"q_cos": q_cos, "q_sin": sin * HD ** -0.5, "k_cos": cos, "k_sin": sin}
    return {n: a.astype(np.float32) for n, a in t.items()}


def frequencies(L):
    even = np.arange(0, L, 2)
    if L // 4 >= P:
        even = np.concatenate([even[::2], even[1::2]])
    return np.concatenate([even, np.arange(1, L, 2)])


def filter_times(L):
    if L == CTX:
        return np.arange(L)
    F, M = np.arange(L // 2), L - np.arange(L // 2)
    M[0] = L // 2
    return np.stack([F.reshape(-1, P), M.reshape(-1, P)], axis=1).reshape(-1)


def table_tiles(a):
    t = a.reshape(-1, P, P).transpose(1, 0, 2)
    return np.concatenate([t, np.zeros((P, KU - t.shape[1], P))], axis=1)


def filter_tables():
    out = []
    for j, c in filter_units():
        L, jj = (LAT, j) if j < LAT_FT else (CTX, j - LAT_FT)
        f = frequencies(L)[jj * P:(jj + 1) * P].astype(np.float64)
        t = np.arange(L // 2 if L == LAT else L, dtype=np.float64)
        ang = math.pi * t[:, None] * f[None, :] / L
        a = np.sin(ang) if c == 1 else np.cos(ang)
        if L == LAT and even_tile(j) and c != 1:
            a[0] = 1.0
        if L == LAT and not even_tile(j) and c == 1:
            a[0] = np.sin(math.pi * f / 2)
        if c == 2:
            a[:, 0] = np.where(t % 2 == 0, 1.0, -1.0)
        out.append(table_tiles(a))
    return np.stack(out).astype(np.float32)


def hyena_tables():
    def cs(L, times, freqs, sine):
        ang = math.pi * (times[:, None] + 0.5) * freqs[None, :] / L
        a = np.sin(ang) if sine else np.cos(ang)
        if sine and freqs[0] == 0:
            a[:, 0] = np.sin(math.pi * (times + 0.5))
        return a

    fl, fc = frequencies(LAT).astype(np.float64), frequencies(CTX).astype(np.float64)
    tl, tc = np.arange(LAT // 2, dtype=np.float64), np.arange(CTX // 2, dtype=np.float64)
    out = [table_tiles(cs(LAT, tl, fl[j * P:(j + 1) * P], c)) for j in range(LAT_FT) for c in range(2)]
    out.append(np.stack([cs(CTX, tc, fc[j * P:(j + 1) * P], c) for j in range(CTX_FT) for c in range(2)], axis=1))
    half = LAT // 2
    for i in range(HALF_T[0]):
        for q in range(2):
            for sine in range(2):
                odd = sine ^ q
                out.append(table_tiles(cs(LAT, tl[i * P:(i + 1) * P], fl[half * odd:half * (odd + 1)], sine).T))
    out.append(np.stack([cs(CTX, tc, fc[P * (s ^ q):P * (s ^ q) + P], s).T for q in range(2) for s in range(2)],
                        axis=1))
    return np.stack(out).astype(np.float32)


def filter_rows():
    embs, decays = [], []
    bands = (EMB - 1) // 2
    deltas = np.linspace(math.log(1e-2) / 0.3, math.log(1e-2) / 1.5, CH, dtype=np.float32).astype(np.float64)
    for L in (LAT, CTX):
        k = filter_times(L)
        t = np.linspace(0.0, 1.0, L, dtype=np.float32).astype(np.float64)[k]
        w = (np.float32(2.0 * math.pi) * np.arange(L, dtype=np.float32) / np.float32(L)).astype(np.float64)[k]
        f = np.linspace(1e-4, bands - 1, bands, dtype=np.float32).astype(np.float64)
        embs.append(np.concatenate([t[None], np.cos(f[:, None] * w), -np.sin(f[:, None] * w)]))
        decays.append(np.exp(-t[:, None] * np.abs(deltas)))
    wf = np.concatenate([np.full((P, LAT_FT), 1.0 / LAT), np.full((P, CTX_FT), 1.0 / CTX)], axis=1)
    wf[0, 0] *= 0.5
    wf[0, LAT_FT] *= 0.5
    decay = np.concatenate(decays).reshape(-1, P, CH).transpose(1, 0, 2)
    return {n: np.ascontiguousarray(a, dtype=np.float32)
            for n, a in (("emb", np.concatenate(embs, axis=1)), ("decay", decay), ("wf", wf))}


def lay_out(i):
    x = np.concatenate([i["x_prompt"][0], i["x_sample"][0]], axis=0)
    w_in = i["w_in"][0]
    q_end, k_end, v_end = D, 2 * D, 3 * D
    a = {
        "xT": np.ascontiguousarray(x.T).reshape(KD, P, T),
        "cond": np.ascontiguousarray(np.stack([i["c_ctx"], i["c"][0]]).reshape(2, KD, P).transpose(2, 1, 0)),
        "b_ada": tiles_T(i["b_ada"][0]), "n1": tiles_T(i["norm1_g"][0]), "n2": tiles_T(i["norm2_g"][0]),
        "fg": tiles_T(i["final_g"]),
        "w_ada": units(i["w_ada"][0]),
        "w_proj": units(np.concatenate([head_order(w_in[:, :k_end]), w_in[:, v_end:]], axis=1)),
        **rope_tables(),
        "cache_kT": np.ascontiguousarray(head_order(i["cache_k"][0, 0]).reshape(PAST, HEADS, P).transpose(1, 2, 0)),
        "cache_v": np.ascontiguousarray(i["cache_v"][0, 0].reshape(PAST // P, P, HEADS, VD).transpose(2, 1, 0, 3)),
        "lam": np.concatenate([i["lam_q1"], i["lam_q2"], i["lam_k1"], i["lam_k2"]], axis=1),
        "w_br": units(np.concatenate([i["w_br_hy"][0], i["w_br_attn"][0]], axis=0)),
        "w_out": units(i["w_out"][0]),
        "w_mlp": mlp_units(i["w_up"][0], i["w_down"][0]),
        **filter_rows(), "filt_tab": filter_tables(), "hy_tab": hyena_tables(),
        "filt_w1": i["filt_w1"][0], "filt_w2": i["filt_w2"][0],
        "filt_vec": np.ascontiguousarray(np.stack([i["filt_b1"][0], i["filt_b2"][0], i["filt_freq"][0]], axis=1)),
        "filt_w3": i["filt_w3"][0].reshape(HID, 2, 2, CH),
        "hy_bias": np.ascontiguousarray(np.broadcast_to(i["hy_bias"][0], (P, 2, CH))),
        "conv": np.ascontiguousarray(np.stack([*i["conv_w"][0], i["conv_b"][0]]).reshape(4, 3 * CHT, P)
                                     .transpose(2, 1, 0)),
        "subln": np.ascontiguousarray(i["attn_subln_g"].reshape(P, 1)),
        "w_v": np.ascontiguousarray(w_in[:, k_end:v_end].reshape(KD, P, D // 512, 512).transpose(2, 1, 0, 3)),
    }
    return a


_OUTS = {"y": (KD, P, T), "new_k": (HEADS, P, CTX), "new_v": (CTX // P, P, D)}


def kernel(**inputs):
    import concourse.bacc as bacc
    from concourse.bass_utils import run_bass_kernel_spmd

    nc = bacc.Bacc("TRN2", target_bir_lowering=False, num_devices=1)
    arrays = lay_out({n: np.asarray(a) for n, a in inputs.items()})
    d = {}
    for n, a in arrays.items():
        d[n] = nc.dram_tensor(f"in_{n}", a.shape, F32, kind="ExternalInput").ap()
    for n, shape in _OUTS.items():
        d[n] = nc.dram_tensor(f"out_{n}", shape, F32, kind="ExternalOutput").ap()
    build(nc, d)
    r = run_bass_kernel_spmd(nc, [{f"in_{n}": a for n, a in arrays.items()}], core_ids=[0]).results[0]
    y = r["out_y"].reshape(D, T).T
    new_k = head_order(r["out_new_k"].transpose(2, 0, 1).reshape(CTX, D)).reshape(1, 1, CTX, HEADS, 2, HD)
    new_v = r["out_new_v"].reshape(1, 1, CTX, HEADS, VD)
    return (np.ascontiguousarray(y[None, :CTX]), np.ascontiguousarray(y[None, CTX:]), np.ascontiguousarray(new_k),
            np.ascontiguousarray(new_v))
```

```python
from contextlib import ExitStack, contextmanager
import math

import numpy as np
import concourse.bass as bass
from concourse import mybir

F32 = mybir.dt.float32
F32R = mybir.dt.float32r
ALU = mybir.AluOpType
ACT = mybir.ActivationFunctionType
AX = mybir.AxisListType

P = 128
D = 1024
KD = D // P
CTX, LAT, PAST = 256, 1024, 256
T = CTX + LAT
TT = T // P
SEGS = [(0, CTX), (CTX, LAT)]
CHUNKS = [(0, 256), (256, 512), (768, 512)]
NC = len(CHUNKS)
BANKS = 2 * NC
HEADS, HD, VD = 8, 64, 128
CH = 512
CHT = CH // P
FF = 4 * D
EMB, HID = 33, 64
EPS = 1e-6
GRID_W = 64
Q_U, K_U, U_U, G_U = 8, 8, 12, 16
PROJ_U = Q_U + K_U + U_U + G_U
ADA_U = 6 * KD
FIRST_ADA = 2 * KD


class Shared:
    pass


class Room:

    def __init__(self, nc, name, ctx):
        self.nc, self.name, self.ctx, self.sems = nc, name, ctx, []

    def sb(self, name, shape, dt=F32):
        return self.ctx.enter_context(self.nc.sbuf_tensor(f"{self.name}_{name}", shape, dt))

    def bank(self, name):
        return self.ctx.enter_context(self.nc.psum_tensor(f"{self.name}_{name}", [P, 512], F32))

    def sem(self, name):
        self.sems.append(self.nc.alloc_semaphore(name=f"{self.name}_{name}"))
        return self.sems[-1]

    def block(self):
        return self.ctx.enter_context(self.nc.Block())


SEMS_KEPT = 100
USED = []


@contextmanager
def stage(nc, name):
    with ExitStack() as ctx:
        room = Room(nc, name, ctx)
        yield room
    USED.extend(room.sems)
    if len(USED) > SEMS_KEPT:
        nc.clear_and_free_semaphores(USED)
        nc.all_engine_barrier()
        USED.clear()


def stage_consts(nc, g):
    LAM_INIT = 0.8 - 0.6 * math.exp(0.0)
    with stage(nc, "cst") as st:
        loaded, cleared, made, sig, done, lam_mm, lam_e = (
            st.sem(n) for n in ("loaded", "cleared", "made", "sig", "done", "lam_mm", "lam_e"))
        raw = st.sb("cond", [P, KD, 2])
        sg = st.sb("sg", [P, KD, 2])
        lam = st.sb("lam", [1, 4 * HD])
        lam_b, lam_p = st.sb("lamb", [P, 2 * HD]), st.sb("lamp", [P, 2, HD])
        lam_s, lam_x = st.sb("lams", [P, 2]), st.sb("lamx", [P, 2])
        bank = st.bank("b")
        block = st.block()
        LOADS = 7

        @block.sync
        def _(sp):
            for dst, src in ((raw[:], g.d["cond"]), (g.bada[:], g.d["b_ada"]), (g.n1[:], g.d["n1"]),
                             (g.n2[:], g.d["n2"]), (g.fg[:], g.d["fg"]), (lam[:], g.d["lam"]), (g.subln[:], g.d["subln"])):
                sp.dma_start(dst, src).then_inc(loaded, 16)
            sp.wait_ge(loaded, 16 * LOADS)

        @block.gpsimd
        def _(pool):
            pool.memset(g.ident[:], 0.0).then_inc(cleared, 1)
            pool.memset(g.ones[:], 1.0).then_inc(made, 1)
            pool.wait_ge(cleared, 1)
            pool.affine_select(out=g.ident[:], in_=g.ident[:], compare_op=ALU.not_equal, fill=1.0, base=0,
                               pattern=[[-1, P]], channel_multiplier=1).then_inc(made, 1)

        @block.tensor
        def _(pe):
            pe.wait_ge(loaded, 16 * LOADS)
            pe.wait_ge(made, 2)
            pe.matmul(bank[:, 0:4 * HD], g.ones[0:1, :], lam[:], start=True, stop=True).then_inc(lam_mm, 1)

        @block.scalar
        def _(act):
            act.wait_ge(loaded, 16 * LOADS)
            act.activation(sg[:], raw[:], ACT.Sigmoid).then_inc(sig, 1)
            act.wait_ge(done, 5)
            act.activation(lam_x[:], lam_s[:], ACT.Exp).then_inc(lam_e, 1)

        @block.vector
        def _(dve):
            n = [0]

            def step(ins):
                ins.then_inc(done, 1)
                n[0] += 1
                dve.wait_ge(done, n[0])

            dve.wait_ge(sig, 1)
            step(dve.tensor_tensor(g.silu[:], sg[:], raw[:], ALU.mult))
            step(dve.tensor_scalar(g.subln[:], g.subln[:], 1.0 - LAM_INIT, None, ALU.mult))
            dve.wait_ge(lam_mm, 1)
            step(dve.tensor_copy(lam_b[:], bank[:, 0:2 * HD]))
            step(dve.tensor_tensor(lam_p[:].rearrange("p a d -> p (a d)"), lam_b[:], bank[:, 2 * HD:4 * HD],
                                   ALU.mult))
            step(dve.tensor_reduce(lam_s[:], lam_p[:], AX.X, ALU.add))
            dve.wait_ge(lam_e, 1)
            step(dve.scalar_tensor_tensor(out=g.neg_lam[:], in0=lam_x[:, 1:2], scalar=-LAM_INIT, in1=lam_x[:, 0:1],
                                          op0=ALU.add, op1=ALU.subtract))


def stage_norm1(nc, g, h_hi, h_lo):
    with stage(nc, "n1") as st:
        x = st.sb("x", [P, KD, T])
        a = st.sb("a", [P, KD, 2])
        nrm = norm_buffers(st)
        a_done = st.sem("a_done")
        x_in = [st.sem(f"x_in{k}") for k in range(KD)]
        block = st.block()

        @block.sync
        def _(sp):
            for k in range(KD):
                sp.dma_start(x[:, k], g.d["xT"][k]).then_inc(x_in[k], 16)

        @block.tensor
        def _(pe):
            norm_pe(pe, g, nrm)

        @block.vector
        def _(dve):
            for s in range(2):
                m = dve.scalar_tensor_tensor(out=a[:, :, s], in0=g.mod[:, KD:2 * KD, s], scalar=1.0, in1=g.n1[:],
                                             op0=ALU.add, op1=ALU.mult)
            m.then_inc(a_done, 1)
            norm_sum_dve(dve, g, nrm)
            dve.wait_ge(a_done, 1)
            norm_apply_dve(dve, x, nrm, lambda k, s: (a[:, k, s:s + 1], g.mod[:, k, s:s + 1]))

        @block.scalar
        def _(act):
            norm_act(act, x, nrm, x_in)
            split_hi_act(act, nrm, h_hi)

        @block.gpsimd
        def _(pool):
            split_lo_pool(pool, nrm, h_hi, h_lo)


NORM_BUFS = 3


def norm_buffers(st):
    b = Shared()
    b.sq = st.sb("sq", [P, 2, T])
    b.acc = st.sb("acc", [P, T])
    b.var = st.sb("var", [P, TT])
    b.std = st.sb("std", [P, TT])
    b.rstd = st.sb("rstd", [P, TT])
    b.diag = st.sb("diag", [P, TT, P])
    b.xn = st.sb("xn", [P, NORM_BUFS, T])
    b.hf = st.sb("hf", [P, NORM_BUFS, T])
    b.p_sum = st.bank("psum")[:, 0:TT]
    b.p_r = [st.bank(f"pr{c}") for c in range(NC)]
    (b.squared, b.summed, b.token_sums, b.var_done, b.std_done, b.rstd_done, b.diag_done, b.spread, b.xn_done,
     b.hf_done, b.hi_done, b.lo_done) = (
        st.sem(n) for n in ("squared", "summed", "token_sums", "var_done", "std_done", "rstd_done", "diag_done",
                            "spread", "xn_done", "hf_done", "hi_done", "lo_done"))
    return b


def norm_act(act, x, b, x_in=None):
    for k in range(KD):
        if x_in:
            act.wait_ge(x_in[k], 16)
        if k >= 2:
            act.wait_ge(b.summed, k - 1)
        act.activation(b.sq[:, k % 2], x[:, k, :], ACT.Square).then_inc(b.squared, 1)
    act.wait_ge(b.var_done, 1)
    act.activation(b.std[:], b.var[:], ACT.Sqrt).then_inc(b.std_done, 1)


def norm_sum_dve(dve, g, b):
    for k in range(KD):
        dve.wait_ge(b.squared, k + 1)
        if k == 0:
            dve.tensor_copy(b.acc[:], b.sq[:, 0]).then_inc(b.summed, 1)
        else:
            dve.wait_ge(b.summed, k)
            dve.tensor_tensor(b.acc[:], b.acc[:], b.sq[:, k % 2], ALU.add).then_inc(b.summed, 1)
    dve.wait_ge(b.token_sums, 1)
    dve.tensor_scalar(b.var[:], b.p_sum[:], 1.0 / D, EPS, ALU.mult, ALU.add).then_inc(b.var_done, 1)
    dve.wait_ge(b.std_done, 1)
    dve.reciprocal(b.rstd[:], b.std[:]).then_inc(b.rstd_done, 1)
    dve.wait_ge(b.rstd_done, 1)
    for t in range(TT):
        m = dve.tensor_scalar(b.diag[:, t], g.ident[:], b.rstd[:, t:t + 1], None, ALU.mult)
    m.then_inc(b.diag_done, 1)


def norm_pe(pe, g, b):
    pe.wait_ge(b.summed, KD)
    for t in range(TT):
        mm = pe.matmul(b.p_sum[:, t:t + 1], b.acc[:, t * P:(t + 1) * P], g.ones[:, 0:1], start=True, stop=True)
    mm.then_inc(b.token_sums, 1)
    pe.wait_ge(b.diag_done, 1)
    for c, (at, n) in enumerate(CHUNKS):
        for t in range(n // P):
            mm = pe.matmul(b.p_r[c][:, t * P:(t + 1) * P], g.ones[:], b.diag[:, at // P + t],
                           start=True, stop=True)
    mm.then_inc(b.spread, 1)


def norm_apply_dve(dve, x, b, affine):
    dve.wait_ge(b.spread, 1)
    for k in range(KD):
        if k >= NORM_BUFS:
            dve.wait_ge(b.lo_done, k - NORM_BUFS + 1)
        for c, (at, n) in enumerate(CHUNKS):
            m = dve.tensor_tensor(b.xn[:, k % NORM_BUFS, at:at + n], x[:, k, at:at + n], b.p_r[c][:, 0:n], ALU.mult)
        m.then_inc(b.xn_done, 1)
        dve.wait_ge(b.xn_done, k + 1)
        for s, (at, n) in enumerate(SEGS):
            a, sh = affine(k, s)
            cols = slice(at, at + n)
            m = dve.tensor_scalar(b.hf[:, k % NORM_BUFS, cols], b.xn[:, k % NORM_BUFS, cols], a, sh, ALU.mult,
                                  ALU.add)
        m.then_inc(b.hf_done, 1)


def split_hi_act(act, b, hi):
    for k in range(KD):
        act.wait_ge(b.hf_done, k + 1)
        act.activation(hi[:, k, :], b.hf[:, k % NORM_BUFS], ACT.Copy).then_inc(b.hi_done, 1)


def split_lo_pool(pool, b, hi, lo):
    for k in range(KD):
        pool.wait_ge(b.hi_done, k + 1)
        pool.tensor_tensor(lo[:, k, :], b.hf[:, k % NORM_BUFS], hi[:, k, :], ALU.subtract).then_inc(b.lo_done, 1)
    pool.wait_ge(b.lo_done, KD)


def products(pe, out, w_hi, w_lo, x_hi, x_lo, first, last):
    pe.matmul(out, w_hi, x_hi, start=first, stop=False)
    pe.matmul(out, w_hi, x_lo, start=False, stop=False)
    return pe.matmul(out, w_lo, x_hi, start=False, stop=last)


def stage_project(nc, g, h_hi, h_lo):
    N = PROJ_U
    WITH_ADA = ADA_U - FIRST_ADA
    assert WITH_ADA % 2 == 0 and N % 2 == 0 and WITH_ADA < N
    with stage(nc, "prj") as st:
        raw = [st.sb(f"raw{s}", [P, KD, P]) for s in range(2)]
        w_hi = [st.sb(f"whi{s}", [P, KD, P], F32R) for s in range(2)]
        w_lo = [st.sb(f"wlo{s}", [P, KD, P], F32R) for s in range(2)]
        wa = [st.sb(f"wa{s}", [P, D]) for s in range(2)]
        ob = [st.sb(f"ob{s}", [P, T]) for s in range(2)]
        mod2 = st.sb("mod2", [P, WITH_ADA, 2])
        bank = [st.bank(f"b{i}") for i in range(BANKS)]
        cond = st.sb("cond", [P, 2, D])
        sig = st.sb("sig", [P, 2, D])
        prod = st.sb("prod", [P, 2, D])
        dot = st.sb("dot", [P, 2])
        raw_in = [st.sem(f"raw_in{s}") for s in range(2)]
        wa_in = [st.sem(f"wa_in{s}") for s in range(2)]
        stored = [st.sem(f"stored{s}") for s in range(2)]
        hi_done, lo_done, chunk_mm, evac, cond_in, sigm, silu, ada_dot, ada_out, fin = (
            st.sem(n) for n in ("hi_done", "lo_done", "chunk_mm", "evac", "cond_in", "sigm", "silu", "ada_dot",
                                "ada_out", "fin"))
        block = st.block()

        @block.sync
        def _(sp):
            def load(n, s):
                sp.dma_start(raw[s][:], g.d["w_proj"][n]).then_inc(raw_in[s], 16)

            def load_ada(n, s):
                sp.dma_start(wa[s][:], g.d["w_adaT"][n]).then_inc(wa_in[s], 16)

            def store(n, s):
                sp.wait_ge(evac, n * NC + NC + BANKS)
                sp.dma_start(g.projT[n], ob[s][:]).then_inc(stored[s], 16)

            for s in range(2):
                sp.sem_inc(stored[s], 16)
                load(s, s)
                load_ada(s, s)
            sp.dma_start(cond[:], g.d["cond_rows"]).then_inc(cond_in, 16)
            with sp.Fori(0, WITH_ADA // 2 - 1) as i:
                for s in range(2):
                    sp.wait_ge(lo_done, 2 * i + s + 1)
                    load(2 * i + s + 2, s)
                    sp.wait_ge(ada_dot, 2 * (2 * i + s) + 2)
                    load_ada(2 * i + s + 2, s)
                    store(2 * i + s, s)
            with sp.Fori(WITH_ADA // 2 - 1, N // 2 - 1) as i:
                for s in range(2):
                    sp.wait_ge(lo_done, 2 * i + s + 1)
                    load(2 * i + s + 2, s)
                    store(2 * i + s, s)
            for s in range(2):
                store(N - 2 + s, s)
            for s in range(2):
                sp.wait_ge(stored[s], 16 * (N // 2 + 1))

        @block.scalar
        def _(act):
            def split(i, s):
                act.wait_ge(raw_in[s], 16 * i + 16)
                act.activation(w_hi[s][:], raw[s][:], ACT.Copy).then_inc(hi_done, 1)

            for s in range(2):
                split(0, s)
            act.wait_ge(cond_in, 16)
            act.activation(sig[:], cond[:], ACT.Sigmoid).then_inc(sigm, 1)
            with act.Fori(1, N // 2) as i:
                for s in range(2):
                    act.wait_ge(chunk_mm, (2 * i + s - 1) * NC)
                    split(i, s)

        @block.gpsimd
        def _(pool):
            with pool.Fori(0, N // 2) as i:
                for s in range(2):
                    pool.wait_ge(hi_done, 2 * i + s + 1)
                    pool.tensor_tensor(w_lo[s][:], raw[s][:], w_hi[s][:], ALU.subtract).then_inc(lo_done, 1)

        @block.tensor
        def _(pe):
            def unit(i, s):
                pe.wait_ge(lo_done, 2 * i + s + 1)
                for c, (at, n) in enumerate(CHUNKS):
                    pe.wait_ge(evac, (2 * i + s) * NC + c + 1)
                    out = bank[s * NC + c][:, 0:n]
                    for k in range(KD):
                        mm = products(pe, out, w_hi[s][:, k], w_lo[s][:, k], h_hi[:, k, at:at + n],
                                      h_lo[:, k, at:at + n], k == 0, k == KD - 1)
                    mm.then_inc(chunk_mm, 1)

            with pe.Fori(0, N // 2) as i:
                for s in range(2):
                    unit(i, s)

        @block.vector
        def _(dve):
            def unit(i, s):
                dve.wait_ge(stored[s], 16 * i + 16)
                for c, (at, n) in enumerate(CHUNKS):
                    dve.wait_ge(chunk_mm, (2 * i + s) * NC + c + 1)
                    dve.tensor_copy(ob[s][:, at:at + n], bank[s * NC + c][:, 0:n]).then_inc(evac, 1)

            dve.sem_inc(evac, BANKS)
            dve.wait_ge(sigm, 1)
            dve.tensor_tensor(cond[:], cond[:], sig[:], ALU.mult).then_inc(silu, 1)
            dve.wait_ge(silu, 1)
            with dve.Fori(0, WITH_ADA // 2) as i:
                for s in range(2):
                    unit(i, s)
                    dve.wait_ge(wa_in[s], 16 * i + 16)
                    for seg in range(2):
                        if s or seg:
                            dve.wait_ge(ada_dot, 2 * (2 * i + s) + seg)
                        dve.scalar_tensor_tensor(out=prod[:, seg], in0=wa[s][:], scalar=1.0, in1=cond[:, seg],
                                                 op0=ALU.mult, op1=ALU.mult, accum_out=dot[:, seg:seg + 1]
                                                 ).then_inc(ada_dot, 1)
                    dve.wait_ge(ada_dot, 2 * (2 * i + s) + 2)
                    dve.tensor_copy(mod2[:, bass.ds(2 * i + s, 1), :].rearrange("p u s -> p (u s)"), dot[:]
                                    ).then_inc(ada_out, 1)
                    dve.wait_ge(ada_out, 2 * i + s + 1)
            with dve.Fori(WITH_ADA // 2, N // 2) as i:
                for s in range(2):
                    unit(i, s)
            for s in range(2):
                m = dve.tensor_tensor(g.mod[:, FIRST_ADA:ADA_U, s], mod2[:, :, s], g.bada[:, FIRST_ADA:ADA_U],
                                      ALU.add)
            m.then_inc(fin, 1)
            dve.wait_ge(fin, 1)


def stage_values(nc, g, h_hi, h_lo):
    NB = D // 512
    NT = 3 * CHT
    PAD = T + 3
    AT = [(1, 0, CTX), (CTX + 2, CTX, LAT)]
    with stage(nc, "val") as st:
        raw = [st.sb(f"raw{j}", [P, KD // 2, 512]) for j in range(2)]
        w_hi = st.sb("whi", [P, KD, 512], F32R)
        w_lo = st.sb("wlo", [P, KD, 512], F32R)
        ob = [st.sb(f"ob{s}", [P, 512]) for s in range(4)]
        bank = [st.bank(f"b{i}") for i in range(4)]
        raw_in = [st.sem(f"raw_in{j}") for j in range(2)]
        stored = [st.sem(f"stored{s}") for s in range(4)]
        hi_done, lo_done, mm_done, evac = (st.sem(n) for n in ("hi_done", "lo_done", "mm_done", "evac"))
        u, acc = ([st.sb(f"{x}{s}", [P, PAD if x == "u" else T]) for s in range(2)] for x in ("u", "acc"))
        out = [st.sb(f"out{s}", [P, T]) for s in range(2)]
        cw = st.sb("cw", [P, NT, 4])
        cleared, w_in, mid, conv, cached = (st.sem(x) for x in ("cleared", "w_in", "mid", "conv", "cached"))
        u_in, out_stored = ([st.sem(f"{n}{s}") for s in range(2)] for n in ("u_in", "out_stored"))
        block = st.block()

        @block.sync
        def _(sp):
            def load(n, j):
                rows = slice(j * (KD // 2), (j + 1) * (KD // 2))
                sp.dma_start(raw[j][:], g.d["w_v"][n, :, rows, :]).then_inc(raw_in[j], 16)

            for j in range(2):
                load(0, j)
            sp.dma_start(cw[:], g.d["conv"]).then_inc(w_in, 16)
            sp.dma_start(g.new_k, g.projT[Q_U:Q_U + K_U, :, 0:CTX]).then_inc(cached, 16)
            for n in range(NB):
                if n + 1 < NB:
                    for j in range(2):
                        sp.wait_ge(lo_done, 2 * n + j + 1)
                        load(n + 1, j)
                for t in range(TT):
                    o = n * TT + t
                    sp.wait_ge(evac, o + 1)
                    sp.dma_start(g.v[t, :, n * 512:(n + 1) * 512], ob[o % 4][:]).then_inc(stored[o % 4], 16)
            for s in range(4):
                sp.wait_ge(stored[s], 16 * (NB * TT // 4))
            sp.wait_ge(cached, 16)

        @block.scalar
        def _(act):
            for n in range(NB):
                if n:
                    act.wait_ge(mm_done, n * TT)
                for j in range(2):
                    act.wait_ge(raw_in[j], 16 * (n + 1))
                    act.activation(w_hi[:, j * 4:j * 4 + 4, :], raw[j][:], ACT.Copy).then_inc(hi_done, 1)

        @block.gpsimd
        def _(pool):
            for n in range(NB):
                for j in range(2):
                    pool.wait_ge(hi_done, 2 * n + j + 1)
                    pool.tensor_tensor(w_lo[:, j * 4:j * 4 + 4, :], raw[j][:], w_hi[:, j * 4:j * 4 + 4, :],
                                       ALU.subtract).then_inc(lo_done, 1)
                if n == 0:
                    pool.wait_ge(cleared, 1)
                for x in range(NT // 2 + 1) if n == 0 else range(NT // 2 + 1, NT + 1):
                    if x < NT:
                        if x >= 2:
                            pool.wait_ge(conv, x - 1)
                        for col, tok, m in AT:
                            pool.dma_start(u[x % 2][:, col:col + m], g.projT[Q_U + K_U + x, :, tok:tok + m]
                                           ).then_inc(u_in[x % 2], 16)
                    if x:
                        pool.wait_ge(conv, x)
                        pool.dma_start(g.convT[x - 1], out[(x - 1) % 2][:]).then_inc(out_stored[(x - 1) % 2], 16)
            for s in range(2):
                pool.wait_ge(out_stored[s], 16 * (NT // 2))

        @block.tensor
        def _(pe):
            for n in range(NB):
                for t in range(TT):
                    o = n * TT + t
                    if o >= 4:
                        pe.wait_ge(evac, o - 3)
                    for k in range(KD):
                        if t == 0 and k % 4 == 0:
                            pe.wait_ge(lo_done, 2 * n + k // 4 + 1)
                        tok = slice(t * P, (t + 1) * P)
                        mm = products(pe, bank[o % 4][:], h_hi[:, k, tok], h_lo[:, k, tok], w_hi[:, k], w_lo[:, k],
                                      k == 0, k == KD - 1)
                    mm.then_inc(mm_done, 1)

        @block.vector
        def _(dve):
            def convolve(n):
                s = n % 2
                dve.wait_ge(u_in[s], 32 * (n // 2 + 1))
                for col, tok, m in AT:
                    a = dve.tensor_scalar(acc[s][:, tok:tok + m], u[s][:, col:col + m], cw[:, n, 1:2], cw[:, n, 3:4],
                                          ALU.mult, ALU.add)
                a.then_inc(mid, 1)
                dve.wait_ge(mid, 2 * n + 1)
                for col, tok, m in AT:
                    a = dve.scalar_tensor_tensor(out=acc[s][:, tok:tok + m], in0=u[s][:, col - 1:col - 1 + m],
                                                 scalar=cw[:, n, 0:1], in1=acc[s][:, tok:tok + m], op0=ALU.mult,
                                                 op1=ALU.add)
                a.then_inc(mid, 1)
                dve.wait_ge(mid, 2 * n + 2)
                if n >= 2:
                    dve.wait_ge(out_stored[s], 16 * (n // 2))
                for col, tok, m in AT:
                    for at, to in ((0, slice(tok, tok + m // 2)),
                                   (m // 2, slice(tok + m - 1, tok + m // 2 - 1, -1))):
                        after = col + 1 + at
                        a = dve.scalar_tensor_tensor(out=out[s][:, to], in0=u[s][:, after:after + m // 2],
                                                     scalar=cw[:, n, 2:3],
                                                     in1=acc[s][:, tok + at:tok + at + m // 2], op0=ALU.mult,
                                                     op1=ALU.add)
                a.then_inc(conv, 1)
                dve.wait_ge(conv, n + 1)

            for s in range(2):
                m = dve.memset(u[s][:], 0.0)
            m.then_inc(cleared, 1)
            dve.wait_ge(w_in, 16)
            for o in range(NB * TT):
                if 3 <= o < NT + 3:
                    convolve(o - 3)
                dve.wait_ge(mm_done, o + 1)
                if o >= 4:
                    dve.wait_ge(stored[o % 4], 16 * (o // 4))
                dve.tensor_copy(ob[o % 4][:], bank[o % 4][:]).then_inc(evac, 1)


CTX_Q, LAT_Q = CTX // P, LAT // P
UNITS = CTX_Q + LAT_Q
KEYS = CTX + PAST + LAT
PAIR = 2 * UNITS
TBLOCKS = 4


def unit_keys(u):
    return (0, CTX) if u % UNITS < CTX_Q else (CTX, PAST + LAT)


def key_chunks(n):
    return [(at, min(512, n - at)) for at in range(0, n, 512)]


def block_groups(u):
    nb = unit_keys(u)[1] // P
    return [(at, min(TBLOCKS, nb - at)) for at in range(0, nb, TBLOCKS)]


GROUPS_BEFORE, A_BEFORE, B_BEFORE = [0], [0], [0]
for _u in range(PAIR):
    _n = len(block_groups(_u))
    GROUPS_BEFORE.append(GROUPS_BEFORE[-1] + _n)
    B_BEFORE.append(B_BEFORE[-1] + _n // 2)
    A_BEFORE.append(A_BEFORE[-1] + _n - _n // 2)
PAIR_GROUPS, PAIR_A, PAIR_B = GROUPS_BEFORE[PAIR], A_BEFORE[PAIR], B_BEFORE[PAIR]
SPLIT_AT = 6


def stage_attention(nc, g, o_all, l0_all):
    with stage(nc, "att") as st:
        q_cos, q_sin = st.sb("qcos", [P, T]), st.sb("qsin", [P, LAT])
        k_cos, k_sin = st.sb("kcos", [P, LAT]), st.sb("ksin", [P, LAT])
        q_raw = [st.sb(f"qraw{s}", [P, T]) for s in range(2)]
        q_swp = [st.sb(f"qswp{s}", [P, LAT]) for s in range(2)]
        k_raw = [st.sb(f"kraw{s}", [P, KEYS]) for s in range(2)]
        k_swp = [st.sb(f"kswp{s}", [P, LAT]) for s in range(2)]
        v = [st.sb(f"v{s}", [P, KEYS // P, VD]) for s in range(2)]
        q_hi, q_lo = ([st.sb(f"q{x}{s}", [P, T], F32R) for s in range(2)] for x in ("hi", "lo"))
        k_hi, k_lo = ([st.sb(f"k{x}{s}", [P, KEYS], F32R) for s in range(2)] for x in ("hi", "lo"))
        e = [st.sb(f"e{m}", [P, PAST + LAT]) for m in range(2)]
        a = st.sb("a", [P, PAST + LAT])
        aT = [st.sb(f"aT{s}", [P, (PAST + LAT) // P, P]) for s in range(2)]
        nmax = st.sb("nmax", [P, 2])
        l1, rl1, coef = (st.sb(n, [P, 1]) for n in ("l1", "rl1", "coef"))
        scores = [st.ctx.enter_context(nc.psum_tensor(f"att_s{m}", [P, 3 * 512], F32)) for m in range(2)]
        bank_a, bank_b = st.bank("turn_a"), st.bank("turn_b")
        tables_in, q_in, k_in, v_in = st.sem("tables_in"), *([st.sem(f"{n}_in{s}") for s in range(2)] for n in "qkv")
        prep, rotated, ready, split = (st.sem(n) for n in ("prep", "rotated", "ready", "split"))
        qk = [st.sem(f"qk{m}") for m in range(2)]
        maxed = [st.sem(f"maxed{m}") for m in range(2)]
        exped = [st.sem(f"exped{m}") for m in range(2)]
        small, combined, turned, moved_a, moved_b, pv, o_out = (
            st.sem(n) for n in ("small", "combined", "turned", "moved_a", "moved_b", "pv", "o_out"))
        prep_q, q0_split = st.sem("prep_q"), st.sem("q0_split")
        block = st.block()
        PREP = 2
        Q_DMAS = 5
        K_DMAS = 7

        def before(i, u, n):
            return (i, u - n) if u >= n else (i - 1, PAIR + u - n)

        @block.sync
        def _(sp):
            def load_qk(h, s):
                sp.dma_start(q_raw[s][:], g.projT[h]).then_inc(q_in[s], 16)
                sp.dma_start(k_raw[s][:, 0:CTX], g.projT[h + HEADS, :, 0:CTX]).then_inc(k_in[s], 16)
                sp.dma_start(k_raw[s][:, CTX:CTX + PAST], g.d["cache_kT"][h]).then_inc(k_in[s], 16)
                sp.dma_start(k_raw[s][:, CTX + PAST:], g.projT[h + HEADS, :, CTX:]).then_inc(k_in[s], 16)
                for b in range(4):
                    dst, src = slice(32 * b, 32 * b + 32), slice(32 * (b ^ 1), 32 * (b ^ 1) + 32)
                    sp.dma_start(q_swp[s][dst], g.projT[h, src, CTX:]).then_inc(q_in[s], 16)
                    sp.dma_start(k_swp[s][dst], g.projT[h + HEADS, src, CTX:]).then_inc(k_in[s], 16)

            def load_v(h, s):
                sp.dma_start(v[s][:, 0:2], g.v_heads[h, :, 0:2]).then_inc(v_in[s], 16)
                sp.dma_start(v[s][:, 2:4], g.d["cache_v"][h]).then_inc(v_in[s], 16)
                sp.dma_start(v[s][:, 4:], g.v_heads[h, :, 2:]).then_inc(v_in[s], 16)

            load_qk(0, 0)
            for t, src in ((q_cos, g.d["q_cos"]), (q_sin, g.d["q_sin"]), (k_cos, g.d["k_cos"]),
                           (k_sin, g.d["k_sin"])):
                sp.dma_start(t[:], src).then_inc(tables_in, 16)
            load_v(0, 0)
            load_qk(1, 1)
            load_v(1, 1)
            sp.wait_ge(q0_split, 1)
            with sp.Fori(1, HEADS // 2) as i:
                for s in range(2):
                    sp.wait_ge(ready, 2 * i + s - 1)
                    load_qk(2 * i + s, s)
                    sp.wait_ge(pv, (2 * i + s - 1) * UNITS)
                    load_v(2 * i + s, s)

        @block.gpsimd
        def _(pool):
            def head(i, s, shared=False):
                done = (2 * i + s) * PREP
                parts = ((q_raw[s][:], q_raw[s][:, CTX:], q_cos, q_swp[s], q_sin, q_in[s], Q_DMAS),
                         (k_raw[s][:, CTX + PAST:], k_raw[s][:, CTX + PAST:], k_cos, k_swp[s], k_sin, k_in[s], K_DMAS))
                for j, (full, lat, cos, swp, sin, came, dmas) in enumerate(parts):
                    if shared and j == 0:
                        continue
                    pool.wait_ge(came, 16 * dmas * (i + 1))
                    pool.tensor_tensor(full, full, cos[:], ALU.mult)
                    pool.tensor_tensor(swp[:], swp[:], sin[:], ALU.mult).then_inc(prep, 1 + shared)
                    pool.wait_ge(prep, done + j + 1)
                    pool.tensor_tensor(lat, lat, swp[:], ALU.add).then_inc(rotated, 1)
                pool.wait_ge(split, 2 * (2 * i + s) + 2)
                if not shared:
                    pool.tensor_tensor(q_lo[s][:], q_raw[s][:], q_hi[s][:], ALU.subtract)
                pool.tensor_tensor(k_lo[s][:], k_raw[s][:], k_hi[s][:], ALU.subtract).then_inc(ready, 1)

            pool.wait_ge(tables_in, 64)
            head(0, 0, True)
            with pool.Fori(0, HEADS // 2 - 1) as i:
                head(i, 1)
                head(i + 1, 0)
            head(HEADS // 2 - 1, 1)

        @block.tensor
        def _(pe):
            def qk_map(i, u, m, first):
                s, col = u // UNITS, (u % UNITS) * P
                key0, nk = unit_keys(u)
                if m == 0 and first:
                    pe.wait_ge(q0_split, 1)
                if m == 0 and u % UNITS == 0:
                    pe.wait_ge(ready, 2 * i + s + 1)
                if not first:
                    pe.wait_ge(exped[m], i * PAIR + u)
                rows = slice(HD * m, HD * m + HD)
                for at, n in key_chunks(nk):
                    keys = slice(key0 + at, key0 + at + n)
                    mm = products(pe, scores[m][:, at:at + n], q_hi[s][rows, col:col + P], q_lo[s][rows, col:col + P],
                                  k_hi[s][rows, keys], k_lo[s][rows, keys], True, True)
                mm.then_inc(qk[m], 1)

            def turn(i, u, r, first):
                at, nb = block_groups(u)[r]
                if r == 0:
                    pe.wait_ge(combined, i * PAIR + u + 1)
                    if not first:
                        pe.wait_ge(moved_a, i * PAIR_A + A_BEFORE[u])
                elif r == 1:
                    if not first:
                        pe.wait_ge(o_out, i * PAIR + u)
                else:
                    pe.wait_ge(moved_a, i * PAIR_A + A_BEFORE[u] + 1)
                bank = bank_b if r == 1 else bank_a
                for b in range(nb):
                    mm = pe.transpose(bank[:, b * P:(b + 1) * P], a[:, (at + b) * P:(at + b + 1) * P], g.ident[:])
                mm.then_inc(turned, 1)

            def values(i, u):
                s = u // UNITS
                nb = unit_keys(u)[1] // P
                if u % UNITS == 0:
                    pe.wait_ge(v_in[s], 48 * (i + 1))
                pe.wait_ge(moved_a, i * PAIR_A + A_BEFORE[u + 1])
                if len(block_groups(u)) > 1:
                    pe.wait_ge(moved_b, i * PAIR_B + B_BEFORE[u + 1])
                elif not (isinstance(i, int) and i == 0 and u == 0):
                    pe.wait_ge(o_out, i * PAIR + u)
                for b in range(nb):
                    mm = pe.matmul(bank_b[:, 0:VD], aT[u % 2][:, b], v[s][:, unit_keys(u)[0] // P + b],
                                   start=(b == 0), stop=(b == nb - 1))
                mm.then_inc(pv, 1)

            def turns(i, u):
                for r in range(len(block_groups(u))):
                    turn(i, u, r, isinstance(i, int) and i == 0 and u == 0)

            def body(i, peeled):
                for u in range(PAIR):
                    for m in range(2):
                        qk_map(i, u, m, peeled and u == 0)
                    if not (peeled and u < 2):
                        values(*before(i, u, 2))
                    if not (peeled and u < 1):
                        turns(*before(i, u, 1))

            body(0, True)
            with pe.Fori(1, HEADS // 2) as i:
                body(i, False)
            values(HEADS // 2 - 1, PAIR - 2)
            turns(HEADS // 2 - 1, PAIR - 1)
            values(HEADS // 2 - 1, PAIR - 1)

        @block.scalar
        def _(act):
            def exp_map(i, u, m, first):
                nk = unit_keys(u)[1]
                act.wait_ge(maxed[m], i * PAIR + u + 1)
                if not first:
                    act.wait_ge(combined, i * PAIR + u)
                l = l0_all[:, bass.ds(i * PAIR + u, 1)] if m == 0 else l1[:]
                act.activation(e[m][:, 0:nk], scores[m][:, 0:nk], ACT.Exp, bias=nmax[:, m:m + 1],
                               accum_out=l).then_inc(exped[m], 1)

            def move(i, u, r):
                at, nb = block_groups(u)[r]
                act.wait_ge(turned, i * PAIR_GROUPS + GROUPS_BEFORE[u] + r + 1)
                if r == 0 and not (isinstance(i, int) and i == 0 and u < 2):
                    act.wait_ge(pv, i * PAIR + u - 1)
                act.activation(aT[u % 2][:, at:at + nb], bank_a[:, 0:nb * P], ACT.Copy).then_inc(moved_a, 1)

            def split_head(i, s, first):
                if not first:
                    act.wait_ge(qk[1], (2 * i + s - 1) * UNITS)
                act.wait_ge(rotated, 2 * (2 * i + s) + (2 if first and s == 0 else 1))
                act.activation(q_hi[s][:], q_raw[s][:], ACT.Copy).then_inc(split, 1)
                act.wait_ge(rotated, 2 * (2 * i + s) + 2)
                act.activation(k_hi[s][:], k_raw[s][:], ACT.Copy).then_inc(split, 1)

            def output(i, u):
                act.wait_ge(pv, i * PAIR + u + 1)
                act.activation(o_all[:, bass.ds(i * PAIR + u, 1), :].rearrange("p u e -> p (u e)"), bank_b[:, 0:VD],
                               ACT.Copy).then_inc(o_out, 1)

            def body(i, peeled, last):
                for u in range(PAIR):
                    exp_map(i, u, 0, peeled and u == 0)
                    if not (peeled and u < 2):
                        output(*before(i, u, 2))
                    if not (peeled and u < 1):
                        move(*before(i, u, 1), 0)
                    exp_map(i, u, 1, peeled and u == 0)
                    if not (peeled and u < 1) and len(block_groups(before(0, u, 1)[1])) > 2:
                        move(*before(i, u, 1), 2)
                    if u == SPLIT_AT:
                        split_head(i, 1, peeled)
                    if u == UNITS + SPLIT_AT and not last:
                        split_head(i + 1, 0, False)

            split_head(0, 0, True)
            body(0, True, False)
            with act.Fori(1, HEADS // 2 - 1) as i:
                body(i, False, False)
            body(HEADS // 2 - 1, False, True)
            output(HEADS // 2 - 1, PAIR - 2)
            for r in (0, 2):
                move(HEADS // 2 - 1, PAIR - 1, r)
            output(HEADS // 2 - 1, PAIR - 1)

        @block.vector
        def _(dve):
            def row_max(i, u, m, first):
                nk = unit_keys(u)[1]
                dve.wait_ge(qk[m], i * PAIR + u + 1)
                if not first:
                    dve.wait_ge(exped[m], i * PAIR + u)
                dve.tensor_reduce(nmax[:, m:m + 1], scores[m][:, 0:nk], AX.X, ALU.max, negate=True
                                  ).then_inc(maxed[m], 1)

            def move(i, u):
                at, nb = block_groups(u)[1]
                dve.wait_ge(turned, i * PAIR_GROUPS + GROUPS_BEFORE[u] + 2)
                if not (isinstance(i, int) and i == 0 and u < 2):
                    dve.wait_ge(pv, i * PAIR + u - 1)
                dve.tensor_copy(aT[u % 2][:, at:at + nb].rearrange("p b q -> p (b q)"), bank_b[:, 0:nb * P]
                                ).then_inc(moved_b, 1)

            def combine(i, u, first):
                nk = unit_keys(u)[1]
                c = i * PAIR + u
                for m in range(2):
                    dve.wait_ge(exped[m], c + 1)
                dve.reciprocal(rl1[:], l1[:]).then_inc(small, 1)
                dve.wait_ge(small, 2 * c + 1)
                dve.scalar_tensor_tensor(out=coef[:], in0=l0_all[:, bass.ds(c, 1)], scalar=rl1[:], in1=g.neg_lam[:],
                                         op0=ALU.mult, op1=ALU.mult).then_inc(small, 1)
                dve.wait_ge(small, 2 * c + 2)
                if not first:
                    dve.wait_ge(turned, i * PAIR_GROUPS + GROUPS_BEFORE[u])
                dve.scalar_tensor_tensor(out=a[:, 0:nk], in0=e[1][:, 0:nk], scalar=coef[:], in1=e[0][:, 0:nk],
                                         op0=ALU.mult, op1=ALU.add).then_inc(combined, 1)

            def body(i, peeled):
                for u in range(PAIR):
                    if not (peeled and u < 1):
                        combine(*before(i, u, 1), peeled and u == 1)
                    for m in range(2):
                        row_max(i, u, m, peeled and u == 0)
                    if not (peeled and u < 1) and len(block_groups(before(0, u, 1)[1])) > 1:
                        move(*before(i, u, 1))

            dve.wait_ge(tables_in, 64)
            dve.wait_ge(q_in[0], 16 * Q_DMAS)
            dve.tensor_tensor(q_raw[0][:], q_raw[0][:], q_cos[:], ALU.mult)
            dve.tensor_tensor(q_swp[0][:], q_swp[0][:], q_sin[:], ALU.mult).then_inc(prep_q, 1)
            dve.wait_ge(prep_q, 1)
            dve.tensor_tensor(q_raw[0][:, CTX:], q_raw[0][:, CTX:], q_swp[0][:], ALU.add).then_inc(rotated, 1)
            dve.wait_ge(split, 1)
            dve.tensor_tensor(q_lo[0][:], q_raw[0][:], q_hi[0][:], ALU.subtract).then_inc(q0_split, 1)
            body(0, True)
            with dve.Fori(1, HEADS // 2) as i:
                body(i, False)
            combine(HEADS // 2 - 1, PAIR - 1, False)
            move(HEADS // 2 - 1, PAIR - 1)
            dve.wait_ge(o_out, HEADS * UNITS)


def stage_attn_norm(nc, g, o_all, l0_all):
    N = HEADS * UNITS
    G = 2
    NG = N // G
    HG = UNITS // G
    with stage(nc, "an") as st:
        sq = st.sb("sq", [P, 2, UNITS, VD])
        ss, e2, var, std, scale = (st.sb(n, [P, N]) for n in ("ss", "e2", "var", "std", "scale"))
        oT = st.sb("oT", [P, 2, T])
        banks = [st.bank(f"t{i}") for i in range(4)]
        squared, summed, small, stdd, scaled, turned, out = (
            st.sem(n) for n in ("squared", "summed", "small", "stdd", "scaled", "turned", "out"))
        stored = [st.sem(f"stored{s}") for s in range(2)]
        block = st.block()

        @block.sync
        def _(sp):
            for h in range(HEADS):
                sp.wait_ge(out, (h + 1) * HG)
                sp.dma_start(g.oT[h], oT[:, h % 2]).then_inc(stored[h % 2], 16)
            for s in range(2):
                sp.wait_ge(stored[s], 16 * HEADS // 2)

        @block.scalar
        def _(act):
            for h in range(HEADS):
                if h >= 2:
                    act.wait_ge(summed, h - 1)
                act.activation(sq[:, h % 2], o_all[:, h * UNITS:(h + 1) * UNITS, :], ACT.Square).then_inc(squared, 1)
            act.wait_ge(small, 2)
            act.activation(std[:], var[:], ACT.Sqrt).then_inc(stdd, 1)
            for n in range(NG):
                h, u = divmod(n, HG)
                act.wait_ge(turned, n + 1)
                if h >= 2 and u == 0:
                    act.wait_ge(stored[h % 2], 16 * (h // 2))
                act.activation(oT[:, h % 2, u * G * P:(u + 1) * G * P], banks[n % 4][:, 0:G * P], ACT.Copy,
                               scale=g.subln[:]).then_inc(out, 1)

        @block.vector
        def _(dve):
            dve.tensor_tensor(e2[:], l0_all[:], l0_all[:], ALU.mult).then_inc(small, 1)
            for h in range(HEADS):
                dve.wait_ge(squared, h + 1)
                dve.tensor_reduce(ss[:, h * UNITS:(h + 1) * UNITS], sq[:, h % 2], AX.X, ALU.add).then_inc(summed, 1)
            dve.wait_ge(small, 1)
            dve.wait_ge(summed, HEADS)
            dve.scalar_tensor_tensor(out=var[:], in0=e2[:], scalar=EPS * VD, in1=ss[:], op0=ALU.mult, op1=ALU.add
                                     ).then_inc(small, 1)
            dve.wait_ge(stdd, 1)
            dve.reciprocal(scale[:], std[:]).then_inc(small, 1)
            dve.wait_ge(small, 3)
            for n in range(N):
                m = dve.tensor_scalar(o_all[:, n], o_all[:, n], scale[:, n:n + 1], VD ** 0.5, ALU.mult, ALU.mult)
                if n % G == G - 1:
                    m.then_inc(scaled, 1)

        @block.tensor
        def _(pe):
            for n in range(NG):
                pe.wait_ge(scaled, n + 1)
                if n >= 4:
                    pe.wait_ge(out, n - 3)
                for j in range(G):
                    mm = pe.transpose(banks[n % 4][:, j * P:(j + 1) * P], o_all[:, n * G + j], g.ident[:])
                mm.then_inc(turned, 1)


LAT_FT, CTX_FT = LAT // P, CTX // P
FTILES = LAT_FT + CTX_FT
HALF_T = [LAT // 2 // P, CTX // 2 // P]
HT = sum(HALF_T)
KU = 4
SPEC = 3
FILT_LAT_U, FILT_CTX_U = 2 * LAT_FT + 1, 2 * CTX_FT + 1
N_FILT_U = FILT_LAT_U + FILT_CTX_U
FWD_U = 2 * LAT_FT + 1
INV_U = 4 * HALF_T[0] + 1
TWO_PI_HI = 6.28125
TWO_PI_LO = 2 * math.pi - TWO_PI_HI
ROUND = 1.5 * 2.0 ** 23
PI_F = 3.1415925


def even_tile(j):
    return j < LAT_FT // 2 if j < LAT_FT else j - LAT_FT < CTX_FT // 2


def filter_units():
    lat = [(j, c) for j in range(LAT_FT) for c in range(2)]
    ctx = [(LAT_FT + j, c) for j in range(CTX_FT) for c in range(2)]
    return lat + [(0, 2)] + ctx + [(LAT_FT, 2)]


def stage_filter_net(nc, g, h_hi, h_lo, w3_hi, w3_lo):
    N = CTX + LAT
    MLP_CH = [(0, 512), (512, 512), (1024, 256)]
    LOADS = 5
    with stage(nc, "net") as st:
        emb = st.sb("emb", [EMB, N])
        w1, w2 = st.sb("w1", [EMB, HID]), st.sb("w2", [HID, HID])
        w3 = st.sb("w3", [HID, 2, 2, CH])
        vec = st.sb("vec", [HID, 3])
        y, n, h = (st.sb(x, [HID, N]) for x in ("y", "n", "h"))
        bank = [st.bank(f"b{i}") for i in range(len(MLP_CH))]
        loaded, mlp_mm, mlp, hs, w3s, fix = (st.sem(x) for x in ("loaded", "mlp_mm", "mlp", "hs", "w3s", "fix"))
        block = st.block()

        @block.sync
        def _(sp):
            for dst, src in ((emb[:], g.d["emb"]), (w1[:], g.d["filt_w1"]), (w2[:], g.d["filt_w2"]),
                             (vec[:], g.d["filt_vec"]), (w3[:], g.d["filt_w3"])):
                sp.dma_start(dst, src).then_inc(loaded, 16)

        @block.tensor
        def _(pe):
            pe.wait_ge(loaded, 16 * LOADS)
            for layer in range(2):
                if layer:
                    pe.wait_ge(mlp, 5)
                w, x = (w1, emb) if layer == 0 else (w2, h)
                for i, (at, m) in enumerate(MLP_CH):
                    mm = pe.matmul(bank[i][0:HID, 0:m], w[:], x[:, at:at + m], start=True, stop=True)
                mm.then_inc(mlp_mm, 1)

        @block.scalar
        def _(act):
            act.wait_ge(loaded, 16 * LOADS)
            act.activation(w3_hi[:], w3[:], ACT.Copy).then_inc(w3s, 1)
            for layer in range(2):
                act.wait_ge(mlp, 5 * layer + 4)
                act.activation(h[:], y[:], ACT.Sin).then_inc(mlp, 1)
            act.wait_ge(mlp, 10)
            act.activation(h_hi[:], h[:], ACT.Copy).then_inc(hs, 1)

        @block.gpsimd
        def _(pool):
            pool.wait_ge(w3s, 1)
            pool.tensor_tensor(w3_lo[:], w3[:], w3_hi[:], ALU.subtract).then_inc(w3s, 1)
            pool.wait_ge(w3s, 2)

        @block.vector
        def _(dve):
            dve.wait_ge(loaded, 16 * LOADS)
            for layer in range(2):
                dve.wait_ge(mlp_mm, layer + 1)
                base = 5 * layer
                for i, (at, m) in enumerate(MLP_CH):
                    a = dve.tensor_scalar(y[:, at:at + m], bank[i][0:HID, 0:m], vec[:, layer:layer + 1], vec[:, 2:3],
                                          ALU.add, ALU.mult)
                a.then_inc(mlp, 1)
                dve.wait_ge(mlp, base + 1)
                dve.tensor_scalar(n[:], y[:], 1 / (2 * math.pi), ROUND, ALU.mult, ALU.add).then_inc(fix, 1)
                dve.wait_ge(fix, 2 * layer + 1)
                dve.tensor_scalar(n[:], n[:], -ROUND, None, ALU.add).then_inc(fix, 1)
                dve.wait_ge(fix, 2 * layer + 2)
                dve.scalar_tensor_tensor(out=y[:], in0=n[:], scalar=-TWO_PI_HI, in1=y[:], op0=ALU.mult, op1=ALU.add
                                         ).then_inc(mlp, 1)
                dve.wait_ge(mlp, base + 2)
                dve.scalar_tensor_tensor(out=y[:], in0=n[:], scalar=-TWO_PI_LO, in1=y[:], op0=ALU.mult, op1=ALU.add
                                         ).then_inc(mlp, 1)
                dve.wait_ge(mlp, base + 3)
                dve.tensor_scalar(y[:], y[:], PI_F, -PI_F, ALU.min, ALU.max).then_inc(mlp, 1)
            dve.wait_ge(hs, 1)
            dve.tensor_tensor(h_lo[:], h[:], h_hi[:], ALU.subtract).then_inc(hs, 1)
            dve.wait_ge(hs, 2)


def stage_filters(nc, g, h_hi, h_lo, w3_hi, w3_lo):
    NB = 3
    UN = filter_units()
    with stage(nc, "flt") as st:
        decay = st.sb("decay", [P, 2 * HT, CH])
        wf = st.sb("wf", [P, FTILES])
        cb = st.sb("cb", [P, 2, CH])
        t = st.sb("t", [P, 4, CH])
        eo = [st.sb(f"eo{s}", [P, 5, CH]) for s in range(2)]
        wa = [st.sb(f"wa{s}", [P, KD, P]) for s in range(2)]
        pm = st.bank("mod")[:, 0:FIRST_ADA * 2].rearrange("p (u s) -> p u s", s=2)
        NL = 4 * HALF_T[0] + 1
        NX = 4 * HALF_T[1]
        x_hi, x_lo = st.sb("xhi", [P, NL + NX, CH], F32R), st.sb("xlo", [P, NL + NX, CH], F32R)
        raw = [st.sb(f"raw{s}", [P, KU, P]) for s in range(2)]
        t_hi = [st.sb(f"thi{s}", [P, KU, P], F32R) for s in range(2)]
        t_lo = [st.sb(f"tlo{s}", [P, KU, P], F32R) for s in range(2)]
        OB = 4
        ob = [st.sb(f"ob{s}", [P, CH]) for s in range(OB)]
        bank = [st.bank(f"b{i}") for i in range(4 + NB)]
        (loaded, taps, copied, mixed, split_hi, split_lo, tab_hi, tab_lo, spec_mm, scaled, step_done, made, ada_mm,
         mod_done) = (st.sem(x) for x in (
            "loaded", "taps", "copied", "mixed", "split_hi", "split_lo", "tab_hi", "tab_lo", "spec_mm", "scaled",
            "step_done", "made", "ada_mm", "mod_done"))
        ada_in = [st.sem(f"ada_in{s}") for s in range(2)]
        raw_in = [st.sem(f"raw_in{s}") for s in range(2)]
        stored = [st.sem(f"stored{s}") for s in range(OB)]
        block = st.block()
        LOADS = 2
        EARLY = {8: 0, 15: 1}
        ADA_BY_PAIR = [2, 2, 2, 2, 2, 0, 0, 2, 2, 2]
        assert sum(ADA_BY_PAIR) == FIRST_ADA
        PAIRS = HALF_T[0] + HALF_T[1]
        SLOTS = [0]
        for p in range(PAIRS):
            SLOTS.append(SLOTS[-1] + (5 if p == 0 else 4))

        def slots_before(k):
            return k // PAIRS * SLOTS[PAIRS] + SLOTS[k % PAIRS]

        def slots(p):
            if p < HALF_T[0]:
                base = [p, HALF_T[0] + p, 2 * HALF_T[0] + p, 3 * HALF_T[0] + p]
                return base + ([4 * HALF_T[0]] if p == 0 else [])
            return [NL + k for k in range(4)]

        def operands(j, c):
            H = HALF_T[0]
            if j >= LAT_FT:
                return [NL + 0, NL + 1] if c != 1 else [NL + 2, NL + 3]
            if c == 1:
                kind = 3 if even_tile(j) else 2
            else:
                kind = 0 if even_tile(j) else 1
            out = [kind * H + k for k in range(H)]
            if c != 1 and LAT_FT // 4 <= j < LAT_FT // 2:
                out[0] = 4 * H
            return out

        @block.sync
        def _(sp):
            def load_ada(n):
                if n >= 2:
                    sp.wait_ge(ada_mm, n - 1)
                sp.dma_start(wa[n % 2][:], g.d["w_ada"][n]).then_inc(ada_in[n % 2], 16)

            first_order = sum(ADA_BY_PAIR[:PAIRS])
            sp.dma_start(decay[:], g.d["decay"]).then_inc(loaded, 16)
            sp.dma_start(wf[:], g.d["wf"]).then_inc(loaded, 16)
            for n in range(2):
                load_ada(n)
            total = 2 * len(UN)
            for m in range(2):
                sp.dma_start(raw[m][:], g.d["filt_tab"][m]).then_inc(raw_in[m], 16)
            for n in range(2, first_order):
                load_ada(n)
            for m in range(total):
                if m == len(UN) - 2:
                    for n in range(first_order, first_order + 2):
                        load_ada(n)
                if m == len(UN):
                    for n in range(first_order + 2, FIRST_ADA):
                        load_ada(n)
                if m + 2 < total:
                    sp.wait_ge(tab_lo, m + 1)
                    sp.dma_start(raw[m % 2][:], g.d["filt_tab"][(m + 2) % len(UN)]).then_inc(raw_in[m % 2], 16)

        @block.tensor
        def _(pe):
            def modulation(k):
                for n in range(sum(ADA_BY_PAIR[:k]), sum(ADA_BY_PAIR[:k + 1])):
                    pe.wait_ge(ada_in[n % 2], 16 * (n // 2 + 1))
                    for kk in range(KD):
                        mm = pe.matmul(pm[:, n, :], wa[n % 2][:, kk], g.silu[:, kk], start=(kk == 0),
                                       stop=(kk == KD - 1))
                    mm.then_inc(ada_mm, 1)

            def taps_of(o, p):
                k = o * PAIRS + p
                if k:
                    pe.wait_ge(mixed, k)
                for i in range(4):
                    tile = 2 * p + i // 2
                    mm = products(pe, bank[i][:], h_hi[:, tile * P:(tile + 1) * P], h_lo[:, tile * P:(tile + 1) * P],
                                  w3_hi[:, i % 2, o], w3_lo[:, i % 2, o], True, True)
                mm.then_inc(taps, 1)

            for o in range(2):
                for p in range(len(EARLY) if o else 0, PAIRS):
                    taps_of(o, p)
                    modulation(o * PAIRS + p)
                for u, (j, c) in enumerate(UN):
                    m = o * len(UN) + u
                    if o == 0 and u in EARLY:
                        taps_of(1, EARLY[u])
                    pe.wait_ge(tab_lo, m + 1)
                    if u == 0:
                        pe.wait_ge(split_lo, (o + 1) * SLOTS[PAIRS])
                    if m >= NB:
                        pe.wait_ge(scaled, m - NB + 1)
                    ops = operands(j, c)
                    for k, x in enumerate(ops):
                        mm = products(pe, bank[4 + m % NB][:], t_hi[m % 2][:, k], t_lo[m % 2][:, k], x_hi[:, x],
                                      x_lo[:, x], k == 0, k == len(ops) - 1)
                    mm.then_inc(spec_mm, 1)

        @block.scalar
        def _(act):
            def table(m):
                act.wait_ge(raw_in[m % 2], 16 * (m // 2 + 1))
                if m >= 2:
                    act.wait_ge(spec_mm, m - 1)
                act.activation(t_hi[m % 2][:], raw[m % 2][:], ACT.Copy).then_inc(tab_hi, 1)

            def copy(o, p):
                k = o * PAIRS + p
                act.wait_ge(taps, k + 1)
                if k:
                    act.wait_ge(mixed, k)
                for i in range(2):
                    a = act.activation(cb[:, i], bank[2 * i + 1][:], ACT.Copy)
                a.then_inc(copied, 1)

            def split(o, p):
                k = o * PAIRS + p
                act.wait_ge(made, k + 1)
                for i, x in enumerate(slots(p)):
                    act.activation(x_hi[:, x], eo[k % 2][:, i], ACT.Copy).then_inc(split_hi, 1)

            for o in range(2):
                if o:
                    act.wait_ge(spec_mm, len(UN))
                    split(1, 0)
                else:
                    copy(0, 0)
                for p in range(o, PAIRS):
                    if p + 1 < PAIRS and not (o and p + 1 < len(EARLY)):
                        copy(o, p + 1)
                    split(o, p)
                for u in range(len(UN)):
                    if o == 0 and u in EARLY:
                        copy(1, EARLY[u])
                    table(o * len(UN) + u)

        @block.gpsimd
        def _(pool):
            def store(m):
                pool.wait_ge(scaled, m + 1)
                o, (j, c) = m // len(UN), UN[m % len(UN)]
                pool.dma_start(g.spec[o, j, :, c, :], ob[m % OB][:]).then_inc(stored[m % OB], 16)

            for o in range(2):
                for p in range(PAIRS):
                    for i, x in enumerate(slots(p)):
                        pool.wait_ge(split_hi, o * SLOTS[PAIRS] + SLOTS[p] + i + 1)
                        pool.tensor_tensor(x_lo[:, x], eo[(o * PAIRS + p) % 2][:, i], x_hi[:, x], ALU.subtract
                                           ).then_inc(split_lo, 1)
                for u in range(len(UN)):
                    m = o * len(UN) + u
                    if m >= 2:
                        store(m - 2)
                    pool.wait_ge(tab_hi, m + 1)
                    pool.tensor_tensor(t_lo[m % 2][:], raw[m % 2][:], t_hi[m % 2][:], ALU.subtract
                                       ).then_inc(tab_lo, 1)
            for m in range(2 * len(UN) - 2, 2 * len(UN)):
                store(m)
            for s in range(OB):
                pool.wait_ge(stored[s], 16 * (2 * len(UN) // OB))

        @block.vector
        def _(dve):
            dve.wait_ge(loaded, 16 * LOADS)
            done = [0]

            def step(ins):
                ins.then_inc(step_done, 1)
                done[0] += 1
                dve.wait_ge(step_done, done[0])

            def pair(o, p):
                k = o * PAIRS + p
                eo_k = eo[k % 2]
                if k >= 2:
                    dve.wait_ge(split_lo, slots_before(k - 1))
                dve.wait_ge(copied, k + 1)
                for i in range(2):
                    dve.tensor_tensor(t[:, i], bank[2 * i][:], cb[:, i], ALU.add)
                    a = dve.tensor_tensor(t[:, 2 + i], bank[2 * i][:], cb[:, i], ALU.subtract)
                a.then_inc(mixed, 1)
                dve.wait_ge(mixed, k + 1)
                lat = p < HALF_T[0]
                for i in range(2):
                    dst = t if lat else eo_k
                    dve.tensor_tensor(dst[:, i], t[:, i], decay[:, 2 * p + i], ALU.mult)
                    a = dve.tensor_tensor(dst[:, 2 + i], t[:, 2 + i], decay[:, 2 * p + i], ALU.mult)
                step(a)
                if lat:
                    for i in range(2):
                        dve.tensor_tensor(eo_k[:, 2 * i], t[:, 2 * i], t[:, 2 * i + 1], ALU.add)
                        a = dve.tensor_tensor(eo_k[:, 2 * i + 1], t[:, 2 * i], t[:, 2 * i + 1], ALU.subtract)
                    step(a)
                if p == 0:
                    step(dve.tensor_copy(eo_k[:, 4], eo_k[:, 0]))
                    step(dve.tensor_copy(eo_k[0:1, 4], eo_k[0:1, 1]))
                    step(dve.tensor_copy(eo_k[0:1, 1], t[0:1, 0]))
                    step(dve.tensor_copy(eo_k[0:1, 2], t[0:1, 3]))
                dve.sem_inc(made, 1)

            for o in range(2):
                for p in range(len(EARLY) if o else 0, PAIRS):
                    pair(o, p)
                for u, (j, c) in enumerate(UN):
                    m = o * len(UN) + u
                    if o == 0 and u in EARLY:
                        pair(1, EARLY[u])
                    dve.wait_ge(spec_mm, m + 1)
                    if m >= OB:
                        dve.wait_ge(stored[m % OB], 16 * (m // OB))
                    dve.tensor_scalar(ob[m % OB][:], bank[4 + m % NB][:], wf[:, j:j + 1], None, ALU.mult
                                      ).then_inc(scaled, 1)
            dve.wait_ge(ada_mm, FIRST_ADA)
            for s in range(2):
                a = dve.tensor_tensor(g.mod[:, 0:FIRST_ADA, s], pm[:, :, s], g.bada[:, 0:FIRST_ADA], ALU.add)
            a.then_inc(mod_done, 1)
            dve.wait_ge(mod_done, 1)


def stored_columns(mirror, tile):
    first, L, tile = (CTX, LAT, tile) if tile < HALF_T[0] else (0, CTX, tile - HALF_T[0])
    first += mirror * (L // 2)
    return slice(first + tile * P, first + (tile + 1) * P)


def folded_columns(mirror, tile):
    if not mirror:
        return stored_columns(mirror, tile)
    first, L, tile = (CTX, LAT, tile) if tile < HALF_T[0] else (0, CTX, tile - HALF_T[0])
    last = first + L - 1 - tile * P
    return slice(last, last - P if last >= P else None, -1)


def stage_turn(nc, g, z):
    with stage(nc, "tu") as st:
        conv = st.sb("conv", [P, 2 * CHT, T])
        x1 = st.sb("x1", [P, 2, HT, CH])
        bank = [st.bank(f"b{i}") for i in range(4)]
        cached, turned, moved, x1_out = (st.sem(x) for x in ("cached", "turned", "moved", "x1_out"))
        conv_in = [st.sem(f"conv_in{s}") for s in range(2)]
        block = st.block()
        JOBS = [(src, tile, mirror) for src in (1, 0) for tile in range(HT) for mirror in range(2)]

        @block.sync
        def _(sp):
            for n in (*range(CHT, 2 * CHT), *range(CHT)):
                sp.dma_start(conv[:, n], g.convT[n]).then_inc(conv_in[n // CHT], 16)
            sp.dma_start(g.new_v, g.v[0:CTX // P]).then_inc(cached, 16)
            for n in range(HT):
                sp.wait_ge(moved, 2 * n + 2)
                sp.dma_start(g.x1t[n], x1[:, :, n]).then_inc(x1_out, 16)
            sp.wait_ge(x1_out, 16 * HT)
            sp.wait_ge(cached, 16)

        @block.tensor
        def _(pe):
            for n, (src, tile, mirror) in enumerate(JOBS):
                if n % (2 * HT) == 0:
                    pe.wait_ge(conv_in[src], 16 * CHT)
                if n >= 4:
                    pe.wait_ge(moved, n - 3)
                for c in range(CHT):
                    mm = pe.transpose(bank[n % 4][:, c * P:(c + 1) * P],
                                      conv[:, src * CHT + c, stored_columns(mirror, tile)], g.ident[:])
                mm.then_inc(turned, 1)

        @block.scalar
        def _(act):
            for n, (src, tile, mirror) in enumerate(JOBS):
                act.wait_ge(turned, n + 1)
                dst = x1[:, mirror, tile] if src else z[mirror][:, tile]
                act.activation(dst, bank[n % 4][:], ACT.Copy).then_inc(moved, 1)
            act.wait_ge(moved, len(JOBS))


FWD_RUNS = 2 * FTILES
RUNS = FWD_RUNS + 4 * HT
NU = FWD_U + INV_U


def runs_after_unit(m):
    o, u = divmod(m, NU)
    if u < FWD_U - 1:
        n = u + 1
    elif u == FWD_U - 1:
        n = FWD_RUNS
    elif u < NU - 1:
        n = FWD_RUNS + u - FWD_U + 1
    else:
        n = RUNS
    return o * RUNS + n


def next_units(o, j=None, tile=None):
    if j is not None:
        u = [2 * j, 2 * j + 1] if j < LAT_FT else [FWD_U - 1] if j == FTILES - 1 else []
    else:
        u = [FWD_U + 4 * tile + k for k in range(4)] if tile < HALF_T[0] else [NU - 1]
    return [m for m in (o * NU + x + 2 for x in u) if m < 2 * NU]


def stage_hyena(nc, g, z):
    with stage(nc, "hy") as st:
        e_hi, e_lo, o_hi, o_lo = (st.sb(x, [P, HT, CH], F32R) for x in ("ehi", "elo", "ohi", "olo"))
        gc_hi, gc_lo, gs_hi, gs_lo = (st.sb(x, [P, FTILES, CH], F32R) for x in ("gchi", "gclo", "gshi", "gslo"))
        raw = [st.sb(f"raw{s}", [P, KU, P]) for s in range(2)]
        t_hi = [st.sb(f"thi{s}", [P, KU, P], F32R) for s in range(2)]
        t_lo = [st.sb(f"tlo{s}", [P, KU, P], F32R) for s in range(2)]
        spec = [st.sb(f"spec{s}", [P, SPEC, CH]) for s in range(2)]
        scr = [st.sb(f"scr{s}", [P, 4, CH]) for s in range(2)]
        gate = [st.sb(f"gate{s}", [P, 2, CH]) for s in range(2)]
        p_sb = [st.sb(f"p{s}", [P, CH]) for s in range(2)]
        bias = st.sb("bias_b", [P, 2, CH])
        bank = [st.bank(f"b{i}") for i in range(8)]
        names = ("bias_in", "runs", "tab_hi", "tab_lo", "folded", "fold_hi", "fold_lo", "fwd_read", "g_ready", "g_hi",
                 "g_lo", "biased", "p_copied", "q_read", "zdone", "step")
        (bias_in, runs, tab_hi, tab_lo, folded, fold_hi, fold_lo, fwd_read, g_ready, g_hi, g_lo, biased, p_copied,
         q_read, zdone, step_sem) = (st.sem(x) for x in names)
        raw_in = [st.sem(f"raw_in{s}") for s in range(2)]
        spec_in = [st.sem(f"spec_in{s}") for s in range(2)]
        gate_in = [st.sem(f"gate_in{s}") for s in range(2)]
        block = st.block()

        def spectra(j):
            return SPEC if j in (0, LAT_FT) else 2

        @block.sync
        def _(sp):
            def load(m):
                sp.dma_start(raw[m % 2][:], g.d["hy_tab"][m % NU]).then_inc(raw_in[m % 2], 16)

            sp.dma_start(bias[:], g.d["hy_bias"]).then_inc(bias_in, 16)
            for m in range(2):
                load(m)
            for o in range(2):
                for m in [m for j in range(FTILES) for m in next_units(o, j=j)] + [
                        m for i in range(HT) for m in next_units(o, tile=i)]:
                    sp.wait_ge(tab_lo, m - 1)
                    load(m)

        @block.tensor
        def _(pe):
            for o in range(2):
                for j in range(FTILES):
                    if j in (0, LAT_FT):
                        pe.wait_ge(fold_lo, o * HT + (HT if j else HALF_T[0]))
                    n = o * FTILES + j
                    if n >= 2:
                        pe.wait_ge(fwd_read, n - 1)
                    for c in range(2):
                        hi, lo = (e_hi, e_lo) if even_tile(j) == (c == 0) else (o_hi, o_lo)
                        if j < LAT_FT:
                            unit, at, tiles = 2 * j + c, 0, range(HALF_T[0])
                        else:
                            unit, at, tiles = FWD_U - 1, 2 * (j - LAT_FT) + c, range(HALF_T[0], HT)
                        m = o * NU + unit
                        pe.wait_ge(tab_lo, m + 1)
                        for k, tile in enumerate(tiles):
                            mm = products(pe, bank[2 * (n % 2) + c][:], t_hi[m % 2][:, at + k], t_lo[m % 2][:, at + k],
                                          hi[:, tile], lo[:, tile], k == 0, k == len(tiles) - 1)
                        mm.then_inc(runs, 1)
                for i in range(HT):
                    n = o * HT + i
                    if n >= 2:
                        pe.wait_ge(q_read, n - 1)
                    for q in range(2):
                        for half in range(2):
                            hi, lo = (gs_hi, gs_lo) if half else (gc_hi, gc_lo)
                            odd = half ^ q
                            if i < HALF_T[0]:
                                unit, at = FWD_U + 4 * i + 2 * q + half, 0
                                tiles = range(LAT_FT // 2 * odd, LAT_FT // 2 * (odd + 1))
                            else:
                                unit, at, tiles = NU - 1, 2 * q + half, range(LAT_FT + odd, LAT_FT + odd + 1)
                            m = o * NU + unit
                            pe.wait_ge(tab_lo, m + 1)
                            if q == 0 and half == 0 and i in (0, HALF_T[0]):
                                pe.wait_ge(g_lo, 2 * (o * FTILES + (FTILES if i else LAT_FT)))
                            for k, tile in enumerate(tiles):
                                mm = products(pe, bank[4 + 2 * (n % 2) + q][:], t_hi[m % 2][:, at + k],
                                              t_lo[m % 2][:, at + k], hi[:, tile], lo[:, tile],
                                              half == 0 and k == 0, half == 1 and k == len(tiles) - 1)
                            mm.then_inc(runs, 1)

        @block.scalar
        def _(act):
            def table(m):
                act.wait_ge(raw_in[m % 2], 16 * (m // 2 + 1))
                if m >= 2:
                    act.wait_ge(runs, runs_after_unit(m - 2))
                act.activation(t_hi[m % 2][:], raw[m % 2][:], ACT.Copy).then_inc(tab_hi, 1)

            def split_fold(n):
                act.wait_ge(folded, n + 1)
                act.activation(e_hi[:, n % HT], scr[n % 2][:, 0], ACT.Copy).then_inc(fold_hi, 1)
                act.activation(o_hi[:, n % HT], scr[n % 2][:, 1], ACT.Copy).then_inc(fold_hi, 1)

            def split_product(n):
                j = n % FTILES
                act.wait_ge(g_ready, n + 1)
                act.activation(gc_hi[:, j], scr[n % 2][:, 0], ACT.Copy).then_inc(g_hi, 1)
                act.activation(gs_hi[:, j], scr[n % 2][:, 2], ACT.Copy).then_inc(g_hi, 1)

            for i in range(2):
                split_fold(i)
            for m in range(2):
                table(m)
            for i in range(2, HT):
                split_fold(i)
            for o in range(2):
                for j in range(FTILES):
                    ahead = next_units(o, j=j)
                    for m in ahead[:1]:
                        table(m)
                    if j:
                        split_product(o * FTILES + j - 1)
                    for m in ahead[1:]:
                        table(m)
                split_product((o + 1) * FTILES - 1)
                for i in range(HT):
                    ahead = next_units(o, tile=i)
                    if i < HT - 1:
                        table(ahead.pop(0))
                    if o == 0 and i:
                        split_fold(HT + i - 1)
                    for m in ahead:
                        table(m)
                    n = o * HT + i
                    act.wait_ge(runs, o * RUNS + FWD_RUNS + 4 * (i + 1))
                    if n >= 2:
                        act.wait_ge(q_read, n - 1)
                    act.activation(p_sb[n % 2][:], bank[4 + 2 * (n % 2)][:], ACT.Copy).then_inc(p_copied, 1)
                if o == 0:
                    split_fold(2 * HT - 1)

        @block.gpsimd
        def _(pool):
            def load_spec(n):
                o, j = divmod(n, FTILES)
                if n >= 2:
                    pool.wait_ge(fwd_read, n - 1)
                pool.dma_start(spec[n % 2][:, 0:spectra(j)], g.spec[o, j, :, 0:spectra(j), :]
                               ).then_inc(spec_in[n % 2], 16)

            def load_gate(i):
                pool.dma_start(gate[i % 2][:], g.x1t[i]).then_inc(gate_in[i % 2], 16)

            def table(m):
                pool.wait_ge(tab_hi, m + 1)
                pool.tensor_tensor(t_lo[m % 2][:], raw[m % 2][:], t_hi[m % 2][:], ALU.subtract).then_inc(tab_lo, 1)

            for m in range(2):
                load_spec(m)
                load_gate(m)
            for m in range(2):
                table(m)
            for o in range(2):
                for j in range(FTILES):
                    for m in next_units(o, j=j):
                        table(m)
                    if o * FTILES + j + 2 < 2 * FTILES:
                        load_spec(o * FTILES + j + 2)
                if o == 0:
                    pool.wait_ge(bias_in, 16)
                pool.wait_ge(g_lo, 2 * (o + 1) * FTILES)
                for i in range(HT):
                    n = o * HT + i
                    if i >= 2:
                        pool.wait_ge(zdone, n - 1)
                        if o == 0:
                            load_gate(i)
                    for h in range(2):
                        m = pool.tensor_tensor(scr[n % 2][:, 2 + h], z[h][:, i], bias[:, o], ALU.mult)
                    m.then_inc(biased, 1)
                    for m in next_units(o, tile=i):
                        table(m)

        @block.vector
        def _(dve):
            n_steps = [0]

            def step(ins):
                ins.then_inc(step_sem, 1)
                n_steps[0] += 1
                dve.wait_ge(step_sem, n_steps[0])

            def fold(n):
                if n >= 2:
                    dve.wait_ge(fold_lo, n - 1)
                i = n % HT
                dve.tensor_tensor(scr[n % 2][:, 0], z[0][:, i], z[1][:, i], ALU.add)
                dve.tensor_tensor(scr[n % 2][:, 1], z[0][:, i], z[1][:, i], ALU.subtract).then_inc(folded, 1)

            def fold_low(n):
                dve.wait_ge(fold_hi, 2 * n + 2)
                dve.tensor_tensor(e_lo[:, n % HT], scr[n % 2][:, 0], e_hi[:, n % HT], ALU.subtract)
                dve.tensor_tensor(o_lo[:, n % HT], scr[n % 2][:, 1], o_hi[:, n % HT], ALU.subtract
                                  ).then_inc(fold_lo, 1)

            def product_low(n):
                j = n % FTILES
                dve.wait_ge(g_hi, 2 * n + 2)
                dve.tensor_tensor(gc_lo[:, j], scr[n % 2][:, 0], gc_hi[:, j], ALU.subtract).then_inc(g_lo, 1)
                dve.tensor_tensor(gs_lo[:, j], scr[n % 2][:, 2], gs_hi[:, j], ALU.subtract).then_inc(g_lo, 1)

            for i in range(HT):
                fold(i)
                if i:
                    fold_low(i - 1)
            fold_low(HT - 1)
            dve.wait_ge(fold_lo, HT)
            for o in range(2):
                for j in range(FTILES):
                    n = o * FTILES + j
                    w, sp_, c, s = scr[n % 2], spec[n % 2], bank[2 * (n % 2)], bank[2 * (n % 2) + 1]
                    dve.wait_ge(runs, o * RUNS + 2 * j + 2)
                    dve.wait_ge(spec_in[n % 2], 16 * (n // 2 + 1))
                    if n >= 2:
                        dve.wait_ge(g_lo, 2 * n - 2)
                    dve.tensor_tensor(w[:, 0], c[:], sp_[:, 0], ALU.mult)
                    dve.tensor_tensor(w[:, 1], s[:], sp_[:, 1], ALU.mult)
                    dve.tensor_tensor(w[:, 2], s[:], sp_[:, SPEC - 1 if spectra(j) == SPEC else 0], ALU.mult)
                    dve.tensor_tensor(w[:, 3], c[:], sp_[:, 1], ALU.mult).then_inc(fwd_read, 1)
                    dve.wait_ge(fwd_read, n + 1)
                    dve.tensor_tensor(w[:, 0], w[:, 0], w[:, 1], ALU.subtract)
                    dve.tensor_tensor(w[:, 2], w[:, 2], w[:, 3], ALU.add).then_inc(g_ready, 1)
                    if j:
                        product_low(n - 1)
                product_low((o + 1) * FTILES - 1)
                for i in range(HT):
                    n = o * HT + i
                    q = bank[4 + 2 * (n % 2) + 1]
                    if o == 0 and i:
                        fold_low(HT + i - 1)
                    dve.wait_ge(p_copied, n + 1)
                    dve.wait_ge(biased, n + 1)
                    if o == 0:
                        dve.wait_ge(gate_in[i % 2], 16 * (i // 2 + 1))
                    dve.tensor_tensor(z[0][:, i], p_sb[n % 2][:], q[:], ALU.add)
                    dve.tensor_tensor(z[1][:, i], p_sb[n % 2][:], q[:], ALU.subtract).then_inc(q_read, 1)
                    dve.wait_ge(q_read, n + 1)
                    for h in range(2):
                        a = dve.tensor_tensor(z[h][:, i], z[h][:, i], scr[n % 2][:, 2 + h], ALU.add)
                    if o == 0:
                        step(a)
                        for h in range(2):
                            a = dve.tensor_tensor(z[h][:, i], z[h][:, i], gate[i % 2][:, h], ALU.mult)
                    a.then_inc(zdone, 1)
                    dve.wait_ge(zdone, n + 1)
                    if o == 0:
                        fold(HT + i)
                if o == 0:
                    fold_low(2 * HT - 1)


def stage_hyena_out(nc, g, z):
    JOBS = [(m, tile) for tile in range(HT) for m in range(2)]
    with stage(nc, "ho") as st:
        x2 = st.sb("x2", [P, CHT, T])
        o = st.sb("o", [P, CHT, T])
        bank = [st.bank(f"b{i}") for i in range(4)]
        x_in, turned, gated, stored = (st.sem(x) for x in ("x_in", "turned", "gated", "stored"))
        LAT_JOBS = 2 * HALF_T[0]
        block = st.block()

        @block.sync
        def _(sp):
            sp.dma_start(x2[:], g.convT[2 * CHT:].rearrange("c p t -> p c t")).then_inc(x_in, 16)
            ohT = g.ohT.rearrange("c p t -> p c t")
            for jobs, cols in ((LAT_JOBS, slice(CTX, T)), (len(JOBS), slice(0, CTX))):
                sp.wait_ge(gated, jobs)
                sp.dma_start(ohT[:, :, cols], o[:, :, cols]).then_inc(stored, 16)
            sp.wait_ge(stored, 32)

        @block.tensor
        def _(pe):
            for n, (m, tile) in enumerate(JOBS):
                if n >= 4:
                    pe.wait_ge(gated, n - 3)
                for c in range(CHT):
                    mm = pe.transpose(bank[n % 4][:, c * P:(c + 1) * P], z[m][:, tile, c * P:(c + 1) * P], g.ident[:])
                mm.then_inc(turned, 1)

        @block.vector
        def _(dve):
            dve.wait_ge(x_in, 16)
            for n, (m, tile) in enumerate(JOBS):
                dve.wait_ge(turned, n + 1)
                cols = folded_columns(m, tile)
                dve.tensor_tensor(o[:, :, cols], bank[n % 4][:].rearrange("p (c t) -> p c t", c=CHT),
                                  x2[:, :, stored_columns(m, tile)], ALU.mult).then_inc(gated, 1)


GATE1, SHIFT2, SCALE2, GATE2 = (n * KD for n in (2, 3, 4, 5))
SEG_OF = [0, 1, 1]


RAW = 4


def stage_merge(nc, g):
    K = HEADS + CHT
    with stage(nc, "mg") as st:
        o_raw = [st.sb(f"oraw{s}", [P, T]) for s in range(RAW)]
        o_hi, o_lo = (st.sb(x, [P, K, T], F32R) for x in ("ohi", "olo"))
        raw = [st.sb(f"raw{s}", [P, K, P]) for s in range(2)]
        w_hi = [st.sb(f"whi{s}", [P, K, P], F32R) for s in range(2)]
        w_lo = [st.sb(f"wlo{s}", [P, K, P], F32R) for s in range(2)]
        gate = [st.sb(f"gate{s}", [P, 2, T]) for s in range(2)]
        bank = [[st.bank(f"{x}{c}") for c in range(NC)] for x in "ah"]
        raw_in, gate_in, stored = ([st.sem(f"{n}{s}") for s in range(2)] for n in ("raw_in", "gate_in", "stored"))
        o_in = [st.sem(f"o_in{s}") for s in range(RAW)]
        hi_done, lo_done, o_h, o_l, sig, mm, gated, summed = (
            st.sem(x) for x in ("hi_done", "lo_done", "oh_h", "oh_l", "sig", "mm", "gated", "summed"))
        block = st.block()

        @block.sync
        def _(sp):
            def load_w(n, s):
                sp.dma_start(raw[s][:], g.d["w_br"][n]).then_inc(raw_in[s], 16)

            def load_gates(n, s):
                for h in range(2):
                    sp.dma_start(gate[s][:, h], g.projT[Q_U + K_U + U_U + h * KD + n]).then_inc(gate_in[s], 16)

            load_w(0, 0)
            for k in range(K):
                if k >= RAW:
                    sp.wait_ge(o_l, k - RAW + 1)
                sp.dma_start(o_raw[k % RAW][:], g.ohT[k] if k < CHT else g.oT[k - CHT]).then_inc(o_in[k % RAW], 16)
                if k == RAW - 1:
                    load_w(1, 1)
            for s in range(2):
                load_gates(s, s)
            for n in range(KD):
                s = n % 2
                if n + 2 < KD:
                    sp.wait_ge(lo_done, n + 1)
                    load_w(n + 2, s)
                sp.wait_ge(summed, NC * (n + 1))
                sp.dma_start(g.mT[n], gate[s][:, 0]).then_inc(stored[s], 16)
                if n + 2 < KD:
                    sp.wait_ge(stored[s], 16 * (n // 2 + 1))
                    load_gates(n + 2, s)
            for s in range(2):
                sp.wait_ge(stored[s], 16 * KD // 2)

        @block.scalar
        def _(act):
            def weights(n):
                s = n % 2
                act.wait_ge(raw_in[s], 16 * (n // 2 + 1))
                if n >= 2:
                    act.wait_ge(mm, NC * (n - 1))
                act.activation(w_hi[s][:], raw[s][:], ACT.Copy).then_inc(hi_done, 1)

            def gates(n):
                s = n % 2
                act.wait_ge(gate_in[s], 32 * (n // 2 + 1))
                act.activation(gate[s][:], gate[s][:], ACT.Sigmoid).then_inc(sig, 1)

            weights(0)
            for k in range(K):
                act.wait_ge(o_in[k % RAW], 16 * (k // RAW + 1))
                act.activation(o_hi[:, k], o_raw[k % RAW][:], ACT.Copy).then_inc(o_h, 1)
            weights(1)
            gates(0)
            gates(1)
            for n in range(2, KD):
                weights(n)
                gates(n)

        @block.gpsimd
        def _(pool):
            def weights(n):
                pool.wait_ge(hi_done, n + 1)
                pool.tensor_tensor(w_lo[n % 2][:], raw[n % 2][:], w_hi[n % 2][:], ALU.subtract).then_inc(lo_done, 1)

            weights(1)
            for n in range(KD):
                for c, (at, m) in enumerate(CHUNKS):
                    pool.wait_ge(gated, n * NC + c + 1)
                    gt = gate[n % 2]
                    pool.tensor_tensor(gt[:, 0, at:at + m], gt[:, 0, at:at + m], gt[:, 1, at:at + m], ALU.add
                                       ).then_inc(summed, 1)
                if n + 2 < KD:
                    weights(n + 2)

        @block.tensor
        def _(pe):
            for n in range(KD):
                s = n % 2
                pe.wait_ge(lo_done, n + 1)
                for c, (at, m) in enumerate(CHUNKS):
                    if n:
                        pe.wait_ge(gated, (n - 1) * NC + c + 1)
                    for k in range(K):
                        if n == 0 and c == 0:
                            pe.wait_ge(o_l, k + 1)
                        a = products(pe, bank[k < CHT][c][:, 0:m], w_hi[s][:, k], w_lo[s][:, k],
                                     o_hi[:, k, at:at + m], o_lo[:, k, at:at + m], k in (0, CHT),
                                     k in (CHT - 1, K - 1))
                    a.then_inc(mm, 1)

        @block.vector
        def _(dve):
            dve.wait_ge(hi_done, 1)
            dve.tensor_tensor(w_lo[0][:], raw[0][:], w_hi[0][:], ALU.subtract).then_inc(lo_done, 1)
            for k in range(K):
                dve.wait_ge(o_h, k + 1)
                dve.tensor_tensor(o_lo[:, k], o_raw[k % RAW][:], o_hi[:, k], ALU.subtract).then_inc(o_l, 1)
            for n in range(KD):
                dve.wait_ge(sig, n + 1)
                for c, (at, m) in enumerate(CHUNKS):
                    dve.wait_ge(mm, n * NC + c + 1)
                    for h in range(2):
                        part = gate[n % 2][:, h, at:at + m]
                        a = dve.tensor_tensor(part, part, bank[h][c][:, 0:m], ALU.mult)
                    a.then_inc(gated, 1)


def stage_out(nc, g, x1):
    with stage(nc, "ou") as st:
        m_raw = [st.sb(f"mraw{s}", [P, T]) for s in range(RAW)]
        m_hi, m_lo = (st.sb(x, [P, KD, T], F32R) for x in ("mhi", "mlo"))
        raw = [st.sb(f"raw{s}", [P, KD, P]) for s in range(2)]
        w_hi = [st.sb(f"whi{s}", [P, KD, P], F32R) for s in range(2)]
        w_lo = [st.sb(f"wlo{s}", [P, KD, P], F32R) for s in range(2)]
        bank = [st.bank(f"b{i}") for i in range(BANKS)]
        raw_in = [st.sem(f"raw_in{s}") for s in range(2)]
        m_in = [st.sem(f"m_in{s}") for s in range(RAW)]
        x_in, hi_done, lo_done, m_h, m_l, mm, added = (
            st.sem(x) for x in ("x_in", "hi_done", "lo_done", "m_h", "m_l", "mm", "added"))
        block = st.block()

        @block.sync
        def _(sp):
            sp.dma_start(raw[0][:], g.d["w_out"][0]).then_inc(raw_in[0], 16)
            for k in range(KD):
                if k >= RAW:
                    sp.wait_ge(m_l, k - RAW + 1)
                sp.dma_start(m_raw[k % RAW][:], g.mT[k]).then_inc(m_in[k % RAW], 16)
                if k == RAW - 1:
                    sp.dma_start(raw[1][:], g.d["w_out"][1]).then_inc(raw_in[1], 16)
            sp.dma_start(x1[:], g.d["xT"].rearrange("k p t -> p k t")).then_inc(x_in, 16)
            for n in range(2, KD):
                sp.wait_ge(lo_done, n - 1)
                sp.dma_start(raw[n % 2][:], g.d["w_out"][n]).then_inc(raw_in[n % 2], 16)

        @block.scalar
        def _(act):
            def weights(n):
                s = n % 2
                act.wait_ge(raw_in[s], 16 * (n // 2 + 1))
                if n >= 2:
                    act.wait_ge(mm, NC * (n - 1))
                act.activation(w_hi[s][:], raw[s][:], ACT.Copy).then_inc(hi_done, 1)

            weights(0)
            for k in range(KD):
                act.wait_ge(m_in[k % RAW], 16 * (k // RAW + 1))
                act.activation(m_hi[:, k], m_raw[k % RAW][:], ACT.Copy).then_inc(m_h, 1)
            for n in range(1, KD):
                weights(n)

        @block.gpsimd
        def _(pool):
            for n in range(KD):
                pool.wait_ge(hi_done, n + 1)
                pool.tensor_tensor(w_lo[n % 2][:], raw[n % 2][:], w_hi[n % 2][:], ALU.subtract).then_inc(lo_done, 1)

        @block.tensor
        def _(pe):
            for n in range(KD):
                s = n % 2
                pe.wait_ge(lo_done, n + 1)
                for c, (at, m) in enumerate(CHUNKS):
                    o = n * NC + c
                    if o >= BANKS:
                        pe.wait_ge(added, o - BANKS + 1)
                    for k in range(KD):
                        if n == 0 and c == 0:
                            pe.wait_ge(m_l, k + 1)
                        a = products(pe, bank[o % BANKS][:, 0:m], w_hi[s][:, k], w_lo[s][:, k], m_hi[:, k, at:at + m],
                                     m_lo[:, k, at:at + m], k == 0, k == KD - 1)
                    a.then_inc(mm, 1)

        @block.vector
        def _(dve):
            for k in range(KD):
                dve.wait_ge(m_h, k + 1)
                dve.tensor_tensor(m_lo[:, k], m_raw[k % RAW][:], m_hi[:, k], ALU.subtract).then_inc(m_l, 1)
            dve.wait_ge(x_in, 16)
            for n in range(KD):
                for c, (at, m) in enumerate(CHUNKS):
                    o = n * NC + c
                    dve.wait_ge(mm, o + 1)
                    dve.scalar_tensor_tensor(out=x1[:, n, at:at + m], in0=bank[o % BANKS][:, 0:m],
                                             scalar=g.mod[:, GATE1 + n, SEG_OF[c]:SEG_OF[c] + 1],
                                             in1=x1[:, n, at:at + m], op0=ALU.mult, op1=ALU.add).then_inc(added, 1)
            dve.wait_ge(added, KD * NC)


def stage_norm2(nc, g, x1, h_hi, h_lo):
    with stage(nc, "n2") as st:
        a = st.sb("a", [P, KD, 2])
        a_done = st.sem("a_done")
        nrm = norm_buffers(st)
        block = st.block()

        @block.tensor
        def _(pe):
            norm_pe(pe, g, nrm)

        @block.vector
        def _(dve):
            for s in range(2):
                m = dve.scalar_tensor_tensor(out=a[:, :, s], in0=g.mod[:, SCALE2:SCALE2 + KD, s], scalar=1.0,
                                             in1=g.n2[:], op0=ALU.add, op1=ALU.mult)
            m.then_inc(a_done, 1)
            norm_sum_dve(dve, g, nrm)
            dve.wait_ge(a_done, 1)
            norm_apply_dve(dve, x1, nrm, lambda k, s: (a[:, k, s:s + 1], g.mod[:, SHIFT2 + k, s:s + 1]))

        @block.scalar
        def _(act):
            norm_act(act, x1, nrm)
            split_hi_act(act, nrm, h_hi)

        @block.gpsimd
        def _(pool):
            split_lo_pool(pool, nrm, h_hi, h_lo)


def stage_mlp(nc, g, x1, h_hi, h_lo):
    GT = 4
    GROUPS = FF // P // GT
    UP_U, DOWN_U = GT, KD * GT // KD
    U = UP_U + DOWN_U
    PER_DOWN = KD // DOWN_U
    UP_O, DOWN_O = UP_U * NC, KD * NC
    OUTS = UP_O + DOWN_O
    assert U % 2 == 0 and OUTS % BANKS == 0

    def outs_after(k):
        return NC * (k + 1) if k < UP_U else UP_O + NC * PER_DOWN * (k - UP_U + 1)

    with stage(nc, "ml") as st:
        raw = [st.sb(f"raw{s}", [P, KD, P]) for s in range(2)]
        w_hi = [st.sb(f"whi{s}", [P, KD, P], F32R) for s in range(2)]
        w_lo = [st.sb(f"wlo{s}", [P, KD, P], F32R) for s in range(2)]
        u_hi, u_lo = (st.sb(x, [P, GT, T], F32R) for x in ("uhi", "ulo"))
        r = [st.sb(f"r{s}", [P, 512]) for s in range(2)]
        sq = [st.sb(f"sq{s}", [P, 512]) for s in range(2)]
        bank = [st.bank(f"b{i}") for i in range(BANKS)]
        raw_in = [st.sem(f"raw_in{s}") for s in range(2)]
        hi_done, lo_done, mm, relu, squared, u_h, u_l, added = (
            st.sem(x) for x in ("hi_done", "lo_done", "mm", "relu", "squared", "u_h", "u_l", "added"))
        block = st.block()

        @block.sync
        def _(sp):
            def load(n, s):
                sp.dma_start(raw[s][:], g.d["w_mlp"][n]).then_inc(raw_in[s], 16)

            for s in range(2):
                load(s, s)
            with sp.Fori(1, GROUPS * U // 2) as i:
                for s in range(2):
                    sp.wait_ge(lo_done, 2 * i + s - 1)
                    load(2 * i + s, s)

        @block.scalar
        def _(act):
            def weights(i, k, first):
                j, kk = (i, k) if k < U else (i + 1, 0)
                act.wait_ge(raw_in[kk % 2], 16 * (j * (U // 2) + kk // 2 + 1))
                if k >= 2:
                    act.wait_ge(mm, i * OUTS + outs_after(k - 2))
                elif not first:
                    act.wait_ge(mm, (i - 1) * OUTS + outs_after(U + k - 2))
                act.activation(w_hi[kk % 2][:], raw[kk % 2][:], ACT.Copy).then_inc(hi_done, 1)

            def group(i, first, last):
                for k in range(U):
                    if not (last and k == U - 1):
                        weights(i, k + 1, first)
                    if k >= UP_U:
                        continue
                    for c, (at, m) in enumerate(CHUNKS):
                        o = k * NC + c
                        act.wait_ge(mm, i * OUTS + o + 1)
                        if o >= 2 or not first:
                            act.wait_ge(squared, i * UP_O + o - 1)
                        act.activation(r[o % 2][:, 0:m], bank[o % BANKS][:, 0:m], ACT.Relu).then_inc(relu, 1)
                        act.wait_ge(squared, i * UP_O + o + 1)
                        act.activation(u_hi[:, k, at:at + m], sq[o % 2][:, 0:m], ACT.Copy).then_inc(u_h, 1)

            weights(0, 0, True)
            group(0, True, False)
            with act.Fori(1, GROUPS - 1) as i:
                group(i, False, False)
            group(GROUPS - 1, False, True)

        @block.gpsimd
        def _(pool):
            def weights(i, k):
                pool.wait_ge(hi_done, i * U + k + 1)
                pool.tensor_tensor(w_lo[k % 2][:], raw[k % 2][:], w_hi[k % 2][:], ALU.subtract).then_inc(lo_done, 1)

            def group(i, last):
                for k in range(U):
                    if not (last and k == U - 1):
                        weights(i, k + 1)
                    if k >= UP_U:
                        continue
                    for c, (at, m) in enumerate(CHUNKS):
                        o = k * NC + c
                        pool.wait_ge(u_h, i * UP_O + o + 1)
                        pool.tensor_tensor(u_lo[:, k, at:at + m], sq[o % 2][:, 0:m], u_hi[:, k, at:at + m],
                                           ALU.subtract).then_inc(u_l, 1)

            weights(0, 0)
            with pool.Fori(0, GROUPS - 1) as i:
                group(i, False)
            group(GROUPS - 1, True)

        @block.tensor
        def _(pe):
            def free(i, o):
                q = o - BANKS
                if 0 <= q < UP_O:
                    pe.wait_ge(relu, i * UP_O + q + 1)
                else:
                    done = q - UP_O + 1 if q >= 0 else q + 1
                    pe.wait_ge(added, i * DOWN_O + done + BANKS)

            with pe.Fori(0, GROUPS) as i:
                for k in range(U):
                    s = k % 2
                    pe.wait_ge(lo_done, i * U + k + 1)
                    for n in range(1 if k < UP_U else PER_DOWN):
                        for c, (at, m) in enumerate(CHUNKS):
                            o = k * NC + c if k < UP_U else UP_O + ((k - UP_U) * PER_DOWN + n) * NC + c
                            free(i, o)
                            if k < UP_U:
                                ops = [(kk, h_hi[:, kk, at:at + m], h_lo[:, kk, at:at + m]) for kk in range(KD)]
                            else:
                                if k == UP_U and n == 0:
                                    pe.wait_ge(u_l, i * UP_O + (UP_U - 1) * NC + c + 1)
                                ops = [(n * GT + kk, u_hi[:, kk, at:at + m], u_lo[:, kk, at:at + m])
                                       for kk in range(GT)]
                            for kk, (row, hi, lo) in enumerate(ops):
                                a = products(pe, bank[o % BANKS][:, 0:m], w_hi[s][:, row], w_lo[s][:, row], hi, lo,
                                             kk == 0, kk == len(ops) - 1)
                            a.then_inc(mm, 1)

        @block.vector
        def _(dve):
            dve.sem_inc(added, BANKS)
            def group(i, first):
                for o in range(UP_O):
                    k, c = divmod(o, NC)
                    m = CHUNKS[c][1]
                    dve.wait_ge(relu, i * UP_O + o + 1)
                    if not first or o >= 2:
                        dve.wait_ge(u_l, i * UP_O + o - 1)
                    dve.tensor_tensor(sq[o % 2][:, 0:m], r[o % 2][:, 0:m], r[o % 2][:, 0:m], ALU.mult
                                      ).then_inc(squared, 1)
                for n in range(KD):
                    for c, (at, m) in enumerate(CHUNKS):
                        j = n * NC + c
                        o = UP_O + j
                        dve.wait_ge(mm, i * OUTS + o + 1)
                        if not first:
                            dve.wait_ge(added, (i - 1) * DOWN_O + j + 1 + BANKS)
                        dve.scalar_tensor_tensor(out=x1[:, n, at:at + m], in0=bank[o % BANKS][:, 0:m],
                                                 scalar=g.mod[:, GATE2 + n, SEG_OF[c]:SEG_OF[c] + 1],
                                                 in1=x1[:, n, at:at + m], op0=ALU.mult, op1=ALU.add
                                                 ).then_inc(added, 1)

            group(0, True)
            with dve.Fori(1, GROUPS) as i:
                group(i, False)
            dve.wait_ge(added, GROUPS * DOWN_O + BANKS)


def stage_final(nc, g, x1):
    with stage(nc, "fi") as st:
        nrm = norm_buffers(st)
        scaled, stored = st.sem("scaled"), st.sem("stored")
        block = st.block()

        @block.sync
        def _(sp):
            for k in range(KD):
                sp.wait_ge(scaled, k + 1)
                sp.dma_start(g.y[k], x1[:, k]).then_inc(stored, 16)
            sp.wait_ge(stored, 16 * KD)

        @block.tensor
        def _(pe):
            norm_pe(pe, g, nrm)

        @block.scalar
        def _(act):
            norm_act(act, x1, nrm)

        @block.vector
        def _(dve):
            norm_sum_dve(dve, g, nrm)
            dve.wait_ge(nrm.spread, 1)
            for k in range(KD):
                for c, (at, n) in enumerate(CHUNKS):
                    m = dve.scalar_tensor_tensor(out=x1[:, k, at:at + n], in0=x1[:, k, at:at + n],
                                                 scalar=g.fg[:, k:k + 1], in1=nrm.p_r[c][:, 0:n], op0=ALU.mult,
                                                 op1=ALU.mult)
                m.then_inc(scaled, 1)


def build(nc, d, scratch="Internal"):
    USED.clear()
    g = Shared()
    g.d = d

    def dram(name, shape):
        return nc.dram_tensor(name, shape, F32, kind=scratch).ap()

    g.projT = dram("s_projT", (PROJ_U, P, T))
    g.v = dram("s_v", (TT, P, D))
    g.v_heads = g.v.rearrange("t p (h e) -> h p t e", h=HEADS)
    g.oT = dram("s_oT", (HEADS, P, T))
    g.spec = dram("s_spec", (2, FTILES, P, SPEC, CH))
    g.convT = dram("s_convT", (3 * CHT, P, T))
    g.x1t = dram("s_x1t", (HT, P, 2, CH))
    g.ohT = dram("s_ohT", (CHT, P, T))
    g.mT = dram("s_mT", (KD, P, T))
    g.y, g.new_k, g.new_v = d["y"], d["new_k"], d["new_v"]
    with stage(nc, "all") as st:
        g.ident = st.sb("ident", [P, P])
        g.ones = st.sb("ones", [P, P])
        g.silu = st.sb("silu", [P, KD, 2])
        g.bada = st.sb("bada", [P, ADA_U])
        g.n1, g.n2, g.fg = (st.sb(n, [P, KD]) for n in ("n1", "n2", "fg"))
        g.mod = st.sb("mod", [P, ADA_U, 2])
        g.subln, g.neg_lam = st.sb("subln", [P, 1]), st.sb("neglam", [P, 1])
        stage_consts(nc, g)
        with stage(nc, "fh") as fs:
            net = [fs.sb(n, [HID, T], F32R) for n in ("hhi", "hlo")]
            net += [fs.sb(n, [HID, 2, 2, CH], F32R) for n in ("w3hi", "w3lo")]
            stage_filter_net(nc, g, *net)
            stage_filters(nc, g, *net)
        with stage(nc, "h") as hs:
            h_hi = hs.sb("hi", [P, KD, T], F32R)
            h_lo = hs.sb("lo", [P, KD, T], F32R)
            stage_norm1(nc, g, h_hi, h_lo)
            stage_project(nc, g, h_hi, h_lo)
            stage_values(nc, g, h_hi, h_lo)
        with stage(nc, "z") as zs:
            z = [zs.sb(n, [P, HT, CH]) for n in ("F", "M")]
            stage_turn(nc, g, z)
            stage_hyena(nc, g, z)
            stage_hyena_out(nc, g, z)
        with stage(nc, "o") as os_:
            o_all = os_.sb("all", [P, HEADS * UNITS, VD])
            l0_all = os_.sb("l0", [P, HEADS * UNITS])
            stage_attention(nc, g, o_all, l0_all)
            stage_attn_norm(nc, g, o_all, l0_all)
        stage_merge(nc, g)
        with stage(nc, "x") as xs:
            x1 = xs.sb("x1", [P, KD, T])
            stage_out(nc, g, x1)
            with stage(nc, "h2") as hs:
                h_hi = hs.sb("hi", [P, KD, T], F32R)
                h_lo = hs.sb("lo", [P, KD, T], F32R)
                stage_norm2(nc, g, x1, h_hi, h_lo)
                stage_mlp(nc, g, x1, h_hi, h_lo)
            stage_final(nc, g, x1)


def tiles_T(a):
    return np.ascontiguousarray(a.reshape(-1, P).T)


def units(w):
    k, m = w.shape[0] // P, w.shape[1] // P
    return np.ascontiguousarray(w.reshape(k, P, m, P).transpose(2, 1, 0, 3))


def mlp_units(up, down):
    u = units(up).reshape(-1, 4, P, KD, P)
    d = down.reshape(-1, 4, P, KD // 2, 2, P).transpose(0, 3, 2, 4, 1, 5).reshape(-1, 4, P, KD, P)
    return np.ascontiguousarray(np.stack([u, d], axis=1)).reshape(-1, P, KD, P)


def head_order(w):
    return w.reshape(w.shape[:-1] + (-1, 2, 2, 16)).swapaxes(-3, -2).reshape(w.shape)


def rope_tables():
    n = HD // 4
    inv = np.float32(10000.0) ** (-np.arange(n, dtype=np.float32) / np.float32(n))
    pos = np.arange(LAT)
    ang = [(p.astype(np.float32)[None, :] * inv[:, None]).astype(np.float64) for p in (pos // GRID_W, pos % GRID_W)]
    both = np.concatenate(ang, axis=0)
    cos, sin = np.cos(both), np.sin(both)
    cos, sin = np.concatenate([cos] * 4), np.concatenate([-sin, sin, -sin, sin])
    q_cos = np.concatenate([np.ones((P, CTX)), cos], axis=1) * HD ** -0.5
    t = {"q_cos": q_cos, "q_sin": sin * HD ** -0.5, "k_cos": cos, "k_sin": sin}
    return {n: a.astype(np.float32) for n, a in t.items()}


def frequencies(L):
    even = np.arange(0, L, 2)
    if L // 4 >= P:
        even = np.concatenate([even[::2], even[1::2]])
    return np.concatenate([even, np.arange(1, L, 2)])


def filter_times(L):
    if L == CTX:
        return np.arange(L)
    F, M = np.arange(L // 2), L - np.arange(L // 2)
    M[0] = L // 2
    return np.stack([F.reshape(-1, P), M.reshape(-1, P)], axis=1).reshape(-1)


def table_tiles(a):
    t = a.reshape(-1, P, P).transpose(1, 0, 2)
    return np.concatenate([t, np.zeros((P, KU - t.shape[1], P))], axis=1)


def filter_tables():
    out = []
    for j, c in filter_units():
        L, jj = (LAT, j) if j < LAT_FT else (CTX, j - LAT_FT)
        f = frequencies(L)[jj * P:(jj + 1) * P].astype(np.float64)
        t = np.arange(L // 2 if L == LAT else L, dtype=np.float64)
        ang = math.pi * t[:, None] * f[None, :] / L
        a = np.sin(ang) if c == 1 else np.cos(ang)
        if L == LAT and even_tile(j) and c != 1:
            a[0] = 1.0
        if L == LAT and not even_tile(j) and c == 1:
            a[0] = np.sin(math.pi * f / 2)
        if c == 2:
            a[:, 0] = np.where(t % 2 == 0, 1.0, -1.0)
        out.append(table_tiles(a))
    return np.stack(out).astype(np.float32)


def hyena_tables():
    def cs(L, times, freqs, sine):
        ang = math.pi * (times[:, None] + 0.5) * freqs[None, :] / L
        a = np.sin(ang) if sine else np.cos(ang)
        if sine and freqs[0] == 0:
            a[:, 0] = np.sin(math.pi * (times + 0.5))
        return a

    fl, fc = frequencies(LAT).astype(np.float64), frequencies(CTX).astype(np.float64)
    tl, tc = np.arange(LAT // 2, dtype=np.float64), np.arange(CTX // 2, dtype=np.float64)
    out = [table_tiles(cs(LAT, tl, fl[j * P:(j + 1) * P], c)) for j in range(LAT_FT) for c in range(2)]
    out.append(np.stack([cs(CTX, tc, fc[j * P:(j + 1) * P], c) for j in range(CTX_FT) for c in range(2)], axis=1))
    half = LAT // 2
    for i in range(HALF_T[0]):
        for q in range(2):
            for sine in range(2):
                odd = sine ^ q
                out.append(table_tiles(cs(LAT, tl[i * P:(i + 1) * P], fl[half * odd:half * (odd + 1)], sine).T))
    out.append(np.stack([cs(CTX, tc, fc[P * (s ^ q):P * (s ^ q) + P], s).T for q in range(2) for s in range(2)],
                        axis=1))
    return np.stack(out).astype(np.float32)


def filter_rows():
    embs, decays = [], []
    bands = (EMB - 1) // 2
    deltas = np.linspace(math.log(1e-2) / 0.3, math.log(1e-2) / 1.5, CH, dtype=np.float32).astype(np.float64)
    for L in (LAT, CTX):
        k = filter_times(L)
        t = np.linspace(0.0, 1.0, L, dtype=np.float32).astype(np.float64)[k]
        w = (np.float32(2.0 * math.pi) * np.arange(L, dtype=np.float32) / np.float32(L)).astype(np.float64)[k]
        f = np.linspace(1e-4, bands - 1, bands, dtype=np.float32).astype(np.float64)
        embs.append(np.concatenate([t[None], np.cos(f[:, None] * w), -np.sin(f[:, None] * w)]))
        decays.append(np.exp(-t[:, None] * np.abs(deltas)))
    wf = np.concatenate([np.full((P, LAT_FT), 1.0 / LAT), np.full((P, CTX_FT), 1.0 / CTX)], axis=1)
    wf[0, 0] *= 0.5
    wf[0, LAT_FT] *= 0.5
    decay = np.concatenate(decays).reshape(-1, P, CH).transpose(1, 0, 2)
    return {n: np.ascontiguousarray(a, dtype=np.float32)
            for n, a in (("emb", np.concatenate(embs, axis=1)), ("decay", decay), ("wf", wf))}


def lay_out(i):
    x = np.concatenate([i["x_prompt"][0], i["x_sample"][0]], axis=0)
    w_in = i["w_in"][0]
    q_end, k_end, v_end = D, 2 * D, 3 * D
    a = {
        "xT": np.ascontiguousarray(x.T).reshape(KD, P, T),
        "cond": np.ascontiguousarray(np.stack([i["c_ctx"], i["c"][0]]).reshape(2, KD, P).transpose(2, 1, 0)),
        "b_ada": tiles_T(i["b_ada"][0]), "n1": tiles_T(i["norm1_g"][0]), "n2": tiles_T(i["norm2_g"][0]),
        "fg": tiles_T(i["final_g"]),
        "w_ada": units(i["w_ada"][0][:, :FIRST_ADA * P]),
        "w_adaT": np.ascontiguousarray(i["w_ada"][0][:, FIRST_ADA * P:].T).reshape(-1, P, D),
        "cond_rows": np.ascontiguousarray(np.broadcast_to(np.stack([i["c_ctx"], i["c"][0]]), (P, 2, D))),
        "w_proj": units(np.concatenate([head_order(w_in[:, :k_end]), w_in[:, v_end:]], axis=1)),
        **rope_tables(),
        "cache_kT": np.ascontiguousarray(head_order(i["cache_k"][0, 0]).reshape(PAST, HEADS, P).transpose(1, 2, 0)),
        "cache_v": np.ascontiguousarray(i["cache_v"][0, 0].reshape(PAST // P, P, HEADS, VD).transpose(2, 1, 0, 3)),
        "lam": np.concatenate([i["lam_q1"], i["lam_q2"], i["lam_k1"], i["lam_k2"]], axis=1),
        "w_br": units(np.concatenate([i["w_br_hy"][0], i["w_br_attn"][0]], axis=0)),
        "w_out": units(i["w_out"][0]),
        "w_mlp": mlp_units(i["w_up"][0], i["w_down"][0]),
        **filter_rows(), "filt_tab": filter_tables(), "hy_tab": hyena_tables(),
        "filt_w1": i["filt_w1"][0], "filt_w2": i["filt_w2"][0],
        "filt_vec": np.ascontiguousarray(np.stack([i["filt_b1"][0], i["filt_b2"][0], i["filt_freq"][0]], axis=1)),
        "filt_w3": i["filt_w3"][0].reshape(HID, 2, 2, CH),
        "hy_bias": np.ascontiguousarray(np.broadcast_to(i["hy_bias"][0], (P, 2, CH))),
        "conv": np.ascontiguousarray(np.stack([*i["conv_w"][0], i["conv_b"][0]]).reshape(4, 3 * CHT, P)
                                     .transpose(2, 1, 0)),
        "subln": np.ascontiguousarray(i["attn_subln_g"].reshape(P, 1)),
        "w_v": np.ascontiguousarray(w_in[:, k_end:v_end].reshape(KD, P, D // 512, 512).transpose(2, 1, 0, 3)),
    }
    return a


_OUTS = {"y": (KD, P, T), "new_k": (HEADS, P, CTX), "new_v": (CTX // P, P, D)}


def kernel(**inputs):
    import concourse.bacc as bacc
    from concourse.bass_utils import run_bass_kernel_spmd

    nc = bacc.Bacc("TRN2", target_bir_lowering=False, num_devices=1)
    arrays = lay_out({n: np.asarray(a) for n, a in inputs.items()})
    d = {}
    for n, a in arrays.items():
        d[n] = nc.dram_tensor(f"in_{n}", a.shape, F32, kind="ExternalInput").ap()
    for n, shape in _OUTS.items():
        d[n] = nc.dram_tensor(f"out_{n}", shape, F32, kind="ExternalOutput").ap()
    build(nc, d)
    r = run_bass_kernel_spmd(nc, [{f"in_{n}": a for n, a in arrays.items()}], core_ids=[0]).results[0]
    y = r["out_y"].reshape(D, T).T
    new_k = head_order(r["out_new_k"].transpose(2, 0, 1).reshape(CTX, D)).reshape(1, 1, CTX, HEADS, 2, HD)
    new_v = r["out_new_v"].reshape(1, 1, CTX, HEADS, VD)
    return (np.ascontiguousarray(y[None, :CTX]), np.ascontiguousarray(y[None, CTX:]), np.ascontiguousarray(new_k),
            np.ascontiguousarray(new_v))
```
